# Optimizing a Trainium2 kernel written in Bass

```python
import jax, jax.numpy as jnp
from jax import lax
import numpy as np
import math
import jax
import jax.numpy as jnp

D_MODEL = 1024
BATCH = 1
SEQ = 256
DEPTH = 2

CONV_DIM = 512
CONV_WIDTH = 3
NSA_HEADS = 8
NSA_GROUPS = 2
HEADS_PER_GROUP = NSA_HEADS // NSA_GROUPS
HEAD_DIM = 64
ROT_DIM = HEAD_DIM // 4
ROPE_THETA = 500000.0
CMP_BLOCK = 32
CMP_STRIDE = 16
CMP_HIDDEN = 256
SLC_BLOCK = 64
N_SELECT = 16
WINDOW = 512
MEM_LEN = 256
MEM_HEADS = 4
MEM_HEAD_DIM = 128
D_FF = 2816
Q_BLOCK = 128
EPS = 1e-6
NEG = -1e30
BIG = 1e30
SPLIT_SIZES = (CONV_DIM, CONV_DIM, CONV_DIM, NSA_HEADS * HEAD_DIM, 6 * NSA_GROUPS * HEAD_DIM, 3 * NSA_HEADS, MEM_HEADS * MEM_HEAD_DIM, 3 * D_MODEL)
MIX_IN = 3 * CONV_DIM + NSA_HEADS * HEAD_DIM + 6 * NSA_GROUPS * HEAD_DIM + 3 * NSA_HEADS + MEM_HEADS * MEM_HEAD_DIM + 3 * D_MODEL


def rms_norm(x, g):
    xf = x.astype(jnp.float32)
    y = xf * lax.rsqrt(jnp.mean(xf * xf, axis=-1, keepdims=True) + EPS)
    return (y * g.astype(jnp.float32)).astype(x.dtype)

def swiglu(h, w_in, w_out):
    a, b = jnp.split(h @ w_in, 2, axis=-1)
    return (jax.nn.silu(a) * b) @ w_out

def rope_tables(positions):
    inv_freq = ROPE_THETA ** (-jnp.arange(0, ROT_DIM, 2, dtype=jnp.float32) / ROT_DIM)
    ang = positions.astype(jnp.float32)[..., None] * inv_freq
    return jnp.cos(ang)[:, :, None, :], jnp.sin(ang)[:, :, None, :]

def partial_rope(t, cos, sin):
    half = ROT_DIM // 2
    t1, t2, rest = t[..., :half], t[..., half:ROT_DIM], t[..., ROT_DIM:]
    return jnp.concatenate([t1 * cos - t2 * sin, t2 * cos + t1 * sin, rest], axis=-1)

def masked_softmax(s, mask):
    s = jnp.where(mask, s.astype(jnp.float32), NEG)
    m = jnp.max(s, axis=-1, keepdims=True)
    p = jnp.where(mask, jnp.exp(s - m), 0.0)
    return p / jnp.maximum(jnp.sum(p, axis=-1, keepdims=True), 1e-30)

def short_conv(v, w):
    return lax.conv_general_dilated(v, w[:, None, :].astype(v.dtype), window_strides=(1,),
                                    padding=[(CONV_WIDTH - 1, 0)],
                                    dimension_numbers=('NWC', 'WIO', 'NWC'),
                                    feature_group_count=v.shape[-1])

def compress(t, pos_emb, w1, b1, w2):
    b, s, g, d = t.shape
    chunks = t.reshape(b, s // CMP_STRIDE, CMP_STRIDE, g, d)
    blocks = jnp.concatenate([chunks[:, :-1], chunks[:, 1:]], axis=2)
    blocks = blocks + pos_emb[None, None, :, None, :]
    flat = jnp.moveaxis(blocks, 3, 2).reshape(b, -1, g, CMP_BLOCK * d)
    return jax.nn.gelu(flat @ w1 + b1) @ w2

def cmp_to_slc_matrix(n_cmp, n_slc):
    i = jnp.arange(n_cmp)[:, None] * CMP_STRIDE
    j = jnp.arange(n_slc)[None, :] * SLC_BLOCK
    ov = jnp.minimum(i + CMP_BLOCK, j + SLC_BLOCK) - jnp.maximum(i, j)
    return jnp.maximum(ov, 0).astype(jnp.float32) / CMP_BLOCK

def nsa_attention(q, q_rot, k_cmp, v_cmp, k_slc, v_slc, k_win, v_win, gates):
    b, s, h, d = q.shape
    n_cmp = k_cmp.shape[1]
    n_slc = s // SLC_BLOCK
    top = min(N_SELECT, n_slc)
    scale = HEAD_DIM ** -0.5
    q_plain_g = q.reshape(b, s, NSA_GROUPS, HEADS_PER_GROUP, d)
    q_rot_g = q_rot.reshape(b, s, NSA_GROUPS, HEADS_PER_GROUP, d)
    kc = jnp.transpose(k_cmp, (0, 2, 1, 3))
    vc = jnp.transpose(v_cmp, (0, 2, 1, 3))
    cmp_end = jnp.arange(n_cmp) * CMP_STRIDE + CMP_BLOCK - 1
    overlap = cmp_to_slc_matrix(n_cmp, n_slc)
    ks_blocks = k_slc.reshape(b, n_slc, SLC_BLOCK, NSA_GROUPS, d).transpose(0, 3, 1, 2, 4)
    vs_blocks = v_slc.reshape(b, n_slc, SLC_BLOCK, NSA_GROUPS, d).transpose(0, 3, 1, 2, 4)
    pad = ((0, 0), (WINDOW, 0), (0, 0), (0, 0))
    kw_pad = jnp.pad(k_win, pad)
    vw_pad = jnp.pad(v_win, pad)
    bi = jnp.arange(b)[:, None, None, None]
    gi = jnp.arange(NSA_GROUPS)[None, :, None, None]
    blk = jnp.arange(n_slc)

    def block(start):
        t = start + jnp.arange(Q_BLOCK)
        qp = lax.dynamic_slice_in_dim(q_plain_g, start, Q_BLOCK, axis=1)
        qr = lax.dynamic_slice_in_dim(q_rot_g, start, Q_BLOCK, axis=1)
        s_c = jnp.einsum('bqghd,bgnd->bghqn', qp, kc) * scale
        p_c = masked_softmax(s_c, cmp_end[None, :] <= t[:, None])
        o_c = jnp.einsum('bghqn,bgnd->bqghd', p_c.astype(vc.dtype), vc)
        imp = jnp.einsum('bghqn,nj->bgqj', p_c, overlap)
        cur = (t // SLC_BLOCK)[:, None]
        forced = (blk == 0) | (blk == cur) | (blk == cur - 1)
        imp = jnp.where(blk > cur, NEG, jnp.where(forced, BIG, imp))
        _, idx = lax.top_k(imp, top)
        ks = ks_blocks[bi, gi, idx].reshape(b, NSA_GROUPS, Q_BLOCK, top * SLC_BLOCK, d)
        vs = vs_blocks[bi, gi, idx].reshape(b, NSA_GROUPS, Q_BLOCK, top * SLC_BLOCK, d)
        kpos = (idx[..., None] * SLC_BLOCK + jnp.arange(SLC_BLOCK)).reshape(b, NSA_GROUPS, Q_BLOCK, top * SLC_BLOCK)
        m_s = kpos <= t[None, None, :, None]
        s_s = jnp.einsum('bqghd,bgqld->bghql', qr, ks) * scale
        p_s = masked_softmax(s_s, m_s[:, :, None])
        o_s = jnp.einsum('bghql,bgqld->bqghd', p_s.astype(vs.dtype), vs)
        kw = lax.dynamic_slice_in_dim(kw_pad, start, WINDOW + Q_BLOCK, axis=1)
        vw = lax.dynamic_slice_in_dim(vw_pad, start, WINDOW + Q_BLOCK, axis=1)
        wpos = start - WINDOW + jnp.arange(WINDOW + Q_BLOCK)
        m_w = (wpos[None, :] >= 0) & (wpos[None, :] <= t[:, None]) & (wpos[None, :] > t[:, None] - WINDOW)
        s_w = jnp.einsum('bqghd,bkgd->bghqk', qr, kw) * scale
        p_w = masked_softmax(s_w, m_w)
        o_w = jnp.einsum('bghqk,bkgd->bqghd', p_w.astype(vw.dtype), vw)
        g = lax.dynamic_slice_in_dim(gates, start, Q_BLOCK, axis=1)
        return g[..., 0:1] * o_c + g[..., 1:2] * o_s + g[..., 2:3] * o_w

    out = lax.map(block, jnp.arange(s // Q_BLOCK) * Q_BLOCK)
    return jnp.moveaxis(out, 0, 1).reshape(b, s, h * d)

def token_mixer(h, mem, cos, sin, mem_g, w_in, conv_w, cmp_pos_k, cmp_pos_v,
                ck_w1, ck_b1, ck_w2, cv_w1, cv_b1, cv_w2,
                w_mem_kv, w_br_conv, w_br_nsa, w_br_mem, w_out):
    b, s, _ = h.shape
    points, acc = [], 0
    for n in SPLIT_SIZES[:-1]:
        acc += n
        points.append(acc)
    u, bg, cg, q, kv, nsa_g, q_mem, merge_g = jnp.split(h @ w_in, points, axis=-1)
    cos = cos.astype(h.dtype)
    sin = sin.astype(h.dtype)
    y_conv = bg * short_conv(cg * u, conv_w)
    q = q.reshape(b, s, NSA_HEADS, HEAD_DIM)
    kv = kv.reshape(b, s, 6, NSA_GROUPS, HEAD_DIM)
    k_cmp = compress(kv[:, :, 0], cmp_pos_k, ck_w1, ck_b1, ck_w2)
    v_cmp = compress(kv[:, :, 1], cmp_pos_v, cv_w1, cv_b1, cv_w2)
    k_slc = partial_rope(kv[:, :, 2], cos, sin)
    k_win = partial_rope(kv[:, :, 4], cos, sin)
    q_rot = partial_rope(q, cos, sin)
    gates = jax.nn.sigmoid(nsa_g).reshape(b, s, NSA_GROUPS, HEADS_PER_GROUP, 3)
    y_nsa = nsa_attention(q, q_rot, k_cmp, v_cmp, k_slc, kv[:, :, 3], k_win, kv[:, :, 5], gates)
    m_len = mem.shape[1]
    mkv = (rms_norm(mem, mem_g) @ w_mem_kv).reshape(b, m_len, 2, MEM_HEADS, MEM_HEAD_DIM)
    q_m = q_mem.reshape(b, s, MEM_HEADS, MEM_HEAD_DIM)
    s_m = jnp.einsum('bshd,bmhd->bhsm', q_m, mkv[:, :, 0]).astype(jnp.float32) * (MEM_HEAD_DIM ** -0.5)
    p_m = jax.nn.softmax(s_m, axis=-1)
    y_mem = jnp.einsum('bhsm,bmhd->bshd', p_m.astype(mkv.dtype), mkv[:, :, 1]).reshape(b, s, MEM_HEADS * MEM_HEAD_DIM)
    g_conv, g_nsa, g_mem = jnp.split(jax.nn.sigmoid(merge_g), 3, axis=-1)
    merged = g_conv * (y_conv @ w_br_conv) + g_nsa * (y_nsa @ w_br_nsa) + g_mem * (y_mem @ w_br_mem)
    return merged @ w_out

def first_inputs(seed: int = 0) -> dict:
    key = jax.random.key(seed)
    keys = iter(jax.random.split(key, 40))
    L = DEPTH

    def dense(shape, fan_in):
        return jax.random.normal(next(keys), shape, jnp.float32) * fan_in ** -0.5

    def gain(shape):
        return 1.0 + 0.05 * jax.random.normal(next(keys), shape, jnp.float32)

    def small(shape, scale):
        return scale * jax.random.normal(next(keys), shape, jnp.float32)

    x = jax.random.normal(next(keys), (BATCH, SEQ, D_MODEL), jnp.float32)
    mem = jax.random.normal(next(keys), (BATCH, MEM_LEN, D_MODEL), jnp.float32)
    offset = jax.random.randint(next(keys), (BATCH, 1), 0, 4096, dtype=jnp.int32)
    positions = (jnp.arange(SEQ, dtype=jnp.int32)[None, :] + offset).astype(jnp.int32)
    return {
        'x': x,
        'mem': mem,
        'positions': positions,
        'ffn1_norm_pre': gain((L, D_MODEL)),
        'ffn1_norm_post': gain((L, D_MODEL)),
        'ffn1_w_in': dense((L, D_MODEL, 2 * D_FF), D_MODEL),
        'ffn1_w_out': dense((L, D_FF, D_MODEL), D_FF),
        'mix_norm_pre': gain((L, D_MODEL)),
        'mix_norm_post': gain((L, D_MODEL)),
        'mem_norm': gain((L, D_MODEL)),
        'w_mix_in': dense((L, D_MODEL, MIX_IN), D_MODEL),
        'conv_w': dense((L, CONV_WIDTH, CONV_DIM), CONV_WIDTH),
        'cmp_pos_k': small((L, CMP_BLOCK, HEAD_DIM), 0.1),
        'cmp_pos_v': small((L, CMP_BLOCK, HEAD_DIM), 0.1),
        'cmp_k_w1': dense((L, CMP_BLOCK * HEAD_DIM, CMP_HIDDEN), CMP_BLOCK * HEAD_DIM),
        'cmp_k_b1': small((L, CMP_HIDDEN), 0.01),
        'cmp_k_w2': dense((L, CMP_HIDDEN, HEAD_DIM), CMP_HIDDEN),
        'cmp_v_w1': dense((L, CMP_BLOCK * HEAD_DIM, CMP_HIDDEN), CMP_BLOCK * HEAD_DIM),
        'cmp_v_b1': small((L, CMP_HIDDEN), 0.01),
        'cmp_v_w2': dense((L, CMP_HIDDEN, HEAD_DIM), CMP_HIDDEN),
        'w_mem_kv': dense((L, D_MODEL, 2 * MEM_HEADS * MEM_HEAD_DIM), D_MODEL),
        'w_branch_conv': dense((L, CONV_DIM, D_MODEL), CONV_DIM),
        'w_branch_nsa': dense((L, NSA_HEADS * HEAD_DIM, D_MODEL), NSA_HEADS * HEAD_DIM),
        'w_branch_mem': dense((L, MEM_HEADS * MEM_HEAD_DIM, D_MODEL), MEM_HEADS * MEM_HEAD_DIM),
        'w_mix_out': dense((L, D_MODEL, D_MODEL), D_MODEL),
        'ffn2_norm_pre': gain((L, D_MODEL)),
        'ffn2_norm_post': gain((L, D_MODEL)),
        'ffn2_w_in': dense((L, D_MODEL, 2 * D_FF), D_MODEL),
        'ffn2_w_out': dense((L, D_FF, D_MODEL), D_FF),
    }

def first_block(x, mem, positions, ffn1_norm_pre, ffn1_norm_post, ffn1_w_in, ffn1_w_out,
              mix_norm_pre, mix_norm_post, mem_norm, w_mix_in, conv_w,
              cmp_pos_k, cmp_pos_v, cmp_k_w1, cmp_k_b1, cmp_k_w2, cmp_v_w1, cmp_v_b1, cmp_v_w2,
              w_mem_kv, w_branch_conv, w_branch_nsa, w_branch_mem, w_mix_out,
              ffn2_norm_pre, ffn2_norm_post, ffn2_w_in, ffn2_w_out):
    cos, sin = rope_tables(positions)
    for l in range(DEPTH):
        h = rms_norm(x, ffn1_norm_pre[l])
        x = x + 0.5 * rms_norm(swiglu(h, ffn1_w_in[l], ffn1_w_out[l]), ffn1_norm_post[l])
        h = rms_norm(x, mix_norm_pre[l])
        y = token_mixer(h, mem, cos, sin, mem_norm[l], w_mix_in[l], conv_w[l],
                        cmp_pos_k[l], cmp_pos_v[l], cmp_k_w1[l], cmp_k_b1[l], cmp_k_w2[l],
                        cmp_v_w1[l], cmp_v_b1[l], cmp_v_w2[l], w_mem_kv[l],
                        w_branch_conv[l], w_branch_nsa[l], w_branch_mem[l], w_mix_out[l])
        x = x + rms_norm(y, mix_norm_post[l])
        h = rms_norm(x, ffn2_norm_pre[l])
        x = x + 0.5 * rms_norm(swiglu(h, ffn2_w_in[l], ffn2_w_out[l]), ffn2_norm_post[l])
    return x


RMS_EPS = 1e-6

SSD_HEAD_DIM = 64
SSD_D_INNER = D_MODEL
SSD_HEADS = SSD_D_INNER // SSD_HEAD_DIM
SSD_GROUPS = 4
SSD_D_STATE = 128
SSD_CONV = 4
SSD_CHUNK = 256
SSD_CONV_DIM = SSD_D_INNER + 2 * SSD_GROUPS * SSD_D_STATE

DIL_PAIRS = ((128, 1), (512, 4), (2048, 16))
DIL_HEAD_DIM = 64
DIL_HEADS_PER_GROUP = 8
DIL_HEADS = DIL_HEADS_PER_GROUP * len(DIL_PAIRS)
DIL_QKV = DIL_HEADS * DIL_HEAD_DIM
DIL_OUT = DIL_HEADS_PER_GROUP * DIL_HEAD_DIM

MOBA_HEAD_DIM = 64
MOBA_WIDTH = D_MODEL
MOBA_HEADS = MOBA_WIDTH // MOBA_HEAD_DIM
MOBA_BLOCK = 256
MOBA_TOPK = 3
MOBA_Q_CHUNK = 16

EVEN_IN_SIZES = (SSD_D_INNER, SSD_CONV_DIM, SSD_HEADS, DIL_QKV, DIL_QKV, DIL_QKV, DIL_OUT)
EVEN_IN = sum(EVEN_IN_SIZES)
EVEN_MIX = SSD_D_INNER + DIL_OUT
ODD_IN = 4 * MOBA_WIDTH
N_EVEN = (DEPTH + 1) // 2
N_ODD = DEPTH // 2


def rms_norm_2(x, w):
    xf = x.astype(jnp.float32)
    y = xf * lax.rsqrt(jnp.mean(xf * xf, axis=-1, keepdims=True) + RMS_EPS)
    return (y * w.astype(jnp.float32)).astype(x.dtype)

def partial_rope_2(x, pos):
    e = x.shape[-1]
    rd = e // 4
    half = rd // 2
    inv = ROPE_THETA ** (-jnp.arange(half, dtype=jnp.float32) * 2.0 / rd)
    ang = pos.astype(jnp.float32)[:, None] * inv[None, :]
    cos = jnp.cos(ang)[:, None, :]
    sin = jnp.sin(ang)[:, None, :]
    xr = x[..., :rd].astype(jnp.float32)
    x1, x2 = xr[..., :half], xr[..., half:]
    rot = jnp.concatenate([x1 * cos - x2 * sin, x2 * cos + x1 * sin], axis=-1)
    return jnp.concatenate([rot.astype(x.dtype), x[..., rd:]], axis=-1)

def split_cols(t, sizes):
    outs, o = [], 0
    for s in sizes:
        outs.append(t[..., o:o + s])
        o += s
    return outs

def causal_dwconv(x, w, b):
    K = w.shape[1]
    rhs = jnp.transpose(w)[:, None, :].astype(x.dtype)
    y = lax.conv_general_dilated(x, rhs, window_strides=(1,), padding=((K - 1, 0),),
                                 dimension_numbers=("NWC", "WIO", "NWC"),
                                 feature_group_count=x.shape[-1])
    return y + b.astype(x.dtype)

def segsum(a):
    T = a.shape[-1]
    cs = jnp.cumsum(a, axis=-1)
    diff = cs[..., :, None] - cs[..., None, :]
    mask = jnp.tril(jnp.ones((T, T), dtype=bool))
    return jnp.where(mask, diff, -jnp.inf)

def ssd_chunked_scan(x, dt, A, Bm, Cm):
    Bsz, S, H, P = x.shape
    G, N = Bm.shape[2], Bm.shape[3]
    J = H // G
    L = SSD_CHUNK
    pad = (-S) % L
    xdt = x.astype(jnp.float32) * dt[..., None]
    a = dt * A
    Bf = Bm.astype(jnp.float32)
    Cf = Cm.astype(jnp.float32)
    if pad:
        padseq = lambda t: jnp.pad(t, [(0, 0), (0, pad)] + [(0, 0)] * (t.ndim - 2))
        xdt, a, Bf, Cf = padseq(xdt), padseq(a), padseq(Bf), padseq(Cf)
    nc = (S + pad) // L
    xdt = xdt.reshape(Bsz, nc, L, G, J, P)
    Bc = Bf.reshape(Bsz, nc, L, G, N)
    Cc = Cf.reshape(Bsz, nc, L, G, N)
    a = a.reshape(Bsz, nc, L, G, J).transpose(0, 3, 4, 1, 2)
    a_cs = jnp.cumsum(a, axis=-1)
    cb = jnp.einsum("bclgn,bcsgn->bgcls", Cc, Bc)
    m = cb[:, :, None] * jnp.exp(segsum(a))
    y_diag = jnp.einsum("bgjcls,bcsgjp->bclgjp", m, xdt)
    w_end = jnp.exp(a_cs[..., -1:] - a_cs).transpose(0, 3, 4, 1, 2)
    states = jnp.einsum("bclgn,bclgjp->bcgjpn", Bc, xdt * w_end[..., None])
    a_last = jnp.pad(a_cs[..., -1], [(0, 0)] * 3 + [(1, 0)])
    decay_chunk = jnp.exp(segsum(a_last))
    states0 = jnp.concatenate([jnp.zeros_like(states[:, :1]), states], axis=1)
    entering = jnp.einsum("bgjzc,bcgjpn->bzgjpn", decay_chunk, states0)[:, :-1]
    w_start = jnp.exp(a_cs).transpose(0, 3, 4, 1, 2)
    y_off = jnp.einsum("bclgn,bcgjpn->bclgjp", Cc, entering) * w_start[..., None]
    return (y_diag + y_off).reshape(Bsz, nc * L, H, P)[:, :S]

def dilated_group(q, k, v, window, dil):
    Bsz, S, h, e = q.shape
    band = window // dil
    Lsub = S // dil
    nb = -(-Lsub // band)
    Lp = nb * band

    def to_sub(t):
        t = t.astype(jnp.float32).reshape(Bsz, Lsub, dil, h, e).transpose(0, 3, 2, 1, 4)
        t = jnp.pad(t, ((0, 0), (0, 0), (0, 0), (0, Lp - Lsub), (0, 0)))
        return t.reshape(Bsz, h, dil, nb, band, e)

    def with_prev(t):
        prev = jnp.pad(t, ((0, 0), (0, 0), (0, 0), (1, 0), (0, 0), (0, 0)))[:, :, :, :-1]
        return jnp.concatenate([prev, t], axis=4)

    qs = to_sub(q)
    kb = with_prev(to_sub(k))
    vb = with_prev(to_sub(v))
    s = jnp.einsum("bhrnqe,bhrnke->bhrnqk", qs, kb) * (e ** -0.5)
    i = jnp.arange(band)[:, None]
    j = jnp.arange(2 * band)[None, :]
    dist = i + band - j
    n = jnp.arange(nb)[:, None, None]
    valid = (dist >= 0) & (dist <= band) & ((n * band + j[None] - band) >= 0)
    s = jnp.where(valid, s, -jnp.inf)
    mx = jnp.max(s, axis=-1, keepdims=True)
    p = jnp.exp(s - mx)
    den = jnp.sum(p, axis=-1)
    o = jnp.einsum("bhrnqk,bhrnke->bhrnqe", p, vb) / den[..., None]
    lse = mx[..., 0] + jnp.log(den)
    o = o.reshape(Bsz, h, dil, Lp, e)[:, :, :, :Lsub].transpose(0, 3, 2, 1, 4).reshape(Bsz, S, h, e)
    lse = lse.reshape(Bsz, h, dil, Lp)[:, :, :, :Lsub].transpose(0, 3, 2, 1).reshape(Bsz, S, h)
    return o, lse

def moba_attention(q, k, v):
    Bsz, S, H, e = q.shape
    blk = MOBA_BLOCK
    nblk = -(-S // blk)
    Sp = nblk * blk
    scale = e ** -0.5

    def heads_first(t):
        t = t.astype(jnp.float32).transpose(0, 2, 1, 3)
        return jnp.pad(t, ((0, 0), (0, 0), (0, Sp - S), (0, 0)))

    qh = heads_first(q)
    kb = heads_first(k).reshape(Bsz, H, nblk, blk, e)
    vb = heads_first(v).reshape(Bsz, H, nblk, blk, e)
    kmean = jnp.mean(kb, axis=3)
    gate = jnp.einsum("bhte,bhne->bhtn", qh, kmean)
    tblk = jnp.arange(Sp) // blk
    past = jnp.arange(nblk)[None, :] < tblk[:, None]
    gate = jnp.where(past, gate, -jnp.inf)
    ksel = min(MOBA_TOPK, nblk)
    _, sel = lax.top_k(gate, ksel)
    sel_valid = sel < tblk[:, None]

    Qc = MOBA_Q_CHUNK
    nq = Sp // Qc
    qc = qh.reshape(Bsz, H, nq, Qc, e).transpose(2, 0, 1, 3, 4)
    selc = sel.reshape(Bsz, H, nq, Qc, ksel).transpose(2, 0, 1, 3, 4)
    valc = sel_valid.reshape(Bsz, H, nq, Qc, ksel).transpose(2, 0, 1, 3, 4)
    bi = jnp.arange(Bsz)[:, None, None, None]
    hi = jnp.arange(H)[None, :, None, None]

    def one_chunk(args):
        c, q_c, sel_c, val_c = args
        own = (c * Qc) // blk
        k_sel = kb[bi, hi, sel_c]
        v_sel = vb[bi, hi, sel_c]
        s_sel = jnp.einsum("bhqe,bhqjke->bhqjk", q_c, k_sel) * scale
        s_sel = jnp.where(val_c[..., None], s_sel, -jnp.inf).reshape(Bsz, H, Qc, ksel * blk)
        k_own = lax.dynamic_index_in_dim(kb, own, axis=2, keepdims=False)
        v_own = lax.dynamic_index_in_dim(vb, own, axis=2, keepdims=False)
        s_own = jnp.einsum("bhqe,bhke->bhqk", q_c, k_own) * scale
        qpos = c * Qc + jnp.arange(Qc)
        kpos = own * blk + jnp.arange(blk)
        s_own = jnp.where(kpos[None, :] <= qpos[:, None], s_own, -jnp.inf)
        p = jax.nn.softmax(jnp.concatenate([s_sel, s_own], axis=-1), axis=-1)
        p_sel = p[..., :ksel * blk].reshape(Bsz, H, Qc, ksel, blk)
        return (jnp.einsum("bhqjk,bhqjke->bhqe", p_sel, v_sel)
                + jnp.einsum("bhqk,bhke->bhqe", p[..., ksel * blk:], v_own))

    out = lax.map(one_chunk, (jnp.arange(nq), qc, selc, valc))
    return out.transpose(1, 0, 3, 2, 4).reshape(Bsz, Sp, H, e)[:, :S]

def ssd_dilated_layer(x, norm_w, w_in, conv_w, conv_b, dt_bias, a_log, d_skip, ssd_norm_w,
                      q_norm, k_norm, w_out, pos):
    Bsz, S, _ = x.shape
    h = rms_norm_2(x, norm_w)
    proj = jnp.einsum("bsd,df->bsf", h, w_in.astype(h.dtype))
    z, xbc, dt, q, k, v, g = split_cols(proj, EVEN_IN_SIZES)
    xbc = jax.nn.silu(causal_dwconv(xbc, conv_w, conv_b))
    xs, bm, cm = split_cols(xbc, (SSD_D_INNER, SSD_GROUPS * SSD_D_STATE, SSD_GROUPS * SSD_D_STATE))
    xs = xs.reshape(Bsz, S, SSD_HEADS, SSD_HEAD_DIM)
    dt = jax.nn.softplus(dt.astype(jnp.float32) + dt_bias.astype(jnp.float32))
    A = -jnp.exp(a_log.astype(jnp.float32))
    y = ssd_chunked_scan(xs, dt, A, bm.reshape(Bsz, S, SSD_GROUPS, SSD_D_STATE),
                         cm.reshape(Bsz, S, SSD_GROUPS, SSD_D_STATE))
    y = y + d_skip.astype(jnp.float32)[:, None] * xs.astype(jnp.float32)
    y = y.reshape(Bsz, S, SSD_D_INNER) * jax.nn.silu(z.astype(jnp.float32))
    y = rms_norm_2(y.reshape(Bsz, S, SSD_GROUPS, -1),
                 ssd_norm_w.reshape(SSD_GROUPS, -1)).reshape(Bsz, S, SSD_D_INNER)
    q = partial_rope_2(rms_norm_2(q.reshape(Bsz, S, DIL_HEADS, DIL_HEAD_DIM), q_norm), pos)
    k = partial_rope_2(rms_norm_2(k.reshape(Bsz, S, DIL_HEADS, DIL_HEAD_DIM), k_norm), pos)
    v = v.reshape(Bsz, S, DIL_HEADS, DIL_HEAD_DIM)
    outs, lses = [], []
    for gi, (window, dil) in enumerate(DIL_PAIRS):
        hs = slice(gi * DIL_HEADS_PER_GROUP, (gi + 1) * DIL_HEADS_PER_GROUP)
        o_g, lse_g = dilated_group(q[:, :, hs], k[:, :, hs], v[:, :, hs], window, dil)
        outs.append(o_g)
        lses.append(lse_g)
    wts = jax.nn.softmax(jnp.stack(lses, axis=0), axis=0)
    o = jnp.sum(wts[..., None] * jnp.stack(outs, axis=0), axis=0)
    o = o.reshape(Bsz, S, DIL_OUT) * jax.nn.silu(g.astype(jnp.float32))
    mixed = jnp.concatenate([y.astype(jnp.float32), o], axis=-1).astype(x.dtype)
    return x + jnp.einsum("bsf,fd->bsd", mixed, w_out.astype(x.dtype))

def moba_layer(x, norm_w, w_in, q_norm, k_norm, w_out, pos):
    Bsz, S, _ = x.shape
    h = rms_norm_2(x, norm_w)
    proj = jnp.einsum("bsd,df->bsf", h, w_in.astype(h.dtype))
    q, k, v, g = split_cols(proj, (MOBA_WIDTH,) * 4)
    q = partial_rope_2(rms_norm_2(q.reshape(Bsz, S, MOBA_HEADS, MOBA_HEAD_DIM), q_norm), pos)
    k = partial_rope_2(rms_norm_2(k.reshape(Bsz, S, MOBA_HEADS, MOBA_HEAD_DIM), k_norm), pos)
    v = v.reshape(Bsz, S, MOBA_HEADS, MOBA_HEAD_DIM)
    o = moba_attention(q, k, v).reshape(Bsz, S, MOBA_WIDTH) * jax.nn.silu(g.astype(jnp.float32))
    return x + jnp.einsum("bsf,fd->bsd", o.astype(x.dtype), w_out.astype(x.dtype))

def second_inputs(seed: int = 0) -> dict:
    key = jax.random.key(seed)
    ks = jax.random.split(key, 20)
    f32 = jnp.float32
    nrm = lambda k, shape, s: jax.random.normal(k, shape, f32) * s
    x = jax.random.normal(ks[0], (BATCH, SEQ, D_MODEL), f32)
    even_norm_w = 1.0 + nrm(ks[1], (N_EVEN, D_MODEL), 0.05)
    even_w_in = nrm(ks[2], (N_EVEN, D_MODEL, EVEN_IN), D_MODEL ** -0.5)
    even_conv_w = nrm(ks[3], (N_EVEN, SSD_CONV_DIM, SSD_CONV), SSD_CONV ** -0.5)
    even_conv_b = nrm(ks[4], (N_EVEN, SSD_CONV_DIM), 0.01)
    dt0 = jnp.exp(jax.random.uniform(ks[5], (N_EVEN, SSD_HEADS), f32,
                                     math.log(1e-3), math.log(1e-1)))
    even_dt_bias = dt0 + jnp.log(-jnp.expm1(-dt0))
    even_a_log = jnp.log(jax.random.uniform(ks[6], (N_EVEN, SSD_HEADS), f32, 1.0, 16.0))
    even_d_skip = 1.0 + nrm(ks[7], (N_EVEN, SSD_HEADS), 0.1)
    even_ssd_norm_w = 1.0 + nrm(ks[8], (N_EVEN, SSD_D_INNER), 0.05)
    even_q_norm = 1.0 + nrm(ks[9], (N_EVEN, DIL_HEAD_DIM), 0.05)
    even_k_norm = 1.0 + nrm(ks[10], (N_EVEN, DIL_HEAD_DIM), 0.05)
    even_w_out = nrm(ks[11], (N_EVEN, EVEN_MIX, D_MODEL), EVEN_MIX ** -0.5)
    odd_norm_w = 1.0 + nrm(ks[12], (N_ODD, D_MODEL), 0.05)
    odd_w_in = nrm(ks[13], (N_ODD, D_MODEL, ODD_IN), D_MODEL ** -0.5)
    odd_q_norm = 1.0 + nrm(ks[14], (N_ODD, MOBA_HEAD_DIM), 0.05)
    odd_k_norm = 1.0 + nrm(ks[15], (N_ODD, MOBA_HEAD_DIM), 0.05)
    odd_w_out = nrm(ks[16], (N_ODD, MOBA_WIDTH, D_MODEL), MOBA_WIDTH ** -0.5)
    return {"x": x, "even_norm_w": even_norm_w, "even_w_in": even_w_in,
            "even_conv_w": even_conv_w, "even_conv_b": even_conv_b,
            "even_dt_bias": even_dt_bias, "even_a_log": even_a_log, "even_d_skip": even_d_skip,
            "even_ssd_norm_w": even_ssd_norm_w, "even_q_norm": even_q_norm,
            "even_k_norm": even_k_norm, "even_w_out": even_w_out,
            "odd_norm_w": odd_norm_w, "odd_w_in": odd_w_in, "odd_q_norm": odd_q_norm,
            "odd_k_norm": odd_k_norm, "odd_w_out": odd_w_out}

def second_block(x, even_norm_w, even_w_in, even_conv_w, even_conv_b, even_dt_bias, even_a_log,
              even_d_skip, even_ssd_norm_w, even_q_norm, even_k_norm, even_w_out,
              odd_norm_w, odd_w_in, odd_q_norm, odd_k_norm, odd_w_out):
    pos = jnp.arange(x.shape[1], dtype=jnp.int32)
    for layer in range(DEPTH):
        li = layer // 2
        if layer % 2 == 0:
            x = ssd_dilated_layer(x, even_norm_w[li], even_w_in[li], even_conv_w[li],
                                  even_conv_b[li], even_dt_bias[li], even_a_log[li],
                                  even_d_skip[li], even_ssd_norm_w[li], even_q_norm[li],
                                  even_k_norm[li], even_w_out[li], pos)
        else:
            x = moba_layer(x, odd_norm_w[li], odd_w_in[li], odd_q_norm[li], odd_k_norm[li],
                           odd_w_out[li], pos)
    return x


def setup_inputs(seed=0):
    out = dict(first_inputs(seed))
    for name, value in second_inputs(seed + 1).items():
        if name != "x":
            out[name + "_2"] = value
    return out


def reference(
    x, mem, positions, ffn1_norm_pre, ffn1_norm_post, ffn1_w_in, ffn1_w_out, mix_norm_pre,
    mix_norm_post, mem_norm, w_mix_in, conv_w, cmp_pos_k, cmp_pos_v, cmp_k_w1, cmp_k_b1,
    cmp_k_w2, cmp_v_w1, cmp_v_b1, cmp_v_w2, w_mem_kv, w_branch_conv, w_branch_nsa, w_branch_mem,
    w_mix_out, ffn2_norm_pre, ffn2_norm_post, ffn2_w_in, ffn2_w_out, even_norm_w_2, even_w_in_2,
    even_conv_w_2, even_conv_b_2, even_dt_bias_2, even_a_log_2, even_d_skip_2,
    even_ssd_norm_w_2, even_q_norm_2, even_k_norm_2, even_w_out_2, odd_norm_w_2, odd_w_in_2,
    odd_q_norm_2, odd_k_norm_2, odd_w_out_2,
):
    x = first_block(
        x, mem, positions, ffn1_norm_pre, ffn1_norm_post, ffn1_w_in, ffn1_w_out, mix_norm_pre,
        mix_norm_post, mem_norm, w_mix_in, conv_w, cmp_pos_k, cmp_pos_v, cmp_k_w1, cmp_k_b1,
        cmp_k_w2, cmp_v_w1, cmp_v_b1, cmp_v_w2, w_mem_kv, w_branch_conv, w_branch_nsa,
        w_branch_mem, w_mix_out, ffn2_norm_pre, ffn2_norm_post, ffn2_w_in, ffn2_w_out,
    )
    return second_block(
        x, even_norm_w_2, even_w_in_2, even_conv_w_2, even_conv_b_2, even_dt_bias_2,
        even_a_log_2, even_d_skip_2, even_ssd_norm_w_2, even_q_norm_2, even_k_norm_2,
        even_w_out_2, odd_norm_w_2, odd_w_in_2, odd_q_norm_2, odd_k_norm_2, odd_w_out_2,
    )


_drawn_inputs = setup_inputs


def setup_inputs(seed=0):
    import zlib

    import numpy as np

    out = dict(_drawn_inputs(seed))
    spreads = {}
    factors = {'mem_norm': 6.194,
     'cmp_pos_k': 8.0,
     'cmp_k_b1': 31.362,
     'cmp_v_b1': 8.0,
     'even_conv_b_2': 8.0,
     'even_ssd_norm_w_2': 2.826,
     'even_q_norm_2': 8.0,
     'even_k_norm_2': 8.0,
     'odd_norm_w_2': 8.0,
     'odd_q_norm_2': 8.0,
     'odd_k_norm_2': 8.0}
    for name, (base, spread) in spreads.items():
        noise = np.random.default_rng([zlib.crc32(name.encode()), seed]).standard_normal(out[name].shape)
        drawn = base * np.exp(spread * noise) if base else spread * noise
        out[name] = jnp.asarray(drawn.astype(out[name].dtype))
    for name, factor in factors.items():
        out[name] = (out[name] * factor).astype(out[name].dtype)
    return out
```

```python
from contextlib import ExitStack

import concourse.bass as bass
import numpy as np
from concourse import mybir

F32 = mybir.dt.float32
F32R = mybir.dt.float32r
I32 = mybir.dt.int32
ALU = mybir.AluOpType
ACT = mybir.ActivationFunctionType
AX = mybir.AxisListType

P = 128
SEQ, NT = 256, 2
D, KD = 1024, 8
DEPTH = 2
FF = 2816
FT = FF // P
CONV, CF = 512, 4
HD = 64
NHEAD = 8
NCMP = SEQ // 16 - 1
ROT = 8
THETA = 500000.0
MAGIC = 1.5 * 2.0**23
SSD_H, DIL_H, MOBA_H = 16, 24, 16
EPS = 1e-6
NEG = -1e30
SCALE = HD**-0.5
SCALE_MEM = 128**-0.5

CHUNK, SLOTS = 3072, 4
ACT_OWN, DVE_OWN = 15, 108
TWO_PI = (6.28125, 0.0019350051879882812, 3.0199159795e-07)
PI_BELOW = 3.1415925
MTILE = KD * P

FFN_CHUNKS, A_CHUNKS, B_CHUNKS, C_CHUNKS, D_CHUNKS = FT, 9, 1, 3, 4
GATE_CHUNKS, BRANCH_CHUNKS, OUT_CHUNKS = 8, 4, 3
AT_FFN1 = 0
AT_A = FFN_CHUNKS
AT_B = AT_A + A_CHUNKS
AT_C = AT_B + B_CHUNKS
AT_D = AT_C + C_CHUNKS
AT_GATE = AT_D + D_CHUNKS
AT_BRANCH = AT_GATE + GATE_CHUNKS
AT_OUT = AT_BRANCH + BRANCH_CHUNKS
AT_FFN2 = AT_OUT + OUT_CHUNKS
LAYER_CHUNKS = AT_FFN2 + FFN_CHUNKS
EVEN_A, EVEN_B, EVEN_OUT = 7, 15, 4
ODD_B, ODD_A, ODD_OUT = 8, 3, 3
AT_EA = DEPTH * LAYER_CHUNKS
AT_EB = AT_EA + EVEN_A
AT_EO = AT_EB + EVEN_B
AT_OB = AT_EO + EVEN_OUT
AT_OA = AT_OB + ODD_B
AT_OO = AT_OA + ODD_A
CHUNKS = AT_OO + ODD_OUT
LAST_SLOT = (LAYER_CHUNKS - 1) % SLOTS
assert LAYER_CHUNKS % SLOTS == 0 and CHUNKS % SLOTS == 0

UNIT, HIGHS = CHUNK // 3, 6
AHEAD = 4
U_FFN1, U_A, U_FFN2, U_EA, U_EB, U_OB, U_OA = (3 * at for at in (AT_FFN1, AT_A, AT_FFN2, AT_EA, AT_EB, AT_OB, AT_OA))
N_FFN, N_A, N_EA, N_EB, N_OB, N_OA = 3 * FT, 26, 20, 44, 24, 8
LAYER_SPLIT = [*range(U_FFN1, U_FFN1 + N_FFN), *range(U_A, U_A + N_A), *range(U_FFN2, U_FFN2 + N_FFN)]
TAIL_SPLIT = [*range(U_EA, U_EA + N_EA), *range(U_EB, U_EB + N_EB), *range(U_OB, U_OB + N_OB),
              *range(U_OA, U_OA + N_OA)]
assert 3 * LAYER_CHUNKS % HIGHS == 0


def occupants(units, before):
    last = {u % HIGHS: n for n, u in zip(range(-HIGHS, 0), before)}
    free_at = []
    for n, u in enumerate(units):
        free_at.append(last[u % HIGHS] + 1)
        last[u % HIGHS] = n
    return free_at


LAYER_ROOM = occupants(LAYER_SPLIT, LAYER_SPLIT[-HIGHS:])
TAIL_ROOM = occupants(TAIL_SPLIT, LAYER_SPLIT[-HIGHS:])


BANKS = {"G": 2, "T": 2, "Y": 4}
MIX_TILES = (
    [n for f in range(CF) for n in (("u", f), ("cg", f), ("bg", f))]
    + [("q", a) for a in range(4)] + [("kslc", 0), ("kwin", 0)]
    + [("kc", 0), ("kc", 1), ("vc", 0), ("vc", 1)] + [("qm", h) for h in range(4)]
)
ROPED = [("q", a) for a in range(4)] + [("kslc", 0), ("kwin", 0)]
MIX_UNITS = [("nsa", u // 2, u % 2) for u in range(8)] + [("mem", h, 0) for h in range(4)]
EVEN_UNITS = [("dil", h, 0) for h in range(8)]
ODD_UNITS = [("moba", h, 0) for h in range(MOBA_H)]
BRANCHES = {"nsa": 2, "mem": 1, "dil": 3, "moba": 1}


class Jobs:

    def __init__(self):
        self.count = dict.fromkeys(BANKS, 0)
        self.number = {}

    def add(self, ring, *name):
        self.number[name] = (ring, self.count[ring])
        self.count[ring] += 1

    def norm(self, name):
        for i in range(NT):
            for half in range(2):
                self.add("T", "norm", name, i, half)

    def four(self, name):
        for j in range(4):
            self.add("Y", name, j)

    def attention(self, tag, units):
        for s in range(len(units) + 2):
            if s < len(units):
                for b in range(BRANCHES[units[s][0]]):
                    self.add("G", "S", tag, s, b)
            if tag == "mix" and s < KD:
                for b in range(3):
                    self.add("G", "gate", s, b)
            if 1 <= s <= len(units):
                for b in range(BRANCHES[units[s - 1][0]]):
                    self.add("T", "PT", tag, s - 1, b)
            if s >= 2:
                self.add("Y", "PV", tag, s - 2)

    def ffn(self, f):
        self.norm(("ffn", f))
        for t in range(FT):
            self.add("G", "ff", f, t)
        self.four(("ffn_out", f))


def layer_jobs():
    j = Jobs()
    j.ffn(0)
    j.norm("mix")
    for kind, at in MIX_TILES:
        j.add("G", kind, at)
    for kind, at in ROPED:
        j.add("T", "rot", kind, at)
    for i in range(NT):
        j.add("Y", "tok", i)
    for h in range(4):
        j.add("G", "mk", h)
    for i in range(NT):
        j.add("Y", "mv", i)
    for c in range(2):
        for m in range(2):
            j.add("G", "hid", c, m)
    for name in (("cmp_kv",), ("cmp_S", 0), ("cmp_S", 1), ("cmp_PT",)):
        j.add("T", *name)
    j.attention("mix", MIX_UNITS)
    for m in range(KD):
        for b in range(3):
            j.add("G", "branch", m, b)
    j.four("mixed")
    j.ffn(1)
    assert all(j.count[r] % BANKS[r] == 0 for r in BANKS), j.count
    return j


def tail_jobs():
    j = Jobs()
    j.norm("even")
    for t in range(16):
        j.add("G", "xbc", t)
    for t in range(4):
        j.add("G", "eg", t)
    for n in range(4):
        j.add("T", "xs", n)
    for c in range(11):
        for i in range(NT):
            j.add("Y", "eb", c, i)
    for i in range(NT):
        j.add("Y", "dt", i)
    for n in range(12):
        j.add("T", "qkT", "dil", n)
    for g in range(4):
        j.add("G", "cb", g)
    for name in ("acs", "acsT"):
        j.add("T", name)
    j.four("scan")
    for n in range(8):
        j.add("G", "decay", n)
    j.attention("dil", EVEN_UNITS)
    for n in range(4):
        j.add("T", "yT", n)
    j.four("even_out")
    j.norm("odd")
    for c in range(6):
        for i in range(NT):
            j.add("Y", "ob", c, i)
    for t in range(8):
        j.add("G", "og", t)
    for n in range(8):
        j.add("T", "qkT", "moba", n)
    j.attention("moba", ODD_UNITS)
    j.four("odd_out")
    return j


FRONT = Jobs()
FRONT.norm("mem")
LAYER, TAIL = layer_jobs(), tail_jobs()

CONST = {
    "ident": P, "causal": 384, "dil0": 384, "dil1": 384, "dil2": 384, "reach": 384,
    "cmp_add": 2 * NCMP, "cmp_one": 2 * NCMP, "upto": P, "ones": P, "rotate": P, "inv": 1,
    "cos2": 2 * ROT, "sin2": 2 * ROT,
}
PARAM = {
    "g1": KD, "gm": KD, "g2": KD, "gmem": KD, "convw": CF * 3, "posk": 16, "posv": 16,
    "b1k": 2, "b1v": 2, "w2k": 2 * HD, "w2v": 2 * HD,
}
PARAM2 = {
    "ge": KD, "go": KD, "gssd": KD, "cw": 64, "cb": 16, "dtb": SSD_H, "alog": SSD_H, "dskip": SSD_H,
    "qn_dil": HD, "kn_dil": HD, "qn_moba": HD, "kn_moba": HD,
}


def columns(table):
    at, found = 0, {}
    for name, n in table.items():
        found[name] = (at, at + n)
        at += n
    return found, at


def build(nc, weights, par, par2, const, posts, x_in, mem_in, pos_in, out):
    ctx = ExitStack()
    with ctx:
        def sb(name, shape, dt=F32):
            return ctx.enter_context(nc.sbuf_tensor(name, shape, dt))

        def sem(name):
            return ctx.enter_context(nc.semaphore(name))

        def bc(ap, axis, n):
            shape = list(ap.shape)
            shape.insert(axis, n)
            return ap.unsqueeze(axis).broadcast_to(shape)

        psum = ctx.enter_context(nc.psum_tensor("psum", [P, 8, 512], F32))
        FIRST_BANK = {"G": 0, "T": 2, "Y": 4}
        full = [sem(f"full{b}") for b in range(8)]
        free = [sem(f"free{b}") for b in range(8)]

        lay = [0]

        class Job:

            def __init__(self, *name, plus=0):
                part = FRONT if name in FRONT.number else LAYER if name in LAYER.number else TAIL
                ring, n = part.number[name]
                self.at = FIRST_BANK[ring] + n % BANKS[ring]
                self.bank = psum[:, self.at, :]
                before = 0
                if part is not FRONT:
                    before = lay[0] * (LAYER.count[ring] // BANKS[ring]) + FRONT.count[ring] // BANKS[ring]
                self.round = before + (n // BANKS[ring]) + plus
                self.full, self.free = full[self.at], free[self.at]

            def wait_empty(self, eng):
                eng.wait_ge(self.free, self.round + 1)

            def wait_full(self, eng):
                eng.wait_ge(self.full, self.round + 1)

            def wait_emptied(self, eng):
                eng.wait_ge(self.free, self.round + 2)

        def all_emptied(eng, names):
            for job in {job.at: job for job in (Job(*name) for name in names)}.values():
                job.wait_emptied(eng)

        class Split:

            def __init__(self, u, it=0):
                tail = u >= U_EA
                table, room = (TAIL_SPLIT, TAIL_ROOM) if tail else (LAYER_SPLIT, LAYER_ROOM)
                if not tail and u >= 3 * LAYER_CHUNKS:
                    n = len(LAYER_SPLIT) + table.index(u - 3 * LAYER_CHUNKS)
                    free_at = n - HIGHS + 1
                else:
                    n = table.index(u)
                    free_at = room[n]
                before, rounds = ((DEPTH * len(LAYER_SPLIT), 0) if tail else
                                  (lay[0] * len(LAYER_SPLIT), lay[0] * (LAYER_CHUNKS // SLOTS)))
                before = before + it * (3 * SLOTS)
                self.slot, part = u // 3 % SLOTS, slice(u % 3 * UNIT, (u % 3 + 1) * UNIT)
                self.arrived = 16 * (rounds + it + (u // 3 // SLOTS + 1))
                self.room = before + (free_at + HIGHS)
                self.count = before + (n + 1)
                self.raw, self.low = ring[:, self.slot, part], ring_r[:, self.slot, part]
                self.high = highs[:, u % HIGHS, :]

        def high_part(eng, u, it=0):
            unit = Split(u, it)
            eng.wait_ge(w_full[unit.slot], unit.arrived)
            eng.wait_ge(h_room, unit.room)
            eng.activation(unit.high, unit.raw, ACT.Copy).then_inc(h_ready, 1)

        def low_part(eng, u, it=0):
            unit = Split(u, it)
            eng.wait_ge(h_ready, unit.count)
            eng.tensor_tensor(unit.low, unit.raw, unit.high.bitcast(F32), ALU.subtract).then_inc(l_ready, 1)

        def two_names(name, shape):
            with nc.sbuf_tensor(name, shape, F32) as plain:
                pass
            return plain, sb(name + "_r", shape, F32R)

        ring, ring_r = two_names("ring", [P, SLOTS, CHUNK])
        cst_at, n_const = columns(CONST)
        par_at, n_par = columns(PARAM)
        par2_at, n_par2 = columns(PARAM2)
        cst = sb("cst", [P, n_const])
        pars = sb("pars", [P, DEPTH * n_par])
        pl = sb("pl", [P, n_par])
        p2 = sb("p2", [P, n_par2])

        def C(name):
            return cst[:, cst_at[name][0]:cst_at[name][1]]

        def A(name):
            return pl[:, par_at[name][0]:par_at[name][1]]

        def A2(name):
            return p2[:, par2_at[name][0]:par2_at[name][1]]

        ident = C("ident")
        x = sb("x", [P, NT, D])
        xs, xs_r = two_names("xs", [P, NT, D])
        hT = sb("hT", [P, KD, SEQ])
        gpost = sb("gpost", [P, 2, D])
        small = sb("small", [P, 96])
        eps = small[:, 0:1]
        ss, std, rstd = small[:, 2:4], small[:, 4:6], small[:, 6:8]
        pss, pstd, prstd = small[:, 8:10], small[:, 10:12], small[:, 12:14]
        mx3 = small[:, 16:28].rearrange("p (u n) -> p u n", u=2)
        nmx = small[:, 28:36].rearrange("p (u n) -> p u n", u=2)
        sm = small[:, 36:44].rearrange("p (u n) -> p u n", u=2)
        rs = small[:, 44:52].rearrange("p (u n) -> p u n", u=2)
        act = sb("act", [P, 2, 2, SEQ])
        sil, gT = act[:, 0], act[:, 1]
        Sb = sb("Sb", [P, 2, 3 * 384])
        PTs, PTs_r = two_names("PTs", [P, 2, 3 * 384])
        Sflat = Sb[:, :, :].rearrange("p u n -> p (u n)")
        PTflat = PTs[:, :, :].rearrange("p u n -> p (u n)")
        junk = Sflat[:, 0:D]
        REGION = 22700
        region, region_r = two_names("region", [P, REGION])

        class Space:

            def __init__(self, ap, size):
                self.ap, self.size, self.at = ap, size, 0

            def take(self, *shape):
                n = int(np.prod(shape))
                a, self.at = self.at, self.at + n
                assert self.at <= self.size, self.at
                names = "abcd"[:len(shape)]
                return self.ap[:, a:a + n].rearrange(
                    f"p ({' '.join(names)}) -> p {' '.join(names)}", **dict(zip(names, shape)))

        r1 = Space(region[:, :], REGION)
        sg = r1.take(KD * 3, SEQ)
        hmT = sg[:, 0:KD, :]
        memT = r1.take(KD, SEQ)
        cosT, sinT = r1.take(SEQ), r1.take(SEQ)
        yconvT, ynsaT, ymemT = r1.take(CF, SEQ), r1.take(4, SEQ), r1.take(4, SEQ)
        ropes = r1.take(2, 6, SEQ)
        rope_in, rope_out = ropes[:, 0], ropes[:, 1]
        mergedT = ropes.rearrange("p a b t -> p (a b) t")[:, 0:KD, :]
        hk, hv = r1.take(2, 2 * NCMP), r1.take(2, 2, 4, 32)
        kcT, vc = r1.take(NCMP), r1.take(2, HD)
        vtok, gate = r1.take(NT, 2 * P), r1.take(NT, 24)
        at_h = r1.at
        mkT, mv, qmT = r1.take(4, SEQ), r1.take(NT, 512), r1.take(4, SEQ)
        cs, cstat = r1.take(NT, NHEAD, NCMP), r1.take(4, NT * NHEAD)
        Pc, PcT = r1.take(NT, NHEAD, 32), r1.take(2, SEQ)
        mt = r1.take(2, SEQ)
        s1 = Space(Sflat, 2304)
        usb, cu, cacc = s1.take(2, SEQ), s1.take(2, SEQ + 2), s1.take(2, SEQ)
        s2 = Space(PTflat, 2304)
        rt = s2.take(2, 2, SEQ)
        flat = s2.take(2, 16, 2, NCMP)
        r2 = Space(region[:, :], REGION)
        qkT = r2.take(24, SEQ)
        QK = r2.take(2, NT, DIL_H * HD)
        V = r2.take(NT, DIL_H * HD)
        xbcT = r2.take(16, SEQ)
        xtok = r2.take(NT, D)
        dts = r2.take(8, NT * SSD_H)
        neg_a = r2.take(SSD_H)
        acsT = r2.take(SEQ)
        stat = r2.take(4, 2 * NT * DIL_H)
        Z = gpost
        egT = act[:, :, :, :].rearrange("p a b t -> p (a b) t")
        s3 = Space(Sflat, 2304)
        xp, cv = s3.take(2, SEQ + 3), s3.take(2, SEQ)
        r3 = Space(QK.rearrange("p a b c -> p (a b c)"), 2 * NT * DIL_H * HD)
        mixedT, cbm, ebuf = r3.take(12, SEQ), r3.take(4, 384), r3.take(2, 2, 384)
        ysb = xbcT[:, 0:8, :].rearrange("p (i f) t -> p i (f t)", i=NT)
        yt = xbcT[:, 8:16, :].rearrange("p (i f) t -> p i (f t)", i=NT)
        ogT = xbcT[:, 0:8, :]
        highs = region_r[:, 0:HIGHS * UNIT].rearrange("p (s c) -> p s c", s=HIGHS)

        def parts(ap):
            return ap.rearrange("p (i k t) -> p i k t", i=NT, k=KD)

        hL = parts(xs_r[:, :, :].rearrange("p i n -> p (i n)"))
        hH1 = parts(region_r[:, at_h:at_h + NT * D])
        hH2 = parts(PTs_r[:, :, :].rearrange("p u n -> p (u n)")[:, 0:NT * D])
        g_parts = region_r[:, at_h + NT * D:at_h + NT * D + 4 * SEQ].rearrange("p (h c t) -> p h c t", h=2, c=2)
        gH, gL = g_parts[:, 0], g_parts[:, 1]

        w_full = [sem(f"w_full{s}") for s in range(SLOTS)]
        w_used = [sem(f"w_used{s}") for s in range(SLOTS)]
        h_ready, l_ready = sem("h_ready"), sem("l_ready")
        h_room = sem("h_room")
        nH_ready, nL_ready = sem("nH_ready"), sem("nL_ready")
        g_steps = sem("g_steps")
        gp_full = [sem(f"gp_full{s}") for s in range(2)]
        const_in, small_in, x_here, mem_here, pos_here = (sem(n) for n in ("const_in", "small_in", "x_here", "mem_here", "pos_here"))
        x_ready = sem("x_ready")
        std_ready = sem("std_ready")
        xs_ready = sem("xs_ready")
        post_std = sem("post_std")
        sil_ready = sem("sil_ready")
        rope_ready, hm_ready = sem("rope_ready"), sem("hm_ready")
        cmp_sub, cmp_exp, cmp_p = sem("cmp_sub"), sem("cmp_exp"), sem("cmp_p")
        mx_ready = sem("mx_ready")
        exp_done = sem("exp_done")
        p_ready = sem("p_ready")
        merged = sem("merged")
        conv_done, conv_act = sem("conv_done"), sem("conv_act")
        qk_var, qk_std, qk_ready = sem("qk_var"), sem("qk_std"), sem("qk_ready")
        dt_abs, dt_exp, a_ready, xdt_ready = sem("dt_abs"), sem("dt_exp"), sem("a_ready"), sem("xdt_ready")
        decay_in, decay_exp, decay_done = sem("decay_in"), sem("decay_exp"), sem("decay_done")
        y_sq, y_std, y_ready = sem("y_sq"), sem("y_std"), sem("y_ready")
        trig_in, trig_done = sem("trig_in"), sem("trig_done")
        stored = sem("stored")

        class Own:

            def __init__(self, eng, counted, per_layer):
                self.eng, self.sem, self.per_layer = eng, counted, per_layer
                self.n = self.before = 0

            def __call__(self, instruction):
                instruction.then_inc(self.sem, 1)
                self.n += 1

            def settle(self):
                self.eng.wait_ge(self.sem, self.before + lay[0] * self.per_layer + self.n)

            def layer_begins(self):
                self.before, self.n = self.n, 0

            def layer_ends(self):
                assert self.n == self.per_layer, (self.sem, self.n)
                self.n = 0

        def layers(eng, body, counter=None):
            if counter is not None:
                counter.layer_begins()
            with eng.Fori(0, DEPTH) as index:
                lay[0] = index
                body()
            if counter is not None:
                counter.layer_ends()
            lay[0] = DEPTH

        def repeat(eng, n, body):
            with eng.Fori(0, n) as index:
                body(index)

        def unit_base(tag):
            return {"mix": lay[0] * len(MIX_UNITS), "dil": DEPTH * len(MIX_UNITS),
                    "moba": DEPTH * len(MIX_UNITS) + len(EVEN_UNITS)}[tag]

        def prob_tiles(kind, s, b):
            p = Sb[:, s % 2, :]
            if kind == "mem":
                at = [i * SEQ + n * P for n in range(NT) for i in range(NT)]
            elif kind == "dil":
                at = [b * P, 384 + b * SEQ, 384 + b * SEQ + P]
            else:
                at = [b * 384 + n * P for n in range(3)]
            return [p[:, a:a + P] for a in at]

        def out_half(unit):
            kind, h, g = unit
            if kind == "mem":
                return slice(0, P)
            half = g if kind == "nsa" else h % 2
            return slice(half * HD, (half + 1) * HD)

        def probs_of(kind, s):
            if kind == "mem":
                return [((0, SEQ), 0), ((SEQ, 2 * SEQ), 1)]
            if kind == "dil":
                return [((0, 384), 0), ((384, 1152), 1)]
            return [(r, 2 * b + i) for b in range(BRANCHES[kind])
                    for i, r in enumerate(((b * 384, b * 384 + P), (b * 384 + P, b * 384 + 384)))]

        block = ctx.enter_context(nc.Block())

        @block.sync
        def _(sp):
            lay[0] = 0
            sp.dma_start(xs[:, :, :], mem_in).then_inc(mem_here, 16)
            sp.dma_start(cst[:, :], const).then_inc(const_in, 16)
            for s in range(SLOTS):
                sp.dma_start(ring[:, s, :], weights[s]).then_inc(w_full[s], 16)

            def round_of_slots(r):
                for s in range(SLOTS):
                    sp.wait_ge(w_used[s], r + (s == LAST_SLOT))
                    sp.dma_start(ring[:, s, :], weights[r * SLOTS + s]).then_inc(w_full[s], 16)

            with sp.Fori(1, CHUNKS // SLOTS) as r:
                round_of_slots(r)
            lay[0] = DEPTH
            for i in range(NT):
                for half in range(2):
                    Job("odd_out", 2 * i + half).wait_emptied(sp)
                sp.dma_start(out[:, i], x[:, i, :]).then_inc(stored, 16)
            sp.wait_ge(stored, 16 * NT)

        @block.gpsimd
        def _(pool):
            lay[0] = 0
            pool.dma_start(x[:, :, :], x_in).then_inc(x_here, 16)
            pool.dma_start(pars[:, :], par).then_inc(small_in, 16)
            pool.dma_start(p2[:, :], par2).then_inc(small_in, 16)
            pool.dma_start(rope_out[:, 0, :].bitcast(I32), pos_in[0].partition_broadcast(P)).then_inc(pos_here, 16)

            def body():
                for j, slot in enumerate((0, 1, 0)):
                    pool.wait_ge(x_ready, 2 + 6 * lay[0] + (2 if j == 2 else 0))
                    pool.dma_start(gpost[:, slot, :], posts[3 * lay[0] + j].partition_broadcast(P))\
                        .then_inc(gp_full[slot], 16)

            layers(pool, body)
            pool.wait_ge(l_ready, DEPTH * len(LAYER_SPLIT) + AHEAD)
            for u in TAIL_SPLIT[AHEAD:]:
                low_part(pool, u)

        @block.tensor
        def _(pe):
            lay[0] = 0
            used = []

            def mm(bank, lhsT, rhs, start, stop, signal=None):
                ins = pe.matmul(bank, lhsT, rhs, start=start, stop=stop)
                if signal is not None:
                    ins.then_inc(signal, 1)
                elif used:
                    ins.then_inc(used.pop(0), 1)

            def turn(bank, tile, signal=None):
                ins = pe.transpose(bank, tile, ident)
                if signal is not None:
                    ins.then_inc(signal, 1)
                elif used:
                    ins.then_inc(used.pop(0), 1)

            def chunk(n, plus=0):
                pe.wait_ge(w_full[n % SLOTS], 16 * (chunk_round(n) + plus + 1))
                return ring[:, n % SLOTS, :]

            def chunk_round(n):
                if n < LAYER_CHUNKS and lay[0] is not DEPTH:
                    return lay[0] * (LAYER_CHUNKS // SLOTS) + n // SLOTS
                return n // SLOTS

            def norm(name, k):
                for i in range(NT):
                    pe.wait_ge(xs_ready, NT * k + i + 1)
                    for half in range(2):
                        job = Job("norm", name, i, half)
                        job.wait_empty(pe)
                        for kk in range(4):
                            f = 4 * half + kk
                            turn(job.bank[:, kk * P:(kk + 1) * P], xs[:, i, f * P:(f + 1) * P],
                                 job.full if kk == 3 else None)

            def normed(name):
                all_emptied(pe, [("norm", name, i, half) for i in range(NT) for half in range(2)])

            def feature_tile(job, w, rhs=hT, k=KD):
                job.wait_empty(pe)
                for kk in range(k):
                    mm(job.bank[:, 0:SEQ], w[:, kk * P:(kk + 1) * P], rhs[:, kk, :],
                       kk == 0, kk == k - 1, job.full if kk == k - 1 else None)

            def parted(k):
                pe.wait_ge(nL_ready, 4 * (k + 1))

            def products(out, lhs, rhs, start, stop, signal=None):
                pairs = ((0, 0), (0, 1), (1, 0))
                for n, (a, b) in enumerate(pairs):
                    mm(out, lhs[a], rhs[b], start and n == 0, stop and n == 2, signal if n == 2 else None)

            def split_tile(job, half, u, it=0, hH=None):
                unit = Split(u, it)
                pe.wait_ge(l_ready, unit.count)
                to = job.bank[:, half * SEQ:(half + 1) * SEQ].rearrange("p (i t) -> p i t", i=NT)
                return unit, [(to, [w[:, kk * P:(kk + 1) * P] for w in (unit.high, unit.low)],
                               [h[:, :, kk, :] for h in (hH, hL)], kk == 0, kk == KD - 1) for kk in range(KD)]

            def split_feature(job, u, hH):
                job.wait_empty(pe)
                _, todo = split_tile(job, 0, u, 0, hH)
                for n, args in enumerate(todo):
                    products(*args, job.full if n == KD - 1 else None)
                used.append(h_room)

            def ffn(f, k):
                at = U_FFN2 if f else U_FFN1
                norm(("ffn", f), k)
                parted(k - 1)
                outs = [Job(("ffn_out", f), j) for j in range(4)]

                def up(t, it=0):
                    job = Job("ff", f, t, plus=2 * it)
                    job.wait_empty(pe)
                    ua, ub = at + (3 * t - 1 if t else 0), at + (3 * t if t else 1)
                    _, todo = split_tile(job, 0, ua, it, hH1)
                    for n, args in enumerate(todo):
                        products(*args, h_room if n == KD - 1 else None)
                    if ua % 3 == 2:
                        used.append(w_used[ua // 3 % SLOTS])
                    _, todo = split_tile(job, 1, ub, it, hH1)
                    for n, args in enumerate(todo):
                        products(*args, job.full if n == KD - 1 else None)
                    used.append(h_room)

                def down(t, it=0, first=False, last=False):
                    Job("ff", f, t, plus=2 * it).wait_emptied(pe)
                    u = at + (3 * t + 4 if t < FT - 1 else 3 * t + 2)
                    unit = Split(u, it)
                    pe.wait_ge(l_ready, unit.count)
                    for j, out_job in enumerate(outs):
                        i, half = j // 2, j % 2
                        if first:
                            out_job.wait_empty(pe)
                        products(out_job.bank, [g[:, t % 2, i * P:(i + 1) * P] for g in (gH, gL)],
                                 [w[:, half * 512:(half + 1) * 512] for w in (unit.high, unit.low)],
                                 first, last, out_job.full if last else h_room if j == 3 else None)
                    if last:
                        used.extend((w_used[u // 3 % SLOTS], h_room))

                up(0)
                up(1)
                down(0, first=True)

                def body(it):
                    for c in range(SLOTS):
                        up(2 + c, it)
                        down(1 + c, it)

                repeat(pe, (FT - 2) // SLOTS, body)
                down(FT - 1, last=True)

            def attention(tag, units, q_of, k_of, v_of, extra=None):
                base = unit_base(tag)

                def scores(s):
                    kind = units[s][0]
                    for b in range(BRANCHES[kind]):
                        job = Job("S", tag, s, b)
                        job.wait_empty(pe)
                        q, k = q_of(s, b), k_of(s, b)
                        if kind == "mem":
                            for i in range(NT):
                                mm(job.bank[:, i * SEQ:(i + 1) * SEQ], q[:, i * P:(i + 1) * P], k,
                                   True, True, job.full if i else None)
                        else:
                            mm(job.bank[:, 0:P], q[:, 0:P], k[:, 0:P], True, True)
                            mm(job.bank[:, P:3 * P], q[:, P:SEQ], k, True, True, job.full)

                def turns(s):
                    pe.wait_ge(p_ready, base + s + 1)
                    for b in range(BRANCHES[units[s][0]]):
                        job = Job("PT", tag, s, b)
                        job.wait_empty(pe)
                        tiles = prob_tiles(units[s][0], s, b)
                        for n, tile in enumerate(tiles):
                            turn(job.bank[:, n * P:(n + 1) * P], tile, job.full if n == len(tiles) - 1 else None)

                def outputs(s):
                    kind = units[s][0]
                    job = Job("PV", tag, s)
                    job.wait_empty(pe)
                    todo = []
                    half = out_half(units[s])
                    for b in range(BRANCHES[kind]):
                        Job("PT", tag, s, b).wait_emptied(pe)
                        pt = PTs[:, s % 2, b * 384:]
                        if kind == "mem":
                            pt = PTs[:, s % 2, :]
                            for n in range(NT):
                                todo.append((job.bank[:, 0:SEQ], v_of(s, b)[n], pt[:, n * SEQ:(n + 1) * SEQ]))
                        else:
                            v0, v1 = v_of(s, b)
                            todo.append((job.bank[half, 0:SEQ], v0, pt[:, 0:SEQ]))
                            todo.append((job.bank[half, P:SEQ], v1, pt[:, SEQ:3 * P]))
                    if kind == "nsa":
                        _, a, g = units[s]
                        rows = slice(32 * a, 32 * a + 32)
                        todo.append((job.bank[half, 0:SEQ], vc[rows, g, :], PcT[rows, g, :]))
                    for n, (o, v, p) in enumerate(todo):
                        mm(o, v, p, n == 0, n == len(todo) - 1, job.full if n == len(todo) - 1 else None)

                for s in range(len(units) + 2):
                    if s < len(units):
                        scores(s)
                    if extra is not None:
                        extra(s)
                    if 1 <= s <= len(units):
                        turns(s - 1)
                    if s >= 2:
                        outputs(s - 2)

            def mixer(k):
                norm("mix", k)
                normed("mix")
                parted(k - 1)
                turn_next = []

                def rotated():
                    if turn_next:
                        kind, at = turn_next.pop(0)
                        Job(kind, at).wait_emptied(pe)
                        job = Job("rot", kind, at)
                        job.wait_empty(pe)
                        pe.matmul(job.bank[:, 0:SEQ], C("rotate"), rope_in[:, ROPED.index((kind, at)), :],
                                  start=True, stop=True).then_inc(job.full, 1)

                for n, (kind, at) in enumerate(MIX_TILES):
                    split_feature(Job(kind, at), U_A + n, hH1)
                    if n % 3 == 2 or n == len(MIX_TILES) - 1:
                        used.append(w_used[(AT_A + n // 3) % SLOTS])
                    rotated()
                    if (kind, at) in ROPED:
                        turn_next.append((kind, at))
                w = chunk(AT_B)
                for i in range(NT):
                    job = Job("tok", i)
                    job.wait_empty(pe)
                    for kk in range(KD):
                        mm(job.bank[:, 0:280], hT[:, kk, i * P:(i + 1) * P], w[:, kk * 280:(kk + 1) * 280],
                           kk == 0, kk == KD - 1, job.full if kk == KD - 1 else None)
                used.append(w_used[AT_B % SLOTS])
                pe.wait_ge(hm_ready, lay[0] + 1)
                w = chunk(AT_C)
                for h in range(3):
                    feature_tile(Job("mk", h), w[:, h * MTILE:], hmT)
                used.append(w_used[AT_C % SLOTS])
                w = chunk(AT_C + 1)
                feature_tile(Job("mk", 3), w, hmT)
                jobs = [Job("mv", i) for i in range(NT)]
                for kk in range(KD):
                    if kk == 4:
                        used.append(w_used[(AT_C + 1) % SLOTS])
                        w = chunk(AT_C + 2)
                    at = (MTILE if kk < 4 else 0) + kk % 4 * 512
                    for i, job in enumerate(jobs):
                        if kk == 0:
                            job.wait_empty(pe)
                        mm(job.bank, hmT[:, kk, i * P:(i + 1) * P], w[:, at:at + 512],
                           kk == 0, kk == KD - 1, job.full if kk == KD - 1 else None)
                used.append(w_used[(AT_C + 2) % SLOTS])
                for c in range(2):
                    for g in range(2):
                        Job("kc" if c == 0 else "vc", g).wait_emptied(pe)
                    jobs = [Job("hid", c, m) for m in range(2)]
                    for jj in range(16):
                        if jj % 8 == 0:
                            w = chunk(AT_D + 2 * c + jj // 8)
                        for m, job in enumerate(jobs):
                            if jj == 0:
                                job.wait_empty(pe)
                            at = jj % 8 * 256 + m * P
                            mm(job.bank[:, 0:2 * NCMP], w[:, at:at + P],
                               flat[:, c, jj, :, :].rearrange("p g n -> p (g n)"),
                               jj == 0, jj == 15, job.full if jj == 15 else None)
                        if jj % 8 == 7:
                            used.append(w_used[(AT_D + 2 * c + jj // 8) % SLOTS])
                job = Job("cmp_kv")
                job.wait_empty(pe)
                for m in range(2):
                    Job("hid", 0, m).wait_emptied(pe)
                for g in range(2):
                    for m in range(2):
                        mm(job.bank[g * HD:(g + 1) * HD, 0:NCMP], A("w2k")[:, m * HD:(m + 1) * HD],
                           hk[:, m, g * NCMP:(g + 1) * NCMP], m == 0, m == 1)
                for m in range(2):
                    Job("hid", 1, m).wait_emptied(pe)
                for g in range(2):
                    for m in range(2):
                        mm(job.bank[:, (g + 1) * HD:(g + 2) * HD], hv[:, m, g].rearrange("p j n -> p (j n)"),
                           A("w2v")[:, m * HD:(m + 1) * HD], m == 0, m == 1, job.full if g and m else None)
                job.wait_emptied(pe)
                for g in range(2):
                    job = Job("cmp_S", g)
                    job.wait_empty(pe)
                    rows = slice(g * HD, (g + 1) * HD)
                    for i in range(NT):
                        for a in range(4):
                            at = (i * 4 + a) * NCMP
                            mm(job.bank[:, at:at + NCMP], rope_in[rows, a, i * P:(i + 1) * P], kcT[rows, :],
                               True, True, job.full if i and a == 3 else None)

                def compressed_turned():
                    pe.wait_ge(cmp_p, lay[0] + 1)
                    job = Job("cmp_PT")
                    job.wait_empty(pe)
                    for g in range(2):
                        for i in range(NT):
                            turn(job.bank[:, g * SEQ + i * P:g * SEQ + (i + 1) * P],
                                 Pc[:, i, 4 * g:4 * g + 4, :].rearrange("p h n -> p (h n)"),
                                 job.full if g and i else None)

                def gates(s):
                    if s < KD:
                        w = chunk(AT_GATE + s)
                        for b in range(3):
                            feature_tile(Job("gate", s, b), w[:, b * MTILE:])
                        used.append(w_used[(AT_GATE + s) % SLOTS])
                    if s == 0:
                        compressed_turned()

                def q_of(s, b):
                    kind, a, g = MIX_UNITS[s]
                    return qmT[:, a, :] if kind == "mem" else rope_out[g * HD:(g + 1) * HD, a, :]

                def k_of(s, b):
                    kind, a, g = MIX_UNITS[s]
                    return mkT[:, a, :] if kind == "mem" else rope_out[g * HD:(g + 1) * HD, 4 + b, :]

                def v_of(s, b):
                    kind, a, g = MIX_UNITS[s]
                    if kind == "mem":
                        return [mv[:, n, a * P:(a + 1) * P] for n in range(NT)]
                    at = b * P + g * HD
                    return [vtok[:, n, at:at + HD] for n in range(NT)]

                pe.wait_ge(rope_ready, (lay[0] + 1) * len(ROPED))
                all_emptied(pe, [(n, i) for n in ("tok", "mv") for i in range(NT)]
                            + [(n, h) for n in ("qm", "mk") for h in range(4)])
                attention("mix", MIX_UNITS, q_of, k_of, v_of, gates)
                all_emptied(pe, [("PV", "mix", u) for u in range(len(MIX_UNITS))])
                for m in range(KD):
                    if m % 2 == 0:
                        w = chunk(AT_BRANCH + m // 2)
                    for b, y in enumerate((yconvT, ynsaT, ymemT)):
                        feature_tile(Job("branch", m, b), w[:, (m % 2 * 3 + b) * 512:], y, 4)
                    if m % 2 == 1:
                        used.append(w_used[(AT_BRANCH + m // 2) % SLOTS])
                project("mixed", AT_OUT, KD, mergedT, lambda kk: pe.wait_ge(merged, KD * lay[0] + kk + 1))

            def project(name, at, k, lhs, before):
                jobs = [Job(name, j) for j in range(4)]
                for kk in range(k):
                    if kk % 3 == 0:
                        w = chunk(at + kk // 3)
                    before(kk)
                    for j, job in enumerate(jobs):
                        i, half = j // 2, j % 2
                        if kk == 0:
                            job.wait_empty(pe)
                        c = kk % 3 * D + half * 512
                        mm(job.bank, lhs[:, kk, i * P:(i + 1) * P], w[:, c:c + 512],
                           kk == 0, kk == k - 1, job.full if kk == k - 1 else None)
                    if kk % 3 == 2 or kk == k - 1:
                        used.append(w_used[(at + kk // 3) % SLOTS])

            def token_blocks(name, blocks, at):
                for c in range(blocks):
                    jobs = [Job(name, c, i) for i in range(NT)]
                    for kk in range(KD):
                        n = c * KD + kk
                        if n % 2 == 0:
                            unit = Split(3 * at + n // 2)
                            pe.wait_ge(l_ready, unit.count)
                        for i, job in enumerate(jobs):
                            if kk == 0:
                                job.wait_empty(pe)
                            products(job.bank, [h[:, i, kk, :] for h in (hH2, hL)],
                                     [w[:, n % 2 * 512:(n % 2 + 1) * 512] for w in (unit.high, unit.low)],
                                     kk == 0, kk == KD - 1, job.full if kk == KD - 1 else None)
                        if n % 2:
                            used.append(h_room)
                        if n % 6 == 5:
                            used.append(w_used[(at + n // 6) % SLOTS])

            def heads_turned(tag, n_jobs, tiles):
                for n in range(n_jobs):
                    qk, f = divmod(2 * n, tiles)
                    job = Job("qkT", tag, n)
                    job.wait_empty(pe)
                    base = 4 if tag == "moba" else 0
                    pe.wait_ge(qk_ready, base + 2 * qk + 2)
                    for t in range(2):
                        for i in range(NT):
                            turn(job.bank[:, t * SEQ + i * P:t * SEQ + (i + 1) * P],
                                 QK[:, qk, i, (f + t) * P:(f + t + 1) * P], job.full if t and i else None)
                all_emptied(pe, [("qkT", tag, n) for n in range(n_jobs)])

            pe.wait_ge(const_in, 16)
            pe.wait_ge(small_in, 32)
            norm("mem", 0)

            def body():
                used[:] = [w_used[LAST_SLOT], h_room]
                ffn(0, 1 + 3 * lay[0])
                mixer(2 + 3 * lay[0])
                ffn(1, 3 + 3 * lay[0])
                assert used == [w_used[LAST_SLOT], h_room] and used[1] is h_room

            layers(pe, body)

            norm("even", 7)
            normed("even")
            parted(6)
            for n in range(20):
                split_feature(Job("xbc", n) if n < 16 else Job("eg", n - 16), U_EA + n, hH2)
                if n % 3 == 2 or n == 19:
                    used.append(w_used[(AT_EA + n // 3) % SLOTS])
            pe.wait_ge(conv_act, 16)
            for n in range(4):
                i, half = n // 2, n % 2
                job = Job("xs", n)
                job.wait_empty(pe)
                for kk in range(4):
                    turn(job.bank[:, kk * P:(kk + 1) * P], xbcT[:, 4 * half + kk, i * P:(i + 1) * P],
                         job.full if kk == 3 else None)
            token_blocks("eb", 11, AT_EB)
            w = chunk(AT_EO - 1)
            for i in range(NT):
                job = Job("dt", i)
                job.wait_empty(pe)
                for kk in range(KD):
                    at = 4 * 512 + kk * SSD_H
                    mm(job.bank[:, 0:SSD_H], hT[:, kk, i * P:(i + 1) * P], w[:, at:at + SSD_H],
                       kk == 0, kk == KD - 1, job.full if kk == KD - 1 else None)
            used.append(w_used[(AT_EO - 1) % SLOTS])
            heads_turned("dil", 12, 12)
            for g in range(4):
                job = Job("cb", g)
                job.wait_empty(pe)
                b_, c_ = xbcT[:, 8 + g, :], xbcT[:, 12 + g, :]
                mm(job.bank[:, 0:SEQ], b_[:, 0:P], c_, True, True)
                mm(job.bank[:, SEQ:3 * P], b_[:, P:SEQ], c_[:, P:SEQ], True, True, job.full)
            pe.wait_ge(a_ready, 1)
            job = Job("acs")
            job.wait_empty(pe)
            a = dts[:, 7, :].rearrange("p (i h) -> p i h", i=NT)
            mm(job.bank[:, 0:SSD_H], C("upto"), a[:, 0, :], True, True)
            mm(job.bank[:, SSD_H:2 * SSD_H], C("ones"), a[:, 0, :], True, False)
            mm(job.bank[:, SSD_H:2 * SSD_H], C("upto"), a[:, 1, :], False, True, job.full)
            job.wait_emptied(pe)
            acs = dts[:, 2, :].rearrange("p (i h) -> p i h", i=NT)
            job = Job("acsT")
            job.wait_empty(pe)
            for i in range(NT):
                turn(job.bank[0:SSD_H, i * P:(i + 1) * P], acs[:, i, :], job.full if i else None)
            job.wait_emptied(pe)
            pe.wait_ge(xdt_ready, 1)
            outs = [Job("scan", j) for j in range(4)]
            for n in range(9):
                if n < 8:
                    job = Job("decay", n)
                    job.wait_empty(pe)
                    for hh in range(2):
                        h = 2 * n + hh
                        mm(job.bank[:, hh * SEQ:(hh + 1) * SEQ], ident[0:SSD_H, h:h + 1].broadcast_to([SSD_H, P]),
                           acsT[0:SSD_H, :], True, True, job.full if hh else None)
                if n >= 1:
                    pe.wait_ge(decay_done, n)
                    for hh in range(2):
                        h = 2 * (n - 1) + hh
                        e, cols = ebuf[:, (n - 1) % 2, hh, :], slice(h % 8 * HD, (h % 8 + 1) * HD)
                        j0, j1 = outs[h // 8], outs[2 + h // 8]
                        if h % 8 == 0:
                            j0.wait_empty(pe)
                            j1.wait_empty(pe)
                        last = h % 8 == 7
                        mm(j0.bank[:, cols], e[:, 0:P], xs[:, 0, h * HD:(h + 1) * HD], True, True,
                           j0.full if last else None)
                        mm(j1.bank[:, cols], e[:, P:2 * P], xs[:, 0, h * HD:(h + 1) * HD], True, False)
                        mm(j1.bank[:, cols], e[:, 2 * P:3 * P], xs[:, 1, h * HD:(h + 1) * HD], False, True,
                           j1.full if last else None)

            def head_rows(tile, half):
                return qkT[half * HD:(half + 1) * HD, tile, :]

            attention("dil", EVEN_UNITS,
                      lambda s, b: head_rows(4 * b + s // 2, s % 2),
                      lambda s, b: head_rows(12 + 4 * b + s // 2, s % 2),
                      lambda s, b: [V[:, n, (8 * b + s) * HD:(8 * b + s + 1) * HD] for n in range(NT)])
            pe.wait_ge(y_ready, 1)
            for n in range(4):
                i, half = n // 2, n % 2
                job = Job("yT", n)
                job.wait_empty(pe)
                for kk in range(4):
                    f = 4 * half + kk
                    turn(job.bank[:, kk * P:(kk + 1) * P], ysb[:, i, f * P:(f + 1) * P],
                         job.full if kk == 3 else None)
            all_emptied(pe, [("yT", n) for n in range(4)] + [("PV", "dil", s) for s in range(8)])
            project("even_out", AT_EO, 12, mixedT, lambda kk: None)

            norm("odd", 8)
            normed("odd")
            parted(7)
            token_blocks("ob", 6, AT_OB)
            for n in range(8):
                split_feature(Job("og", n), U_OA + n, hH2)
                if n % 3 == 2 or n == 7:
                    used.append(w_used[(AT_OA + n // 3) % SLOTS])
            heads_turned("moba", 8, 8)
            attention("moba", ODD_UNITS,
                      lambda s, b: head_rows(s // 2, s % 2),
                      lambda s, b: head_rows(8 + s // 2, s % 2),
                      lambda s, b: [V[:, n, s * HD:(s + 1) * HD] for n in range(NT)])
            all_emptied(pe, [("PV", "moba", s) for s in range(MOBA_H)])
            project("odd_out", AT_OO, 8, mixedT, lambda kk: None)

        @block.scalar
        def _(act_):
            lay[0] = 0
            own = Own(act_, sem("act_own"), ACT_OWN)

            def norm(k, source=x, after=None):
                for i in range(NT):
                    if after is not None:
                        for half in range(2):
                            Job(after, 2 * i + half).wait_emptied(act_)
                    elif source is x:
                        act_.wait_ge(x_ready, NT * (k - 1) + i + 1)
                    own(act_.activation(junk, source[:, i, :], ACT.Square, accum_out=ss[:, i:i + 1]))
                    own.settle()
                    act_.activation(std[:, i:i + 1], ss[:, i:i + 1], ACT.Sqrt, bias=eps, scale=1.0 / D)\
                        .then_inc(std_ready, 1)

            def post(name):
                for i in range(NT):
                    for half in range(2):
                        Job(name, 2 * i + half).wait_full(act_)
                    y = psum[:, 4 + 2 * i:6 + 2 * i, :].rearrange("p b n -> p (b n)")
                    own(act_.activation(junk, y, ACT.Square, accum_out=pss[:, i:i + 1]))
                    own.settle()
                    act_.activation(pstd[:, i:i + 1], pss[:, i:i + 1], ACT.Sqrt, bias=eps, scale=1.0 / D)\
                        .then_inc(post_std, 1)

            def split(first, lo, hi):
                for u in range(first + lo, first + hi):
                    high_part(act_, u)

            def norm_parts(name, hH):
                for i in range(NT):
                    for half in range(2):
                        Job("norm", name, i, half).wait_emptied(act_)
                        act_.activation(hH[:, i, 4 * half:4 * half + 4, :],
                                        hT[:, 4 * half:4 * half + 4, i * P:(i + 1) * P], ACT.Copy).then_inc(nH_ready, 1)

            def ffn(f, k):
                norm(k)
                norm_parts(("ffn", f), hH1)
                first = U_FFN2 if f else U_FFN1
                split(first, AHEAD, HIGHS)

                def silu(t, it=0):
                    job = Job("ff", f, t, plus=2 * it)
                    job.wait_full(act_)
                    act_.activation(sil[:, t % 2, :], job.bank[:, 0:SEQ], ACT.Silu).then_inc(sil_ready, 1)

                def body(it):
                    for c in range(SLOTS):
                        silu(c, it)
                        for n in range(3):
                            high_part(act_, first + HIGHS + 3 * c + n, it)

                repeat(act_, (FT - 2) // SLOTS, body)
                silu(FT - 2)
                silu(FT - 1)
                split(U_A if f == 0 else 3 * LAYER_CHUNKS, 0, AHEAD)
                post(("ffn_out", f))

            def copy(job, dst, src, func=ACT.Copy, **kw):
                job.wait_full(act_)
                act_.activation(dst, src, func, **kw).then_inc(job.free, 1)

            def attention(tag, units, extra=None):
                base = unit_base(tag)

                def exps(s):
                    kind = units[s][0]
                    act_.wait_ge(mx_ready, base + s + 1)
                    scale = SCALE_MEM if kind == "mem" else SCALE
                    todo = probs_of(kind, s)
                    for n, ((a, b), c) in enumerate(todo):
                        ins = act_.activation(Sb[:, s % 2, a:b], Sb[:, s % 2, a:b], ACT.Exp, bias=nmx[:, s % 2, c:c + 1],
                                              scale=scale, accum_out=sm[:, s % 2, c:c + 1])
                        if n == len(todo) - 1:
                            ins.then_inc(exp_done, 1)

                def evacuate(s):
                    kind = units[s][0]
                    for b in range(BRANCHES[kind]):
                        job = Job("PT", tag, s, b)
                        if b == 0 and s >= 2:
                            Job("PV", tag, s - 2).wait_full(act_)
                        n = 512 if kind == "mem" else 384
                        copy(job, PTs[:, s % 2, b * 384:b * 384 + n], job.bank[:, 0:n])

                for s in range(len(units) + 1):
                    if s < len(units):
                        exps(s)
                    if extra is not None:
                        extra(s)
                    if s >= 1:
                        evacuate(s - 1)

            def mixer(k):
                norm(k)
                norm_parts("mix", hH1)
                split(U_A, AHEAD, HIGHS)
                for n, (kind, at) in enumerate(MIX_TILES):
                    if 1 <= n < N_A - HIGHS + 1:
                        high_part(act_, U_A + n + HIGHS - 1)
                    job = Job(kind, at)
                    if kind == "u":
                        copy(job, usb[:, at % 2, :], job.bank[:, 0:SEQ])
                    elif (kind, at) in ROPED:
                        copy(job, rope_in[:, ROPED.index((kind, at)), :], job.bank[:, 0:SEQ])
                    elif kind == "qm":
                        copy(job, qmT[:, at, :], job.bank[:, 0:SEQ])
                for i in range(NT):
                    job = Job("tok", i)
                    job.wait_full(act_)
                    own(act_.activation(vtok[:, i, :], job.bank[:, 0:2 * P], ACT.Copy))
                    copy(job, gate[:, i, :], job.bank[:, 2 * P:2 * P + 24], ACT.Sigmoid)
                for h in range(4):
                    job = Job("mk", h)
                    copy(job, mkT[:, h, :], job.bank[:, 0:SEQ])
                for i in range(NT):
                    job = Job("mv", i)
                    copy(job, mv[:, i, :], job.bank)
                for m in range(2):
                    job = Job("hid", 0, m)
                    copy(job, hk[:, m, :], job.bank[:, 0:2 * NCMP], ACT.Gelu_apprx_tanh, bias=A("b1k")[:, m:m + 1])
                for m in range(2):
                    job = Job("hid", 1, m)
                    job.wait_full(act_)
                    for g in range(2):
                        ins = act_.activation(hv[:, m, g, :, 0:NCMP],
                                              bc(job.bank[:, g * NCMP:(g + 1) * NCMP], 1, 4),
                                              ACT.Gelu_apprx_tanh, bias=A("b1v")[:, m:m + 1])
                        if g == 1:
                            ins.then_inc(job.free, 1)
                job = Job("cmp_kv")
                job.wait_full(act_)
                own(act_.activation(kcT, job.bank[:, 0:NCMP], ACT.Copy))
                copy(job, vc, job.bank[:, HD:3 * HD].rearrange("p (g d) -> p g d", g=2))
                act_.wait_ge(cmp_sub, lay[0] + 1)
                act_.activation(cs, cs, ACT.Exp, scale=SCALE).then_inc(cmp_exp, 1)

                def gates(s):
                    if s < KD:
                        for b in range(3):
                            job = Job("gate", s, b)
                            copy(job, sg[:, 3 * s + b, :], job.bank[:, 0:SEQ], ACT.Sigmoid)
                    if s == 0:
                        job = Job("cmp_PT")
                        copy(job, PcT, job.bank.rearrange("p (g t) -> p g t", g=2))

                attention("mix", MIX_UNITS, gates)
                act_.wait_ge(merged, KD * lay[0] + KD)
                split(U_FFN2, 0, AHEAD)
                post("mixed")

            act_.wait_ge(mem_here, 16)
            act_.wait_ge(x_ready, 2)
            norm(0, xs)
            act_.activation(small[:, 14:15], eps, ACT.Copy).then_inc(h_room, HIGHS - 1)
            split(U_FFN1, 0, AHEAD)
            act_.wait_ge(trig_in, 1)
            act_.wait_ge(xs_ready, NT)
            own(act_.activation(sinT, sinT, ACT.Sin))
            act_.activation(cosT, cosT, ACT.Sin).then_inc(trig_done, 1)

            def body():
                ffn(0, 1 + 3 * lay[0])
                mixer(2 + 3 * lay[0])
                ffn(1, 3 + 3 * lay[0])

            layers(act_, body, own)

            norm(7)
            norm_parts("even", hH2)
            split(U_EA, AHEAD, HIGHS)
            act_.wait_ge(conv_done, 1)

            def convolved(t):
                act_.wait_ge(conv_done, t + 2)
                act_.activation(xbcT[:, t, :], cv[:, t % 2, :], ACT.Silu, bias=A2("cb")[:, t:t + 1])\
                    .then_inc(conv_act, 1)

            for t in range(16):
                if 1 <= t < N_EA - HIGHS + 1:
                    high_part(act_, U_EA + t + HIGHS - 1)
                job = Job("xbc", t)
                copy(job, xp[:, t % 2, 3:3 + SEQ], job.bank[:, 0:SEQ])
                if t >= 1:
                    convolved(t - 1)
            convolved(15)
            for t in range(4):
                job = Job("eg", t)
                copy(job, egT[:, t, :], job.bank[:, 0:SEQ], ACT.Silu)
            split(U_EB, 0, 4)
            for n in range(4):
                i, half = n // 2, n % 2
                job = Job("xs", n)
                copy(job, xtok[:, i, half * 512:(half + 1) * 512], job.bank)

            def qk_roots(n, heads):
                act_.wait_ge(qk_var, n)
                v = stat[:, 1, 0:4 * heads]
                act_.activation(stat[:, 2, 0:4 * heads], v, ACT.Sqrt).then_inc(qk_std, 1)

            for c in range(11):
                split(U_EB, 4 * c + 4, min(4 * c + 8, N_EB))
                for i in range(NT):
                    job = Job("eb", c, i)
                    if c < 6:
                        copy(job, QK[:, c // 3, i, c % 3 * 512:(c % 3 + 1) * 512], job.bank)
                    elif c < 9:
                        copy(job, V[:, i, (c - 6) * 512:(c - 5) * 512], job.bank)
                    else:
                        copy(job, Z[:, i, (c - 9) * 512:(c - 8) * 512], job.bank, ACT.Silu)
                if c == 8:
                    qk_roots(1, DIL_H)
            dt3 = dts[:, :, :].rearrange("p k (i h) -> p k i h", i=NT)
            for i in range(NT):
                job = Job("dt", i)
                copy(job, dt3[:, 0, i, :], job.bank[:, 0:SSD_H])
            own(act_.activation(neg_a, A2("alog"), ACT.Exp))
            act_.wait_ge(dt_abs, 1)
            act_.activation(dts[:, 2, :], dts[:, 2, :], ACT.Exp, scale=-1.0).then_inc(dt_exp, 1)
            for n in range(12):
                job = Job("qkT", "dil", n)
                copy(job, qkT[:, 2 * n:2 * n + 2, :], job.bank.rearrange("p (t s) -> p t s", t=2))
            job = Job("acs")
            copy(job, dts[:, 2, :], job.bank[:, 0:2 * SSD_H])
            job = Job("acsT")
            copy(job, acsT[0:SSD_H, :], job.bank[0:SSD_H, 0:SEQ])
            for n in range(8):
                act_.wait_ge(decay_in, n + 1)
                e = ebuf[:, n % 2]
                act_.activation(e, e, ACT.Exp).then_inc(decay_exp, 1)
            attention("dil", EVEN_UNITS)
            act_.wait_ge(y_sq, 1)
            act_.activation(stat[:, 1, 0:8], stat[:, 0, 0:8], ACT.Sqrt, bias=eps, scale=1.0 / 256)\
                .then_inc(y_std, 1)

            split(U_OB, 0, AHEAD)
            norm(8, after="even_out")
            norm_parts("odd", hH2)
            for c in range(6):
                split(U_OB, 4 * c + 4, 4 * c + 8)
                for i in range(NT):
                    job = Job("ob", c, i)
                    dst = QK[:, c // 2, i] if c < 4 else V[:, i, :]
                    copy(job, dst[:, c % 2 * 512:(c % 2 + 1) * 512], job.bank)
            qk_roots(2, MOBA_H)
            for t in range(8):
                if t + 4 < N_OA:
                    high_part(act_, U_OA + t + 4)
                job = Job("og", t)
                copy(job, ogT[:, t, :], job.bank[:, 0:SEQ], ACT.Silu)
            for n in range(8):
                job = Job("qkT", "moba", n)
                copy(job, qkT[:, 2 * n:2 * n + 2, :], job.bank.rearrange("p (t s) -> p t s", t=2))
            attention("moba", ODD_UNITS)

        @block.vector
        def _(dve):
            lay[0] = 0
            own = Own(dve, sem("dve_own"), DVE_OWN)

            def norm(name, k, gain, dst=hT, source=x):
                for i in range(NT):
                    dve.wait_ge(std_ready, NT * k + i + 1)
                    own(dve.reciprocal(rstd[:, i:i + 1], std[:, i:i + 1]))
                    own.settle()
                    dve.tensor_scalar(xs[:, i, :], source[:, i, :], rstd[:, i:i + 1], None, ALU.mult)\
                        .then_inc(xs_ready, 1)
                for i in range(NT):
                    for half in range(2):
                        job = Job("norm", name, i, half)
                        job.wait_full(dve)
                        to = dst[:, 4 * half:4 * half + 4, i * P:(i + 1) * P]
                        tiles = job.bank.rearrange("p (k t) -> p k t", k=4)
                        if gain is None:
                            ins = dve.tensor_copy(to, tiles)
                        else:
                            ins = dve.tensor_tensor(to, tiles, bc(gain[:, 4 * half:4 * half + 4], 2, P), ALU.mult)
                        ins.then_inc(job.free, 1)

            def norm_parts(name, k, hH):
                for i in range(NT):
                    for half in range(2):
                        dve.wait_ge(nH_ready, 4 * k + 2 * i + half + 1)
                        ks = slice(4 * half, 4 * half + 4)
                        dve.tensor_tensor(hL[:, i, ks, :], hT[:, ks, i * P:(i + 1) * P], hH[:, i, ks, :].bitcast(F32),
                                          ALU.subtract).then_inc(nL_ready, 1)

            def split(first, lo, hi):
                for u in range(first + lo, first + hi):
                    low_part(dve, u)

            def post(name, p, slot, loads, weight):
                dve.wait_ge(gp_full[slot], 16 * loads)
                for i in range(NT):
                    dve.wait_ge(post_std, NT * p + i + 1)
                    own(dve.reciprocal(prstd[:, i:i + 1], pstd[:, i:i + 1]))
                    own.settle()
                    if weight != 1.0:
                        own(dve.tensor_scalar(prstd[:, i:i + 1], prstd[:, i:i + 1], weight, None, ALU.mult))
                        own.settle()
                    jobs = [Job(name, 2 * i + half) for half in range(2)]
                    for half, job in enumerate(jobs):
                        cols = slice(half * 512, (half + 1) * 512)
                        dve.scalar_tensor_tensor(xs[:, i, cols], job.bank, prstd[:, i:i + 1], gpost[:, slot, cols],
                                                 ALU.mult, ALU.mult).then_inc(job.free, 1)
                    for job in jobs:
                        job.wait_emptied(dve)
                    dve.tensor_tensor(x[:, i, :], x[:, i, :], xs[:, i, :], ALU.add).then_inc(x_ready, 1)

            def ffn(f, k, gain):
                norm(("ffn", f), k, gain)
                norm_parts(("ffn", f), k - 1, hH1)
                first = U_FFN2 if f else U_FFN1
                split(first, AHEAD, HIGHS)

                def gated(t, it=0):
                    job = Job("ff", f, t, plus=2 * it)
                    before = lay[0] * (2 * FT) + it * SLOTS + (f * FT + t)
                    dve.wait_ge(sil_ready, before + 1)
                    g = gT[:, t % 2, :]
                    dve.tensor_tensor(g, sil[:, t % 2, :], job.bank[:, SEQ:2 * SEQ], ALU.mult).then_inc(g_steps, 1)
                    dve.wait_ge(g_steps, 2 * before + 1)
                    dve.tensor_copy(gH[:, t % 2, :], g).then_inc(g_steps, 1)
                    dve.wait_ge(g_steps, 2 * before + 2)
                    dve.tensor_tensor(gL[:, t % 2, :], g, gH[:, t % 2, :].bitcast(F32), ALU.subtract)\
                        .then_inc(job.free, 1)

                def body(it):
                    for c in range(SLOTS):
                        gated(c, it)
                        for n in range(3):
                            low_part(dve, first + HIGHS + 3 * c + n, it)

                repeat(dve, (FT - 2) // SLOTS, body)
                gated(FT - 2)
                gated(FT - 1)
                split(U_A if f == 0 else 3 * LAYER_CHUNKS, 0, AHEAD)

            def attention(tag, units, evacuate):
                base = unit_base(tag)

                def front(s):
                    kind = units[s][0]
                    S_, m = Sb[:, s % 2, :], mx3[:, s % 2, :]
                    if s >= 2:
                        Job("PT", tag, s - 2, BRANCHES[units[s - 2][0]] - 1).wait_full(dve)
                    for b in range(BRANCHES[kind]):
                        job = Job("S", tag, s, b)
                        job.wait_full(dve)
                        if kind == "mem":
                            own(dve.tensor_reduce(m[:, 0:2], job.bank.rearrange("p (i n) -> p i n", i=NT), AX.X, ALU.max))
                            dve.tensor_copy(S_[:, 0:512], job.bank).then_inc(job.free, 1)
                            continue
                        own(dve.memset(small[:, 64 + 2 * s + b % 2:65 + 2 * s + b % 2], 0.0))
                        mask = C(f"dil{b}") if kind == "dil" else C("causal")
                        if kind == "dil":
                            to, at = [(b * P, P), (384 + b * SEQ, SEQ)], (b, 3 + b)
                        else:
                            to, at = [(b * 384, P), (b * 384 + P, SEQ)], (2 * b, 2 * b + 1)
                        for i, ((o, n), c) in enumerate(zip(to, at)):
                            src = i * P
                            ins = dve.tensor_tensor_reduce(S_[:, o:o + n], job.bank[:, src:src + n], mask[:, src:src + n],
                                                           1.0, NEG, ALU.add, ALU.max, m[:, c:c + 1])
                            if i:
                                ins.then_inc(job.free, 1)
                            else:
                                own(ins)
                    job.wait_emptied(dve)
                    if kind == "dil":
                        own(dve.tensor_reduce(m[:, 0:2], m[:, 0:6].rearrange("p (i b) -> p i b", i=NT), AX.X, ALU.max))
                        own.settle()
                    n = len(probs_of(kind, s))
                    dve.tensor_scalar(nmx[:, s % 2, 0:n], m[:, 0:n], -(SCALE_MEM if kind == "mem" else SCALE), None,
                                      ALU.mult).then_inc(mx_ready, 1)

                def back(s):
                    kind, a, g = units[s]
                    dve.wait_ge(exp_done, base + s + 1)
                    todo = probs_of(kind, s)
                    r = rs[:, s % 2, 0:len(todo)]
                    own(dve.reciprocal(r, sm[:, s % 2, 0:len(todo)]))
                    own.settle()
                    if kind == "nsa":
                        h = 4 * g + a
                        w = gate[:, :, 3 * h + 1:3 * h + 3].rearrange("p i b -> p b i")
                        own(dve.tensor_tensor(r.rearrange("p (b i) -> p b i", b=2), r.rearrange("p (b i) -> p b i", b=2),
                                              w, ALU.mult))
                        own.settle()
                    for n, ((u, v), c) in enumerate(todo):
                        ins = dve.tensor_scalar(Sb[:, s % 2, u:v], Sb[:, s % 2, u:v], r[:, c:c + 1], None, ALU.mult)
                        if n == len(todo) - 1:
                            ins.then_inc(p_ready, 1)

                def collect(s):
                    job = Job("PV", tag, s)
                    job.wait_full(dve)
                    evacuate(units[s], job, out_half(units[s]))

                for s in range(len(units) + 3):
                    if s < len(units):
                        front(s)
                    if 1 <= s <= len(units):
                        back(s - 1)
                    if s >= 3:
                        collect(s - 3)

            def mixer(k, p):
                norm("mix", k, A("gm"))
                norm_parts("mix", k - 1, hH1)
                split(U_A, AHEAD, HIGHS)
                own(dve.memset(cu[:, :, 0:2], 0.0))
                pending = []

                def rotated():
                    if not pending:
                        return
                    kind, at = pending.pop(0)
                    r = ROPED.index((kind, at))
                    job = Job("rot", kind, at)
                    Job(kind, at).wait_emptied(dve)
                    own(dve.tensor_tensor(rt[:, r % 2, 0, :], rope_in[:, r, :], cosT, ALU.mult))
                    job.wait_full(dve)
                    dve.tensor_tensor(rt[:, r % 2, 1, :], job.bank[:, 0:SEQ], sinT, ALU.mult).then_inc(job.free, 1)
                    own.settle()
                    job.wait_emptied(dve)
                    dve.tensor_tensor(rope_out[:, r, :], rt[:, r % 2, 0, :], rt[:, r % 2, 1, :], ALU.add)\
                        .then_inc(rope_ready, 1)

                for n, (kind, at) in enumerate(MIX_TILES):
                    if 1 <= n < N_A - HIGHS + 1:
                        low_part(dve, U_A + n + HIGHS - 1)
                    job = Job(kind, at)
                    if kind == "cg":
                        c_, v_ = cu[:, at % 2, :], cacc[:, at % 2, :]
                        w = A("convw")[:, 3 * at:3 * at + 3]
                        Job("u", at).wait_emptied(dve)
                        job.wait_full(dve)
                        dve.tensor_tensor(c_[:, 2:2 + SEQ], job.bank[:, 0:SEQ], usb[:, at % 2, :], ALU.mult)\
                            .then_inc(job.free, 1)
                        job.wait_emptied(dve)
                        own(dve.tensor_scalar(v_, c_[:, 0:SEQ], w[:, 0:1], None, ALU.mult))
                        for t in (1, 2):
                            own.settle()
                            own(dve.scalar_tensor_tensor(v_, c_[:, t:t + SEQ], w[:, t:t + 1], v_, ALU.mult, ALU.add))
                    elif kind == "bg":
                        job.wait_full(dve)
                        own.settle()
                        dve.tensor_tensor(yconvT[:, at, :], job.bank[:, 0:SEQ], cacc[:, at % 2, :], ALU.mult)\
                            .then_inc(job.free, 1)
                    elif kind in ("kc", "vc"):
                        c = 0 if kind == "kc" else 1
                        pos = A("posk" if c == 0 else "posv")
                        job.wait_full(dve)
                        for odd in range(2):
                            rows = slice(odd * HD, (odd + 1) * HD)
                            tokens = job.bank[rows, 0:SEQ].rearrange("p (n j two) -> p two j n", j=8, two=2)[:, odd]
                            for jh in range(2):
                                ins = dve.tensor_tensor(flat[rows, c, 8 * jh:8 * jh + 8, at, :],
                                                        tokens[:, :, jh:jh + NCMP],
                                                        bc(pos[rows, 8 * jh:8 * jh + 8], 2, NCMP), ALU.add)
                                if odd and jh:
                                    ins.then_inc(job.free, 1)
                    rotated()
                    if (kind, at) in ROPED:
                        pending.append((kind, at))
                Job("qm", 3).wait_full(dve)
                dve.tensor_tensor(hmT, memT, bc(A("gmem"), 2, SEQ), ALU.mult).then_inc(hm_ready, 1)
                add = C("cmp_add").rearrange("p (i n) -> p i n", i=NT)
                one = C("cmp_one").rearrange("p (i n) -> p i n", i=NT)
                for g in range(2):
                    job = Job("cmp_S", g)
                    job.wait_full(dve)
                    s4 = job.bank[:, 0:NT * 4 * NCMP].rearrange("p (i h n) -> p i h n", i=NT, h=4)
                    for i in range(NT):
                        ins = dve.tensor_tensor(cs[:, i, 4 * g:4 * g + 4], s4[:, i], bc(add[:, i], 1, 4), ALU.add)
                        if i:
                            ins.then_inc(job.free, 1)
                    job.wait_emptied(dve)
                flat_cs = cs.rearrange("p i h n -> p (i h) n")
                own(dve.tensor_reduce(cstat[:, 0, :], flat_cs, AX.X, ALU.max))
                own.settle()
                dve.tensor_tensor(flat_cs, flat_cs, bc(cstat[:, 0, :], 2, NCMP), ALU.subtract).then_inc(cmp_sub, 1)
                dve.wait_ge(cmp_exp, lay[0] + 1)
                for i in range(NT):
                    own(dve.tensor_tensor(cs[:, i], cs[:, i], bc(one[:, i], 1, NHEAD), ALU.mult))
                own.settle()
                own(dve.tensor_reduce(cstat[:, 1, :], flat_cs, AX.X, ALU.add))
                own.settle()
                own(dve.tensor_scalar(cstat[:, 1, :], cstat[:, 1, :], 1e-30, None, ALU.max))
                own.settle()
                own(dve.reciprocal(cstat[:, 2, :], cstat[:, 1, :]))
                own.settle()
                g0 = gate.rearrange("p i (h b) -> p i h b", b=3)[:, :, :, 0]
                c3 = cstat[:, 3, :].rearrange("p (i h) -> p i h", i=NT)
                own(dve.tensor_tensor(c3, cstat[:, 2, :].rearrange("p (i h) -> p i h", i=NT), g0, ALU.mult))
                own.settle()
                for i in range(NT):
                    ins = dve.tensor_tensor(Pc[:, i, :, 0:NCMP], cs[:, i], bc(c3[:, i], 2, NCMP), ALU.mult)
                    if i:
                        ins.then_inc(cmp_p, 1)
                    else:
                        own(ins)

                def evacuate(unit, job, rows):
                    kind, a, g = unit
                    y = ymemT if kind == "mem" else ynsaT
                    dve.tensor_copy(y[rows, a, :], job.bank[rows, 0:SEQ]).then_inc(job.free, 1)

                attention("mix", MIX_UNITS, evacuate)
                for m in range(KD):
                    for b in range(3):
                        job = Job("branch", m, b)
                        job.wait_full(dve)
                        Job("gate", m, b).wait_emptied(dve)
                        dst = mergedT[:, m, :] if b == 0 else mt[:, b - 1, :]
                        dve.tensor_tensor(dst, job.bank[:, 0:SEQ], sg[:, 3 * m + b, :], ALU.mult).then_inc(job.free, 1)
                        job.wait_emptied(dve)
                        if b:
                            ins = dve.tensor_tensor(mergedT[:, m, :], mergedT[:, m, :], mt[:, b - 1, :], ALU.add)
                            if b == 2:
                                ins.then_inc(merged, 1)
                            else:
                                own(ins)
                                own.settle()
                split(U_FFN2, 0, AHEAD)
                post("mixed", p, 1, lay[0] + 1, 1.0)

            dve.memset(eps, EPS).then_inc(x_ready, 1)
            dve.wait_ge(x_here, 16)
            dve.memset(small[:, 1:2], 0.0).then_inc(x_ready, 1)
            for b in range(8):
                dve.memset(small[:, 56 + b:57 + b], 0.0).then_inc(free[b], 1)
            own(dve.memset(hv.rearrange("p m g j n -> p (m g j n)"), 0.0))
            own(dve.memset(Pc.rearrange("p i h n -> p (i h n)"), 0.0))
            dve.wait_ge(pos_here, 16)
            dve.wait_ge(const_in, 16)
            dve.wait_ge(small_in, 32)
            ang, turns_ = rope_in[:, 0, :], rope_in[:, 1, :]
            own(dve.tensor_copy(ang, rope_out[:, 0, :].bitcast(I32)))
            own.settle()
            own(dve.tensor_scalar(ang, ang, C("inv"), None, ALU.mult))
            own.settle()
            own(dve.tensor_scalar(turns_, ang, 1 / (2 * np.pi), MAGIC, ALU.mult, ALU.add))
            own.settle()
            own(dve.tensor_scalar(turns_, turns_, MAGIC, None, ALU.subtract))
            for part in TWO_PI:
                own.settle()
                own(dve.scalar_tensor_tensor(ang, turns_, -part, ang, ALU.mult, ALU.add))
            own.settle()
            own(dve.tensor_scalar(sinT, ang, PI_BELOW, -PI_BELOW, ALU.min, ALU.max))
            own(dve.tensor_scalar(ang, ang, np.pi / 2, None, ALU.add))
            own.settle()
            own(dve.tensor_scalar(turns_, ang, np.pi, -2 * np.pi, ALU.is_gt, ALU.mult))
            own.settle()
            own(dve.tensor_tensor(ang, ang, turns_, ALU.add))
            own.settle()
            dve.tensor_scalar(cosT, ang, PI_BELOW, -PI_BELOW, ALU.min, ALU.max).then_inc(trig_in, 1)
            norm("mem", 0, None, memT, xs)
            dve.wait_ge(trig_done, 1)
            split(U_FFN1, 0, AHEAD)
            n_par = par_at["w2v"][1]

            def body():
                own.settle()
                own(dve.tensor_copy(pl[:, :], pars[:, bass.ds(lay[0] * n_par, n_par)]))
                own.settle()
                ffn(0, 1 + 3 * lay[0], A("g1"))
                post(("ffn_out", 0), 3 * lay[0], 0, 2 * lay[0] + 1, 0.5)
                mixer(2 + 3 * lay[0], 3 * lay[0] + 1)
                ffn(1, 3 + 3 * lay[0], A("g2"))
                post(("ffn_out", 1), 3 * lay[0] + 2, 0, 2 * lay[0] + 2, 0.5)

            layers(dve, body, own)

            norm("even", 7, A2("ge"))
            norm_parts("even", 6, hH2)
            dve.memset(xp[:, :, 0:3], 0.0).then_inc(conv_done, 1)
            for t in range(16):
                w = A2("cw")[:, 4 * t:4 * t + 4]
                c_, v_ = xp[:, t % 2, :], cv[:, t % 2, :]
                Job("xbc", t).wait_emptied(dve)
                if t >= 2:
                    dve.wait_ge(conv_act, t - 1)
                own(dve.tensor_scalar(v_, c_[:, 0:SEQ], w[:, 0:1], None, ALU.mult))
                for j in (1, 2, 3):
                    own.settle()
                    ins = dve.scalar_tensor_tensor(v_, c_[:, j:j + SEQ], w[:, j:j + 1], v_, ALU.mult, ALU.add)
                    if j == 3:
                        ins.then_inc(conv_done, 1)
                    else:
                        own(ins)

            def heads_normed(n, heads, copied, gains, pieces):
                width = heads * HD
                view = [[QK[:, qk, i, 0:width].rearrange("p (h d) -> p h d", h=heads) for i in range(NT)]
                        for qk in range(2)]
                sq = Sflat[:, 0:width]
                sums = stat[:, 0, 0:4 * heads]
                for qk in range(2):
                    for i in range(NT):
                        copied(qk, i)
                        own.settle()
                        own(dve.tensor_tensor(sq, QK[:, qk, i, 0:width], QK[:, qk, i, 0:width], ALU.mult))
                        own.settle()
                        at = (2 * qk + i) * heads
                        own(dve.tensor_reduce(sums[:, at:at + heads], sq.rearrange("p (h d) -> p h d", h=heads),
                                              AX.X, ALU.add))
                own.settle()
                v, root, r = (stat[:, j, 0:4 * heads] for j in (1, 2, 3))
                dve.tensor_scalar(v, sums, 1.0 / HD, EPS, ALU.mult, ALU.add).then_inc(qk_var, 1)
                dve.wait_ge(qk_std, n)
                own(dve.reciprocal(r, root))
                own.settle()
                own(dve.tensor_tensor(sums, r, r, ALU.mult))
                own.settle()
                own(dve.tensor_tensor(sums, sums, v, ALU.mult))
                own.settle()
                own(dve.tensor_scalar(sums, sums, -0.5, 1.5, ALU.mult, ALU.add))
                own.settle()
                own(dve.tensor_tensor(r, r, sums, ALU.mult))
                own.settle()
                cos2 = C("cos2").rearrange("p (i d) -> p i d", i=NT)
                sin2 = C("sin2").rearrange("p (i d) -> p i d", i=NT)
                t_ = Sflat[:, 0:4 * heads * ROT].rearrange("p (k h d) -> p k h d", k=4, h=heads)
                for qk in range(2):
                    for i in range(NT):
                        w = view[qk][i]
                        at = (2 * qk + i) * heads
                        own(dve.tensor_tensor(w, w, bc(r[:, at:at + heads], 2, HD), ALU.mult))
                        own.settle()
                        own(dve.tensor_tensor(w, w, bc(gains[qk], 1, heads), ALU.mult))
                        own.settle()
                        a, b = w[:, :, 0:ROT], w[:, :, ROT:2 * ROT]
                        c, s = bc(cos2[:, i], 1, heads), bc(sin2[:, i], 1, heads)
                        for j, (u, z) in enumerate(((a, c), (b, s), (b, c), (a, s))):
                            own(dve.tensor_tensor(t_[:, j], u, z, ALU.mult))
                        own.settle()
                        own(dve.tensor_tensor(a, t_[:, 0], t_[:, 1], ALU.subtract))
                        dve.tensor_tensor(b, t_[:, 2], t_[:, 3], ALU.add).then_inc(qk_ready, 1)
                        dve.wait_ge(qk_ready, 4 * (n - 1) + 2 * qk + i + 1)

            def even_copied(qk, i):
                for c in range(3):
                    Job("eb", 3 * qk + c, i).wait_emptied(dve)

            heads_normed(1, DIL_H, even_copied, (A2("qn_dil"), A2("kn_dil")), 3)
            dt3 = dts[:, :, :].rearrange("p k (i h) -> p k i h", i=NT)
            for i in range(NT):
                Job("dt", i).wait_emptied(dve)
            own(dve.tensor_tensor(dt3[:, 0], dt3[:, 0], bc(A2("dtb"), 1, NT), ALU.add))
            own.settle()
            own(dve.tensor_scalar(dts[:, 1, :], dts[:, 0, :], 0.0, None, ALU.max))
            own(dve.tensor_scalar(dts[:, 3, :], dts[:, 0, :], -1.0, None, ALU.mult))
            own.settle()
            dve.tensor_tensor(dts[:, 2, :], dts[:, 0, :], dts[:, 3, :], ALU.max).then_inc(dt_abs, 1)
            dve.wait_ge(dt_exp, 1)
            own(dve.tensor_scalar(dts[:, 3, :], dts[:, 2, :], 2.0, None, ALU.add))
            own.settle()
            own(dve.reciprocal(dts[:, 4, :], dts[:, 3, :]))
            own.settle()
            own(dve.tensor_tensor(dts[:, 3, :], dts[:, 2, :], dts[:, 4, :], ALU.mult))
            own.settle()
            own(dve.tensor_tensor(dts[:, 4, :], dts[:, 3, :], dts[:, 3, :], ALU.mult))
            own.settle()
            own(dve.tensor_scalar(dts[:, 5, :], dts[:, 4, :], 1.0 / 17, None, ALU.mult))
            for odd in (15, 13, 11, 9, 7, 5, 3):
                own.settle()
                own(dve.scalar_tensor_tensor(dts[:, 5, :], dts[:, 5, :], 1.0 / odd, dts[:, 4, :], ALU.add, ALU.mult))
            own.settle()
            own(dve.scalar_tensor_tensor(dts[:, 5, :], dts[:, 5, :], 1.0, dts[:, 3, :], ALU.add, ALU.mult))
            own.settle()
            own(dve.scalar_tensor_tensor(dts[:, 6, :], dts[:, 5, :], 2.0, dts[:, 1, :], ALU.mult, ALU.add))
            own(dve.tensor_scalar(neg_a, neg_a, -1.0, None, ALU.mult))
            own.settle()
            dve.tensor_tensor(dt3[:, 7], dt3[:, 6], bc(neg_a, 1, NT), ALU.mult).then_inc(a_ready, 1)
            all_emptied(dve, [("xs", n) for n in range(4)])
            for i in range(NT):
                ins = dve.tensor_tensor(xs[:, i, :].rearrange("p (h d) -> p h d", h=SSD_H),
                                        xtok[:, i, :].rearrange("p (h d) -> p h d", h=SSD_H),
                                        bc(dt3[:, 6, i], 2, HD), ALU.mult)
                if i:
                    ins.then_inc(xdt_ready, 1)
            for g in range(4):
                job = Job("cb", g)
                job.wait_full(dve)
                dve.tensor_tensor(cbm[:, g, :], job.bank[:, 0:384], C("reach"), ALU.mult).then_inc(job.free, 1)
            Job("acs").wait_emptied(dve)
            acs = dts[:, 2, :]
            for n in range(9):
                if n < 8:
                    job = Job("decay", n)
                    job.wait_full(dve)
                    for hh in range(2):
                        h = 2 * n + hh
                        for i in range(NT):
                            e = ebuf[:, n % 2, hh, 0:SEQ] if i == 0 else ebuf[:, n % 2, hh, SEQ:384]
                            ins = dve.tensor_scalar(e, job.bank[:, hh * SEQ + i * P:(hh + 1) * SEQ],
                                                    acs[:, i * SSD_H + h:i * SSD_H + h + 1], 0.0,
                                                    ALU.subtract, ALU.min)
                            if hh and i:
                                ins.then_inc(job.free, 1)
                            else:
                                own(ins)
                    job.wait_emptied(dve)
                    dve.memset(small[:, 1:2], 0.0).then_inc(decay_in, 1)
                if n >= 1:
                    dve.wait_ge(decay_exp, n)
                    e = ebuf[:, (n - 1) % 2]
                    dve.tensor_tensor(e, e, bc(cbm[:, (n - 1) // 2, :], 1, 2), ALU.mult).then_inc(decay_done, 1)

            def even_out(unit, job, rows):
                _, h, _ = unit
                dve.tensor_tensor(mixedT[rows, 8 + h // 2, :], job.bank[rows, 0:SEQ], egT[rows, h // 2, :],
                                  ALU.mult).then_inc(job.free, 1)

            for i in range(NT):
                own(dve.tensor_tensor(yt[:, i, :].rearrange("p (h d) -> p h d", h=SSD_H),
                                      xtok[:, i, :].rearrange("p (h d) -> p h d", h=SSD_H),
                                      bc(A2("dskip"), 2, HD), ALU.mult))
            own.settle()
            for i in range(NT):
                for half in range(2):
                    job = Job("scan", 2 * i + half)
                    cols = slice(half * 512, (half + 1) * 512)
                    job.wait_full(dve)
                    dve.tensor_tensor(ysb[:, i, cols], job.bank, yt[:, i, cols], ALU.add).then_inc(job.free, 1)
                    job.wait_emptied(dve)
            attention("dil", EVEN_UNITS, even_out)
            own(dve.tensor_tensor(ysb, ysb, Z[:, :, :], ALU.mult))
            own.settle()
            own(dve.tensor_tensor(yt, ysb, ysb, ALU.mult))
            own.settle()
            dve.tensor_reduce(stat[:, 0, 0:8], yt.rearrange("p i (g d) -> p (i g) d", g=4), AX.X, ALU.add)\
                .then_inc(y_sq, 1)
            dve.wait_ge(y_std, 1)
            own(dve.reciprocal(stat[:, 2, 0:8], stat[:, 1, 0:8]))
            own.settle()
            y8 = ysb.rearrange("p i (g d) -> p (i g) d", g=4)
            dve.tensor_tensor(y8, y8, bc(stat[:, 2, 0:8], 2, 256), ALU.mult).then_inc(y_ready, 1)
            for n in range(4):
                i, half = n // 2, n % 2
                job = Job("yT", n)
                job.wait_full(dve)
                dve.tensor_tensor(mixedT[:, 4 * half:4 * half + 4, i * P:(i + 1) * P],
                                  job.bank.rearrange("p (k t) -> p k t", k=4),
                                  bc(A2("gssd")[:, 4 * half:4 * half + 4], 2, P), ALU.mult).then_inc(job.free, 1)

            def residual(name):
                for j in range(4):
                    job = Job(name, j)
                    job.wait_full(dve)
                    to = x[:, j // 2, j % 2 * 512:(j % 2 + 1) * 512]
                    dve.tensor_tensor(to, to, job.bank, ALU.add).then_inc(job.free, 1)

            residual("even_out")

            for j in range(4):
                Job("even_out", j).wait_emptied(dve)
            norm("odd", 8, A2("go"))
            norm_parts("odd", 7, hH2)

            def odd_copied(qk, i):
                for c in range(2):
                    Job("ob", 2 * qk + c, i).wait_emptied(dve)

            heads_normed(2, MOBA_H, odd_copied, (A2("qn_moba"), A2("kn_moba")), 2)

            def odd_out(unit, job, rows):
                _, h, _ = unit
                dve.tensor_tensor(mixedT[rows, h // 2, :], job.bank[rows, 0:SEQ], ogT[rows, h // 2, :],
                                  ALU.mult).then_inc(job.free, 1)

            attention("moba", ODD_UNITS, odd_out)
            residual("odd_out")


def constants():
    token = np.arange(SEQ)
    t, s = token[:, None], token[None, :]

    def blocks(ok):
        return np.concatenate([ok[:P, :P], ok[P:, :]], 1)

    def added(ok):
        return np.where(blocks(ok), 0.0, NEG)

    causal = s <= t
    c = {
        "ident": np.eye(P), "causal": added(causal), "dil0": added(causal & (t - s <= 128)),
        "dil1": added(causal & ((t - s) % 4 == 0)), "dil2": added(causal & ((t - s) % 16 == 0)),
    }
    reach = causal.T.astype(float)
    c["reach"] = np.concatenate([reach[:P, :], reach[P:, P:]], 1)
    ends = np.arange(NCMP) * 16 + 31
    seen = (ends[None, None, :] <= token.reshape(NT, P, 1)).transpose(1, 0, 2).reshape(P, -1)
    c["cmp_add"], c["cmp_one"] = np.where(seen, 0.0, NEG), seen
    c["upto"], c["ones"] = reach[:P, :P], np.ones((P, P))
    rotate = np.zeros((P, P))
    inv = np.zeros((P, 1))
    freq = THETA ** (-np.arange(ROT) * 2.0 / (2 * ROT))
    for base in (0, HD):
        for d in range(ROT):
            rotate[base + d + ROT, base + d] = -1.0
            rotate[base + d, base + d + ROT] = 1.0
            inv[base + d] = inv[base + d + ROT] = freq[d]
    c["rotate"], c["inv"] = rotate, inv
    angle = (token[:, None].astype(np.float32) * freq.astype(np.float32)).astype(np.float64)
    for name, f in (("cos2", np.cos), ("sin2", np.sin)):
        c[name] = f(angle).reshape(NT, P, ROT).transpose(1, 0, 2).reshape(P, -1)
    assert all(c[k].shape == (P, CONST[k]) for k in CONST)
    return np.concatenate([c[k] for k in CONST], 1).astype(np.float32)


def by_partition(v):
    return v.reshape(-1, P).T


def mtile(w, a, n=P):
    k = w.shape[0] // P
    return w[:, a:a + n].reshape(k, P, n).transpose(1, 0, 2).reshape(P, k * n)


def packed(rows):
    out = np.zeros((len(rows), P, CHUNK), np.float32)
    for c, pieces in enumerate(rows):
        at = 0
        for piece in pieces:
            out[c, :, at:at + piece.shape[1]] = piece
            at += piece.shape[1]
    return out


def groups(pieces, n):
    return [pieces[i:i + n] for i in range(0, len(pieces), n)]


def layer_chunks(v, l):
    def ffn(w_in, w_out):
        a, b = ([mtile(w_in, z + t * P) for t in range(FT)] for z in (0, FF))
        o = [w_out[t * P:(t + 1) * P] for t in range(FT)]
        tiles = [a[0], b[0], a[1], b[1], o[0]]
        for t in range(2, FT):
            tiles += [a[t], b[t], o[t - 1]]
        return groups(tiles + [o[-1]], 3)

    w = v["w_mix_in"][l]
    q0, kv0 = 3 * CONV, 3 * CONV + 512
    g0 = kv0 + 768
    qm0, mg0 = g0 + 24, g0 + 24 + 512

    def pick(columns):
        return mtile(w[:, columns], 0)

    def head_pair(a):
        return pick(np.r_[q0 + a * HD:q0 + (a + 1) * HD, q0 + (4 + a) * HD:q0 + (5 + a) * HD])

    def twice(c, g):
        at = kv0 + c * P + g * HD
        return pick(np.r_[at:at + HD, at:at + HD])

    tiles = [mtile(w, o * CONV + f * P) for f in range(CF) for o in (0, 2, 1)]
    tiles += [head_pair(a) for a in range(4)] + [mtile(w, kv0 + 2 * P), mtile(w, kv0 + 4 * P)]
    tiles += [twice(c, g) for c in range(2) for g in range(2)] + [mtile(w, qm0 + h * P) for h in range(4)]
    rows = groups(tiles, 3)
    columns_b = np.r_[kv0 + 3 * P:kv0 + 4 * P, kv0 + 5 * P:kv0 + 6 * P, g0:g0 + 24]
    rows += [[mtile(w[:, columns_b], 0, 280)]]
    m = v["w_mem_kv"][l]
    mk = [mtile(m, h * P) for h in range(4)]
    mv = mtile(m, 512, 512)
    rows += [mk[:3], [mk[3], mv[:, :2048]], [mv[:, 2048:]]]
    for name in ("cmp_k_w1", "cmp_v_w1"):
        t = mtile(v[name][l], 0, 256)
        rows += [[t[:, :2048]], [t[:, 2048:]]]
    rows += [[mtile(w, mg0 + b * D + t * P) for b in range(3)] for t in range(KD)]
    nsa = v["w_branch_nsa"][l].reshape(2, 4, HD, D).transpose(1, 0, 2, 3).reshape(512, D)
    branch = (v["w_branch_conv"][l], nsa, v["w_branch_mem"][l])
    rows += [[mtile(w_, t * P) for t in pair for w_ in branch] for pair in groups(list(range(KD)), 2)]
    rows += groups([v["w_mix_out"][l][k * P:(k + 1) * P] for k in range(KD)], 3)
    rows = ffn(v["ffn1_w_in"][l], v["ffn1_w_out"][l]) + rows + ffn(v["ffn2_w_in"][l], v["ffn2_w_out"][l])
    assert len(rows) == LAYER_CHUNKS
    return packed(rows)


def tail_chunks(v):
    w, o = v["even_w_in_2"][0], v["odd_w_in_2"][0]
    xbc0, dt0, q0 = D, 3 * D, 3 * D + SSD_H
    k0, v0, g0 = q0 + 1536, q0 + 3072, q0 + 4608
    rows = groups([mtile(w, xbc0 + t * P) for t in range(16)] + [mtile(w, g0 + t * P) for t in range(4)], 3)

    def blocks(w_, starts):
        return [w_[k * P:(k + 1) * P, a:a + 512] for a in starts for k in range(KD)]

    starts = [b + c * 512 for b in (q0, k0, v0) for c in range(3)] + [0, 512]
    last = groups(blocks(w, starts), 6)
    last[-1] = last[-1] + [mtile(w, dt0, SSD_H)]
    rows += last
    rows += groups([v["even_w_out_2"][0][k * P:(k + 1) * P] for k in range(12)], 3)
    rows += groups(blocks(o, [c * 512 for c in range(6)]), 6)
    rows += groups([mtile(o, 3 * D + t * P) for t in range(8)], 3)
    rows += groups([v["odd_w_out_2"][0][k * P:(k + 1) * P] for k in range(8)], 3)
    assert len(rows) == CHUNKS - DEPTH * LAYER_CHUNKS
    return packed(rows)


def layer_parameters(v, l):
    def positions(p):
        return p.reshape(16, 2, HD).transpose(1, 2, 0).reshape(P, 16)

    p = {
        "g1": by_partition(v["ffn1_norm_pre"][l]), "gm": by_partition(v["mix_norm_pre"][l]),
        "g2": by_partition(v["ffn2_norm_pre"][l]), "gmem": by_partition(v["mem_norm"][l]),
        "convw": v["conv_w"][l].reshape(3, CF, P).transpose(2, 1, 0).reshape(P, -1),
        "posk": positions(v["cmp_pos_k"][l]), "posv": positions(v["cmp_pos_v"][l]),
        "b1k": by_partition(v["cmp_k_b1"][l]), "b1v": by_partition(v["cmp_v_b1"][l]),
        "w2k": mtile(v["cmp_k_w2"][l], 0, HD), "w2v": mtile(v["cmp_v_w2"][l], 0, HD),
    }
    assert all(p[k].shape == (P, PARAM[k]) for k in PARAM)
    return np.concatenate([p[k] for k in PARAM], 1)


def tail_parameters(v):
    def everywhere(a):
        return np.broadcast_to(a, (P, a.size))

    p = {
        "ge": by_partition(v["even_norm_w_2"][0]), "go": by_partition(v["odd_norm_w_2"][0]),
        "gssd": by_partition(v["even_ssd_norm_w_2"][0]),
        "cw": v["even_conv_w_2"][0].reshape(16, P, 4).transpose(1, 0, 2).reshape(P, 64),
        "cb": by_partition(v["even_conv_b_2"][0]),
        "dtb": everywhere(v["even_dt_bias_2"][0]), "alog": everywhere(v["even_a_log_2"][0]),
        "dskip": everywhere(v["even_d_skip_2"][0]), "qn_dil": everywhere(v["even_q_norm_2"][0]),
        "kn_dil": everywhere(v["even_k_norm_2"][0]), "qn_moba": everywhere(v["odd_q_norm_2"][0]),
        "kn_moba": everywhere(v["odd_k_norm_2"][0]),
    }
    assert all(p[k].shape == (P, PARAM2[k]) for k in PARAM2)
    return np.concatenate([p[k] for k in PARAM2], 1)


def kernel(**inputs):
    import concourse.bacc as bacc
    from concourse.bass_utils import run_bass_kernel_spmd

    v = {k: np.asarray(a) for k, a in inputs.items()}

    def tiles(a):
        return np.ascontiguousarray(a[0].reshape(NT, P, D).transpose(1, 0, 2))

    arrays = {
        "weights": np.concatenate([layer_chunks(v, l) for l in range(DEPTH)] + [tail_chunks(v)]),
        "par": np.concatenate([layer_parameters(v, l) for l in range(DEPTH)], 1),
        "par2": tail_parameters(v),
        "const": constants(),
        "posts": np.stack([v[n][l] for l in range(DEPTH) for n in ("ffn1_norm_post", "mix_norm_post", "ffn2_norm_post")]),
        "x": tiles(v["x"]), "mem": tiles(v["mem"]), "positions": v["positions"],
    }
    arrays = {k: np.ascontiguousarray(a) for k, a in arrays.items()}
    nc = bacc.Bacc("TRN2", target_bir_lowering=False, num_devices=1)
    ins = {
        k: nc.dram_tensor(f"in_{k}", a.shape, mybir.dt.from_np(a.dtype), kind="ExternalInput").ap()
        for k, a in arrays.items()
    }
    out = nc.dram_tensor("out", (P, NT, D), F32, kind="ExternalOutput").ap()
    build(nc, ins["weights"], ins["par"], ins["par2"], ins["const"], ins["posts"], ins["x"], ins["mem"],
          ins["positions"], out)
    r = run_bass_kernel_spmd(nc, [{f"in_{k}": a for k, a in arrays.items()}], core_ids=[0])
    got = np.asarray(r.results[0]["out"])
    return np.ascontiguousarray(got.transpose(1, 0, 2).reshape(1, SEQ, D))
```

```python
from contextlib import ExitStack

import concourse.bass as bass
import numpy as np
from concourse import mybir

F32 = mybir.dt.float32
F32R = mybir.dt.float32r
I32 = mybir.dt.int32
ALU = mybir.AluOpType
ACT = mybir.ActivationFunctionType
AX = mybir.AxisListType

P = 128
SEQ, NT = 256, 2
D, KD = 1024, 8
DEPTH = 2
FF = 2816
FT = FF // P
CONV, CF = 512, 4
HD = 64
NHEAD = 8
NCMP = SEQ // 16 - 1
ROT = 8
THETA = 500000.0
MAGIC = 1.5 * 2.0**23
SSD_H, DIL_H, MOBA_H = 16, 24, 16
EPS = 1e-6
NEG = -1e30
SCALE = HD**-0.5
SCALE_MEM = 128**-0.5

CHUNK, SLOTS = 3072, 4
ACT_OWN, DVE_OWN = 21, 104
TWO_PI = (6.28125, 0.0019350051879882812, 3.0199159795e-07)
PI_BELOW = 3.1415925
MTILE = KD * P

FFN_CHUNKS, A_CHUNKS, B_CHUNKS, C_CHUNKS, D_CHUNKS = FT, 9, 1, 3, 4
GATE_CHUNKS, BRANCH_CHUNKS, OUT_CHUNKS = 8, 4, 3
AT_FFN1 = 0
AT_C = FFN_CHUNKS
AT_A = AT_C + C_CHUNKS
AT_B = AT_A + A_CHUNKS
AT_D = AT_B + B_CHUNKS
AT_GATE = AT_D + D_CHUNKS
AT_BRANCH = AT_GATE + GATE_CHUNKS
AT_OUT = AT_BRANCH + BRANCH_CHUNKS
AT_FFN2 = AT_OUT + OUT_CHUNKS
LAYER_CHUNKS = AT_FFN2 + FFN_CHUNKS
EVEN_A, EVEN_B, EVEN_OUT = 7, 15, 4
ODD_B, ODD_A, ODD_OUT = 8, 3, 3
AT_EA = DEPTH * LAYER_CHUNKS
AT_EB = AT_EA + EVEN_A
AT_EO = AT_EB + EVEN_B
AT_OB = AT_EO + EVEN_OUT
AT_OA = AT_OB + ODD_B
AT_OO = AT_OA + ODD_A
CHUNKS = AT_OO + ODD_OUT
LAST_SLOT = (LAYER_CHUNKS - 1) % SLOTS
assert LAYER_CHUNKS % SLOTS == 0 and CHUNKS % SLOTS == 0

UNIT, HIGHS = CHUNK // 3, 6
AHEAD = 3
U_FFN1, U_A, U_B, U_GATE = (3 * at for at in (AT_FFN1, AT_A, AT_B, AT_GATE))
U_BRANCH, U_FFN2 = 3 * AT_BRANCH, 3 * AT_FFN2
U_EA, U_EB, U_OB, U_OA = (3 * at for at in (AT_EA, AT_EB, AT_OB, AT_OA))
N_BRANCH = 12
N_FFN, N_A, N_B, N_GATE, N_EA, N_EB, N_OB, N_OA = 3 * FT, 26, 3, 24, 20, 45, 24, 8
AB_UNITS = [*range(U_A, U_A + N_A), *range(U_B, U_B + N_B)]
GATE_UNITS = [*range(U_GATE, U_GATE + N_GATE)]
BRANCH_UNITS = [*range(U_BRANCH, U_BRANCH + N_BRANCH)]
LAYER_SPLIT = [*range(U_FFN1, U_FFN1 + N_FFN), *AB_UNITS, *GATE_UNITS, *BRANCH_UNITS, *range(U_FFN2, U_FFN2 + N_FFN)]
TAIL_SPLIT = [*range(U_EA, U_EA + N_EA), *range(U_EB, U_EB + N_EB), *range(U_OB, U_OB + N_OB),
              *range(U_OA, U_OA + N_OA)]
assert 3 * LAYER_CHUNKS % HIGHS == 0 and U_B % HIGHS == 0
PLACES = 4


def place(u):
    for kind, first, n in (("gate", U_GATE, N_GATE), ("branch", U_BRANCH, N_BRANCH)):
        if first <= u < first + n:
            return kind, (u - first) % PLACES
    return "ring", u % HIGHS


def occupants(units, before):
    last = {place(u): n for n, u in zip(range(-HIGHS, 0), before)}
    free_at = []
    for n, u in enumerate(units):
        if place(u) not in last:
            last[place(u)] = units.index(u - place(u)[1]) - 1
        free_at.append(last[place(u)] + 1)
        last[place(u)] = n
    return free_at


LAYER_ROOM = occupants(LAYER_SPLIT, LAYER_SPLIT[-HIGHS:])
TAIL_ROOM = occupants(TAIL_SPLIT, LAYER_SPLIT[-HIGHS:])


BANKS = {"G": 2, "T": 2, "Y": 4}
MIX_TILES = (
    [n for f in range(CF) for n in (("u", f), ("cg", f), ("bg", f))]
    + [("q", a) for a in range(4)] + [("kslc", 0), ("kwin", 0)]
    + [("kc", 0), ("kc", 1), ("vc", 0), ("vc", 1)] + [("qm", h) for h in range(4)]
)
ROPED = [("q", a) for a in range(4)] + [("kslc", 0), ("kwin", 0)]
MIX_UNITS = [("mem", h, 0) for h in range(4)] + [("nsa", u // 2, u % 2) for u in range(8)]
EVEN_UNITS = [("dil", h, 0) for h in range(8)]
ODD_UNITS = [("moba", h, 0) for h in range(MOBA_H)]
Y_STEPS = (7, 8, 10, 12)
LAG = {"mix": 2, "dil": 2, "moba": 2}
SCORE_BUFFERS = 3
BRANCHES = {"nsa": 2, "mem": 1, "dil": 3, "moba": 1}


def gates_at(s):
    return range(2 * s, 2 * s + 2) if s < len(MIX_UNITS) else ()


class Jobs:

    def __init__(self):
        self.count = dict.fromkeys(BANKS, 0)
        self.number = {}

    def add(self, ring, *name):
        self.number[name] = (ring, self.count[ring])
        self.count[ring] += 1

    def norm(self, name):
        for i in range(NT):
            for half in range(2):
                self.add("T", "norm", name, i, half)

    def four(self, name):
        for j in range(4):
            self.add("Y", name, j)

    def attention(self, tag, units):
        lag = LAG[tag]
        for s in range(len(units) + lag + 1):
            if s < len(units):
                for b in range(BRANCHES[units[s][0]]):
                    self.add("G", "S", tag, s, b)
            if tag == "mix":
                for n in gates_at(s):
                    self.add("G", "gate", *divmod(n, 3))
            if 0 <= s - lag < len(units):
                for b in range(BRANCHES[units[s - lag][0]]):
                    self.add("T", "PT", tag, s - lag, b)
            if s > lag:
                self.add("Y", "PV", tag, s - lag - 1)

    def ffn(self, f):
        self.norm(("ffn", f))
        for t in range(FT):
            self.add("G", "ff", f, t)
        self.four(("ffn_out", f))


def layer_jobs():
    j = Jobs()
    j.ffn(0)
    for h in range(4):
        j.add("G", "mk", h)
    j.norm("mix")
    for i in range(NT):
        j.add("Y", "mv", i)
    for kind, at in MIX_TILES:
        j.add("G", kind, at)
    for kind, at in ROPED:
        j.add("T", "rot", kind, at)
    for i in range(NT):
        j.add("Y", "tok", i)
    for c in range(2):
        for m in range(2):
            j.add("G", "hid", c, m)
    for name in (("cmp_kv",), ("cmp_S", 0), ("cmp_S", 1), ("cmp_PT",)):
        j.add("T", *name)
    j.attention("mix", MIX_UNITS)
    for m in range(KD):
        for b in range(3):
            j.add("G", "branch", m, b)
    j.four("mixed")
    j.ffn(1)
    assert all(j.count[r] % BANKS[r] == 0 for r in BANKS), j.count
    return j


def tail_jobs():
    j = Jobs()
    j.norm("even")
    for t in range(16):
        j.add("G", "xbc", t)
    for t in range(4):
        j.add("G", "eg", t)
    for n in range(4):
        j.add("T", "xs", n)
    for c in range(11):
        for i in range(NT):
            j.add("Y", "eb", c, i)
    for i in range(NT):
        j.add("Y", "dt", i)
    for n in range(12):
        j.add("T", "qkT", "dil", n)
    for g in range(4):
        j.add("G", "cb", g)
    for name in ("acs", "acsT"):
        j.add("T", name)
    j.four("scan")
    for n in range(8):
        j.add("G", "decay", n)
    j.attention("dil", EVEN_UNITS)
    for n in range(4):
        j.add("T", "yT", n)
    j.four("even_out")
    j.norm("odd")
    for c in range(6):
        for i in range(NT):
            j.add("Y", "ob", c, i)
    for t in range(8):
        j.add("G", "og", t)
    for n in range(8):
        j.add("T", "qkT", "moba", n)
    j.attention("moba", ODD_UNITS)
    j.four("odd_out")
    return j


FRONT = Jobs()
FRONT.norm("mem")
LAYER, TAIL = layer_jobs(), tail_jobs()

CONST = {
    "ident": P, "inv": 1, "causal": 384, "dil0": 384, "dil1": 384, "dil2": 384, "reach": 384,
    "cmp_add": 2 * NCMP, "cmp_one": 2 * NCMP, "upto": P, "ones": P, "rotate": P,
    "cos2": 2 * ROT, "sin2": 2 * ROT,
}
PARAM = {
    "g1": KD, "gm": KD, "g2": KD, "gmem": KD, "convw": CF * 3, "posk": 16, "posv": 16,
    "b1k": 2, "b1v": 2, "w2k": 2 * HD, "w2v": 2 * HD,
}
PARAM2 = {
    "ge": KD, "go": KD, "gssd": KD, "cw": 64, "cb": 16, "dtb": SSD_H, "alog": SSD_H, "dskip": SSD_H,
    "qn_dil": HD, "kn_dil": HD, "qn_moba": HD, "kn_moba": HD,
}


def columns(table):
    at, found = 0, {}
    for name, n in table.items():
        found[name] = (at, at + n)
        at += n
    return found, at


def build(nc, weights, par, par2, const, posts, x_in, mem_in, pos_in, out):
    ctx = ExitStack()
    with ctx:
        def sb(name, shape, dt=F32):
            return ctx.enter_context(nc.sbuf_tensor(name, shape, dt))

        def sem(name):
            return ctx.enter_context(nc.semaphore(name))

        def bc(ap, axis, n):
            shape = list(ap.shape)
            shape.insert(axis, n)
            return ap.unsqueeze(axis).broadcast_to(shape)

        psum = ctx.enter_context(nc.psum_tensor("psum", [P, 8, 512], F32))
        FIRST_BANK = {"G": 0, "T": 2, "Y": 4}
        full = [sem(f"full{b}") for b in range(8)]
        free = [sem(f"free{b}") for b in range(8)]

        lay = [0]

        class Job:

            def __init__(self, *name, plus=0):
                part = FRONT if name in FRONT.number else LAYER if name in LAYER.number else TAIL
                ring, n = part.number[name]
                self.at = FIRST_BANK[ring] + n % BANKS[ring]
                self.bank = psum[:, self.at, :]
                before = 0
                if part is not FRONT:
                    before = lay[0] * (LAYER.count[ring] // BANKS[ring]) + FRONT.count[ring] // BANKS[ring]
                self.round = before + (n // BANKS[ring]) + plus
                self.full, self.free = full[self.at], free[self.at]

            def wait_empty(self, eng):
                eng.wait_ge(self.free, self.round + 1)

            def wait_full(self, eng):
                eng.wait_ge(self.full, self.round + 1)

            def wait_emptied(self, eng):
                eng.wait_ge(self.free, self.round + 2)

        def all_emptied(eng, names):
            for job in {job.at: job for job in (Job(*name) for name in names)}.values():
                job.wait_emptied(eng)

        class Split:

            def __init__(self, u, it=0):
                tail = u >= U_EA
                table, room = (TAIL_SPLIT, TAIL_ROOM) if tail else (LAYER_SPLIT, LAYER_ROOM)
                if not tail and u >= 3 * LAYER_CHUNKS:
                    n = len(LAYER_SPLIT) + table.index(u - 3 * LAYER_CHUNKS)
                    free_at = n - HIGHS + 1
                else:
                    n = table.index(u)
                    free_at = room[n]
                before, rounds = ((DEPTH * len(LAYER_SPLIT), 0) if tail else
                                  (lay[0] * len(LAYER_SPLIT), lay[0] * (LAYER_CHUNKS // SLOTS)))
                before = before + it * (3 * SLOTS)
                self.slot, part = u // 3 % SLOTS, slice(u % 3 * UNIT, (u % 3 + 1) * UNIT)
                self.arrived = 16 * (rounds + it + (u // 3 // SLOTS + 1))
                self.room = before + (free_at + HIGHS)
                self.count = before + (n + 1)
                self.raw, self.low = ring[:, self.slot, part], ring_r[:, self.slot, part]
                kind, at = place(u)
                self.high = {"ring": highs, "gate": gate_highs, "branch": branch_highs}[kind][at]

        def high_part(eng, u, it=0):
            unit = Split(u, it)
            eng.wait_ge(w_full[unit.slot], unit.arrived)
            eng.wait_ge(h_room, unit.room)
            eng.activation(unit.high, unit.raw, ACT.Copy).then_inc(h_ready, 1)

        def low_part(eng, u, it=0):
            unit = Split(u, it)
            eng.wait_ge(h_ready, unit.count)
            eng.tensor_tensor(unit.low, unit.raw, unit.high.bitcast(F32), ALU.subtract).then_inc(l_ready, 1)

        def two_names(name, shape):
            with nc.sbuf_tensor(name, shape, F32) as plain:
                pass
            return plain, sb(name + "_r", shape, F32R)

        ring, ring_r = two_names("ring", [P, SLOTS, CHUNK])
        cst_at, n_const = columns(CONST)
        par_at, n_par = columns(PARAM)
        par2_at, n_par2 = columns(PARAM2)
        cst = sb("cst", [P, n_const])
        pars = sb("pars", [P, DEPTH * n_par])
        pl = sb("pl", [P, n_par])
        p2 = sb("p2", [P, n_par2])

        def C(name):
            return cst[:, cst_at[name][0]:cst_at[name][1]]

        def A(name):
            return pl[:, par_at[name][0]:par_at[name][1]]

        def A2(name):
            return p2[:, par2_at[name][0]:par2_at[name][1]]

        ident = C("ident")
        x = sb("x", [P, NT, D])
        xs, xs_r = two_names("xs", [P, NT, D])
        hH_buffer = sb("hH", [P, NT * D], F32R)
        gpost = sb("gpost", [P, 2, D])
        small = sb("small", [P, 96])
        eps, eps4 = small[:, 0:1], small[:, 1:2]
        ss, std, rstd = small[:, 2:4], small[:, 4:6], small[:, 6:8]
        pss, pstd, prstd = small[:, 8:10], small[:, 10:12], small[:, 12:14]
        mx3 = small[:, 16:28].rearrange("p (u n) -> p u n", u=2)
        nmx = small[:, 28:36].rearrange("p (u n) -> p u n", u=2)
        sm = small[:, 36:44].rearrange("p (u n) -> p u n", u=2)
        rs = small[:, 44:52].rearrange("p (u n) -> p u n", u=2)
        act, act_r = two_names("act", [P, 2, 2, SEQ])
        sil, gT = act[:, 0], act[:, 1]
        Sb = sb("Sb", [P, 2, 3 * 384])
        PTs, PTs_r = two_names("PTs", [P, 2, 3 * 384])
        Sflat = Sb[:, :, :].rearrange("p u n -> p (u n)")
        PTflat = PTs[:, :, :].rearrange("p u n -> p (u n)")
        junk = Sflat[:, 0:D]
        REGION = 22700
        region, region_r = two_names("region", [P, REGION])

        class Space:

            def __init__(self, ap, size):
                self.ap, self.size, self.at = ap, size, 0

            def take(self, *shape):
                n = int(np.prod(shape))
                a, self.at = self.at, self.at + n
                assert self.at <= self.size, self.at
                names = "abcd"[:len(shape)]
                return self.ap[:, a:a + n].rearrange(
                    f"p ({' '.join(names)}) -> p {' '.join(names)}", **dict(zip(names, shape)))

        r1 = Space(region[:, :], REGION)
        sg = r1.take(KD * 3, SEQ)
        memT = r1.take(KD, SEQ)
        cos_angle, sin_angle = r1.take(SEQ), r1.take(SEQ)
        at_y = r1.at
        yconvT, ynsaT, ymemT = r1.take(CF, SEQ), r1.take(4, SEQ), r1.take(4, SEQ)
        hmT = region[:, r1.at - 8 * SEQ:r1.at].rearrange("p (k t) -> p k t", k=KD)
        at_q = r1.at
        ropes = r1.take(2, 6, SEQ)
        rope_in, rope_out = ropes[:, 0], ropes[:, 1]
        mergedT = ropes.rearrange("p a b t -> p (a b) t")[:, 0:KD, :]
        hk, hv = r1.take(2, 2 * NCMP), r1.take(2, 2, 4, 32)
        kcT, vc = r1.take(NCMP), r1.take(2, HD)
        vtok, gate = r1.take(NT, 2 * P), r1.take(NT, 24)
        at_mk = r1.at
        mkT, mv = r1.take(4, SEQ), r1.take(NT, 512)
        at_g = r1.at
        qmT = r1.take(4, SEQ)
        cs, cstat = r1.take(NT, NHEAD, NCMP), r1.take(4, NT * NHEAD)
        Pc, PcT = r1.take(NT, NHEAD, 32), r1.take(2, SEQ)
        at_h = r1.at
        mt = r1.take(2, SEQ)
        s1 = Space(Sflat, 2304)
        usb, cu, cacc = s1.take(2, SEQ), s1.take(2, SEQ + 2), s1.take(2, SEQ)
        cosT, sinT = s1.take(SEQ), s1.take(SEQ)
        s2 = Space(PTflat, 2304)
        rt = s2.take(2, 2, SEQ)
        flat = s2.take(2, 16, 2, NCMP)
        r2 = Space(region[:, :], REGION)
        qkT = r2.take(24, SEQ)
        QK = r2.take(2, NT, DIL_H * HD)
        V = r2.take(NT, DIL_H * HD)
        xbcT = r2.take(16, SEQ)
        xtok = r2.take(NT, D)
        dts = r2.take(8, NT * SSD_H)
        neg_a = r2.take(SSD_H)
        acsT = r2.take(SEQ)
        stat = r2.take(4, 2 * NT * DIL_H)
        Z = gpost
        egT = act[:, :, :, :].rearrange("p a b t -> p (a b) t")
        s3 = Space(Sflat, 2304)
        xp, cv = s3.take(2, SEQ + 3), s3.take(2, SEQ)
        r3 = Space(QK.rearrange("p a b c -> p (a b c)"), 2 * NT * DIL_H * HD)
        mixedT, cbm, ebuf = r3.take(12, SEQ), r3.take(4, 384), r3.take(2, 2, 384)
        ysb = xbcT[:, 0:8, :].rearrange("p (i f) t -> p i (f t)", i=NT)
        yt = xbcT[:, 8:16, :].rearrange("p (i f) t -> p i (f t)", i=NT)
        ogT = xbcT[:, 0:8, :]
        H_ring = region_r[:, 0:HIGHS * UNIT]
        highs = [H_ring[:, s * UNIT:(s + 1) * UNIT] for s in range(HIGHS)]

        def parts(ap):
            return ap.rearrange("p (i k t) -> p i k t", i=NT, k=KD)

        hH = parts(hH_buffer)
        hL = parts(xs_r[:, :, :].rearrange("p i n -> p (i n)"))
        h_whole = parts(xs[:, :, :].rearrange("p i n -> p (i n)"))
        gate_highs = [region_r[:, at_h:at_h + UNIT], region_r[:, at_h + UNIT:at_h + 2 * UNIT],
                      act_r[:, :, :, :].rearrange("p a b t -> p (a b t)"),
                      region_r[:, at_q:at_q + UNIT]]
        yH = region_r[:, at_mk:at_mk + 12 * SEQ].rearrange("p (k t) -> p k t", k=12)
        yL = region_r[:, at_y:at_y + 12 * SEQ].rearrange("p (k t) -> p k t", k=12)
        y_whole = region[:, at_y:at_y + 12 * SEQ].rearrange("p (k t) -> p k t", k=12)
        branch_highs = [buffer[:, half * UNIT:(half + 1) * UNIT]
                        for buffer in (hH_buffer, xs_r[:, :, :].rearrange("p i n -> p (i n)")) for half in range(2)]
        Y_GROUPS = [(0, 4), (8, 12), (4, 5), (5, 6), (6, 7), (7, 8)]
        g_parts = region_r[:, at_g:at_g + 4 * SEQ].rearrange("p (h c t) -> p h c t", h=2, c=2)
        gH, gL = g_parts[:, 0], g_parts[:, 1]

        w_full = [sem(f"w_full{s}") for s in range(SLOTS)]
        w_used = [sem(f"w_used{s}") for s in range(SLOTS)]
        h_ready, l_ready = sem("h_ready"), sem("l_ready")
        h_room = sem("h_room")
        nH_ready, nL_ready = sem("nH_ready"), sem("nL_ready")
        yH_ready, yL_ready = sem("yH_ready"), sem("yL_ready")
        g_steps = sem("g_steps")
        gp_full = [sem(f"gp_full{s}") for s in range(2)]
        ident_in, const_in, par_in, par2_in = (sem(n) for n in ("ident_in", "const_in", "par_in", "par2_in"))
        x_here, mem_here, pos_here = sem("x_here"), sem("mem_here"), sem("pos_here")
        x_ready = sem("x_ready")
        std_ready = sem("std_ready")
        xs_ready = sem("xs_ready")
        post_std = sem("post_std")
        sil_ready = sem("sil_ready")
        rope_ready, hm_ready = sem("rope_ready"), sem("hm_ready")
        cmp_sub, cmp_exp, cmp_p = sem("cmp_sub"), sem("cmp_exp"), sem("cmp_p")
        mx_ready = sem("mx_ready")
        exp_done = sem("exp_done")
        p_ready = sem("p_ready")
        merged = sem("merged")
        conv_done, conv_act = sem("conv_done"), sem("conv_act")
        qk_var, qk_std, qk_ready = sem("qk_var"), sem("qk_std"), sem("qk_ready")
        dt_abs, dt_exp, a_ready, xdt_ready = sem("dt_abs"), sem("dt_exp"), sem("a_ready"), sem("xdt_ready")
        decay_in, decay_exp, decay_done = sem("decay_in"), sem("decay_exp"), sem("decay_done")
        y_sq, y_std, y_ready = sem("y_sq"), sem("y_std"), sem("y_ready")
        trig_in, trig_done = sem("trig_in"), sem("trig_done")
        stored = sem("stored")

        class Own:

            def __init__(self, eng, counted, per_layer):
                self.eng, self.sem, self.per_layer = eng, counted, per_layer
                self.n = self.before = 0

            def __call__(self, instruction):
                instruction.then_inc(self.sem, 1)
                self.n += 1

            def settle(self):
                self.eng.wait_ge(self.sem, self.before + lay[0] * self.per_layer + self.n)

            def layer_begins(self):
                self.before, self.n = self.n, 0

            def layer_ends(self):
                assert self.n == self.per_layer, (self.sem, self.n)
                self.n = 0

        def layers(eng, body, counter=None):
            if counter is not None:
                counter.layer_begins()
            with eng.Fori(0, DEPTH) as index:
                lay[0] = index
                body()
            if counter is not None:
                counter.layer_ends()
            lay[0] = DEPTH

        def repeat(eng, n, body):
            with eng.Fori(0, n) as index:
                body(index)

        def unit_base(tag):
            return {"mix": lay[0] * len(MIX_UNITS), "dil": DEPTH * len(MIX_UNITS),
                    "moba": DEPTH * len(MIX_UNITS) + len(EVEN_UNITS)}[tag]

        def prob_tiles(kind, s, b):
            p = scores_of(kind, s)
            if kind == "mem":
                at = [i * SEQ + n * P for n in range(NT) for i in range(NT)]
            elif kind == "dil":
                at = [b * P, 384 + b * SEQ, 384 + b * SEQ + P]
            else:
                at = [b * 384 + n * P for n in range(3)]
            return [p[:, a:a + P] for a in at]

        def scores_of(kind, s):
            n = s % SCORE_BUFFERS
            if kind == "dil":
                return (Sb[:, 0], Sb[:, 1], xs[:, :, :].rearrange("p i n -> p (i n)")[:, 0:1152])[n]
            return Sflat[:, n * 768:(n + 1) * 768]

        def out_half(unit):
            kind, h, g = unit
            if kind == "mem":
                return slice(0, P)
            half = g if kind == "nsa" else h % 2
            return slice(half * HD, (half + 1) * HD)

        def probs_of(kind, s):
            if kind == "mem":
                return [((0, SEQ), 0), ((SEQ, 2 * SEQ), 1)]
            if kind == "dil":
                return [((0, 384), 0), ((384, 1152), 1)]
            return [(r, 2 * b + i) for b in range(BRANCHES[kind])
                    for i, r in enumerate(((b * 384, b * 384 + P), (b * 384 + P, b * 384 + 384)))]

        block = ctx.enter_context(nc.Block())

        @block.sync
        def _(sp):
            lay[0] = 0
            first = P + 1
            sp.dma_start(cst[:, 0:first], const[:, 0:first]).then_inc(ident_in, 16)
            sp.dma_start(xs[:, :, :], mem_in).then_inc(mem_here, 16)
            sp.dma_start(x[:, :, :], x_in).then_inc(x_here, 16)
            sp.dma_start(pars[:, :], par).then_inc(par_in, 16)
            for s in range(SLOTS):
                sp.dma_start(ring[:, s, :], weights[s]).then_inc(w_full[s], 16)
            sp.dma_start(cst[:, first:], const[:, first:]).then_inc(const_in, 16)
            sp.dma_start(p2[:, :], par2).then_inc(par2_in, 16)

            def round_of_slots(r):
                for s in range(SLOTS):
                    sp.wait_ge(w_used[s], r + (s == LAST_SLOT))
                    sp.dma_start(ring[:, s, :], weights[r * SLOTS + s]).then_inc(w_full[s], 16)

            with sp.Fori(1, CHUNKS // SLOTS) as r:
                round_of_slots(r)
            lay[0] = DEPTH
            for i in range(NT):
                for half in range(2):
                    Job("odd_out", 2 * i + half).wait_emptied(sp)
                sp.dma_start(out[:, i], x[:, i, :]).then_inc(stored, 16)
            sp.wait_ge(stored, 16 * NT)

        @block.gpsimd
        def _(pool):
            lay[0] = 0
            pool.dma_start(rope_out[:, 0, :].bitcast(I32), pos_in[0].partition_broadcast(P)).then_inc(pos_here, 16)

            step = Own(pool, sem("pool_own"), 0)
            step(pool.memset(hv.rearrange("p m g j n -> p (m g j n)"), 0.0))
            step(pool.memset(Pc.rearrange("p i h n -> p (i h n)"), 0.0))
            pool.wait_ge(pos_here, 16)
            pool.wait_ge(ident_in, 16)
            ang, turns_, whole = (rope_in[:, j, :] for j in range(3))
            step(pool.tensor_copy(ang, rope_out[:, 0, :].bitcast(I32)))
            step.settle()
            step(pool.tensor_scalar(ang, ang, C("inv"), None, ALU.mult))
            step.settle()
            step(pool.tensor_scalar(turns_, ang, 1 / (2 * np.pi), MAGIC, ALU.mult, ALU.add))
            step.settle()
            step(pool.tensor_scalar(turns_, turns_, MAGIC, None, ALU.subtract))
            for part in TWO_PI:
                step.settle()
                step(pool.tensor_scalar(whole, turns_, -part, None, ALU.mult))
                step.settle()
                step(pool.tensor_tensor(ang, ang, whole, ALU.add))
            step.settle()
            step(pool.tensor_scalar(sin_angle, ang, PI_BELOW, -PI_BELOW, ALU.min, ALU.max))
            step(pool.tensor_scalar(ang, ang, np.pi / 2, None, ALU.add))
            step.settle()
            step(pool.tensor_scalar(turns_, ang, np.pi, -2 * np.pi, ALU.is_gt, ALU.mult))
            step.settle()
            step(pool.tensor_tensor(ang, ang, turns_, ALU.add))
            step.settle()
            pool.tensor_scalar(cos_angle, ang, PI_BELOW, -PI_BELOW, ALU.min, ALU.max).then_inc(trig_in, 1)

            def body():
                for j, slot in enumerate((0, 1, 0)):
                    pool.wait_ge(x_ready, 2 + 6 * lay[0] + (2 if j == 2 else 0))
                    pool.dma_start(gpost[:, slot, :], posts[3 * lay[0] + j].partition_broadcast(P))\
                        .then_inc(gp_full[slot], 16)
                    if j == 1:
                        pool.wait_ge(l_ready, Split(U_GATE).count - 1)
                        for u in GATE_UNITS + BRANCH_UNITS:
                            low_part(pool, u)

            layers(pool, body)
            pool.wait_ge(l_ready, DEPTH * len(LAYER_SPLIT) + AHEAD)
            for u in TAIL_SPLIT[AHEAD:]:
                low_part(pool, u)

        @block.tensor
        def _(pe):
            lay[0] = 0
            used = []

            def mm(bank, lhsT, rhs, start, stop, signal=None):
                ins = pe.matmul(bank, lhsT, rhs, start=start, stop=stop)
                if signal is not None:
                    ins.then_inc(signal, 1)
                elif used:
                    ins.then_inc(used.pop(0), 1)

            def turn(bank, tile, signal=None):
                ins = pe.transpose(bank, tile, ident)
                if signal is not None:
                    ins.then_inc(signal, 1)
                elif used:
                    ins.then_inc(used.pop(0), 1)

            def chunk(n, plus=0):
                pe.wait_ge(w_full[n % SLOTS], 16 * (chunk_round(n) + plus + 1))
                return ring[:, n % SLOTS, :]

            def chunk_round(n):
                if n < LAYER_CHUNKS and lay[0] is not DEPTH:
                    return lay[0] * (LAYER_CHUNKS // SLOTS) + n // SLOTS
                return n // SLOTS

            def norm(name, k):
                for i in range(NT):
                    pe.wait_ge(xs_ready, NT * k + i + 1)
                    for half in range(2):
                        job = Job("norm", name, i, half)
                        job.wait_empty(pe)
                        for kk in range(4):
                            f = 4 * half + kk
                            turn(job.bank[:, kk * P:(kk + 1) * P], xs[:, i, f * P:(f + 1) * P],
                                 job.full if kk == 3 else None)

            def normed(name):
                all_emptied(pe, [("norm", name, i, half) for i in range(NT) for half in range(2)])

            def feature_tile(job, w, rhs, k=KD):
                job.wait_empty(pe)
                for kk in range(k):
                    mm(job.bank[:, 0:SEQ], w[:, kk * P:(kk + 1) * P], rhs[:, kk, :],
                       kk == 0, kk == k - 1, job.full if kk == k - 1 else None)

            def parted(k):
                pe.wait_ge(nL_ready, 4 * (k + 1))

            def products(out, lhs, rhs, start, stop, signal=None):
                pairs = ((0, 0), (0, 1), (1, 0))
                for n, (a, b) in enumerate(pairs):
                    mm(out, lhs[a], rhs[b], start and n == 0, stop and n == 2, signal if n == 2 else None)

            def split_tile(job, half, u, it=0):
                unit = Split(u, it)
                pe.wait_ge(l_ready, unit.count)
                to = job.bank[:, half * SEQ:(half + 1) * SEQ].rearrange("p (i t) -> p i t", i=NT)
                return unit, [(to, [w[:, kk * P:(kk + 1) * P] for w in (unit.high, unit.low)],
                               [h[:, :, kk, :] for h in (hH, hL)], kk == 0, kk == KD - 1) for kk in range(KD)]

            def split_feature(job, u):
                job.wait_empty(pe)
                _, todo = split_tile(job, 0, u)
                for n, args in enumerate(todo):
                    products(*args, job.full if n == KD - 1 else None)
                used.append(h_room)

            def ffn(f, k):
                at = U_FFN2 if f else U_FFN1
                norm(("ffn", f), k)
                parted(k - 1)
                outs = [Job(("ffn_out", f), j) for j in range(4)]

                def up(t, it=0):
                    job = Job("ff", f, t, plus=2 * it)
                    job.wait_empty(pe)
                    ua, ub = at + (3 * t - 1 if t else 0), at + (3 * t if t else 1)
                    _, todo = split_tile(job, 0, ua, it)
                    for n, args in enumerate(todo):
                        products(*args, h_room if n == KD - 1 else None)
                    if ua % 3 == 2:
                        used.append(w_used[ua // 3 % SLOTS])
                    _, todo = split_tile(job, 1, ub, it)
                    for n, args in enumerate(todo):
                        products(*args, job.full if n == KD - 1 else None)
                    used.append(h_room)

                def down(t, it=0, first=False, last=False):
                    Job("ff", f, t, plus=2 * it).wait_emptied(pe)
                    u = at + (3 * t + 4 if t < FT - 1 else 3 * t + 2)
                    unit = Split(u, it)
                    pe.wait_ge(l_ready, unit.count)
                    for j, out_job in enumerate(outs):
                        i, half = j // 2, j % 2
                        if first:
                            out_job.wait_empty(pe)
                        products(out_job.bank, [g[:, t % 2, i * P:(i + 1) * P] for g in (gH, gL)],
                                 [w[:, half * 512:(half + 1) * 512] for w in (unit.high, unit.low)],
                                 first, last, out_job.full if last else h_room if j == 3 else None)
                    if last:
                        used.extend((w_used[u // 3 % SLOTS], h_room))

                up(0)
                up(1)
                down(0, first=True)

                def body(it):
                    for c in range(SLOTS):
                        up(2 + c, it)
                        down(1 + c, it)

                repeat(pe, (FT - 2) // SLOTS, body)
                down(FT - 1, last=True)

            def attention(tag, units, q_of, k_of, v_of, extra=None):
                base = unit_base(tag)

                def scores(s, branches):
                    kind = units[s][0]
                    for b in branches:
                        job = Job("S", tag, s, b)
                        job.wait_empty(pe)
                        q, k = q_of(s, b), k_of(s, b)
                        if kind == "mem":
                            for i in range(NT):
                                mm(job.bank[:, i * SEQ:(i + 1) * SEQ], q[:, i * P:(i + 1) * P], k,
                                   True, True, job.full if i else None)
                        else:
                            mm(job.bank[:, 0:P], q[:, 0:P], k[:, 0:P], True, True)
                            mm(job.bank[:, P:3 * P], q[:, P:SEQ], k, True, True, job.full)

                def turns(s, branches):
                    pe.wait_ge(p_ready, base + s + 1)
                    for b in branches:
                        job = Job("PT", tag, s, b)
                        job.wait_empty(pe)
                        tiles = prob_tiles(units[s][0], s, b)
                        for n, tile in enumerate(tiles):
                            turn(job.bank[:, n * P:(n + 1) * P], tile, job.full if n == len(tiles) - 1 else None)

                def outputs(s):
                    kind = units[s][0]
                    job = Job("PV", tag, s)
                    job.wait_empty(pe)
                    todo = []
                    half = out_half(units[s])
                    for b in range(BRANCHES[kind]):
                        Job("PT", tag, s, b).wait_emptied(pe)
                        pt = PTs[:, s % 2, b * 384:]
                        if kind == "mem":
                            pt = PTs[:, s % 2, :]
                            for n in range(NT):
                                todo.append((job.bank[:, 0:SEQ], v_of(s, b)[n], pt[:, n * SEQ:(n + 1) * SEQ]))
                        else:
                            v0, v1 = v_of(s, b)
                            todo.append((job.bank[half, 0:SEQ], v0, pt[:, 0:SEQ]))
                            todo.append((job.bank[half, P:SEQ], v1, pt[:, SEQ:3 * P]))
                    if kind == "nsa":
                        _, a, g = units[s]
                        rows = slice(32 * a, 32 * a + 32)
                        todo.append((job.bank[half, 0:SEQ], vc[rows, g, :], PcT[rows, g, :]))
                    for n, (o, v, p) in enumerate(todo):
                        mm(o, v, p, n == 0, n == len(todo) - 1, job.full if n == len(todo) - 1 else None)

                lag = LAG[tag]
                for s in range(len(units) + lag + 1):
                    for some in (range(0, 2), range(2, 3)):
                        if s < len(units):
                            scores(s, [b for b in some if b < BRANCHES[units[s][0]]])
                        if extra is not None and some.start == 0:
                            extra(s)
                        if 0 <= s - lag < len(units):
                            turns(s - lag, [b for b in some if b < BRANCHES[units[s - lag][0]]])
                    if s > lag:
                        outputs(s - lag - 1)

            def mixer(k):
                pe.wait_ge(hm_ready, lay[0] + 1)
                w = chunk(AT_C)
                for h in range(3):
                    feature_tile(Job("mk", h), w[:, h * MTILE:], hmT)
                used.append(w_used[AT_C % SLOTS])
                norm("mix", k)
                w = chunk(AT_C + 1)
                feature_tile(Job("mk", 3), w, hmT)
                jobs = [Job("mv", i) for i in range(NT)]
                for kk in range(KD):
                    if kk == 4:
                        used.append(w_used[(AT_C + 1) % SLOTS])
                        w = chunk(AT_C + 2)
                    at = (MTILE if kk < 4 else 0) + kk % 4 * 512
                    for i, job in enumerate(jobs):
                        if kk == 0:
                            job.wait_empty(pe)
                        mm(job.bank, hmT[:, kk, i * P:(i + 1) * P], w[:, at:at + 512],
                           kk == 0, kk == KD - 1, job.full if kk == KD - 1 else None)
                used.append(w_used[(AT_C + 2) % SLOTS])
                normed("mix")
                pe.wait_ge(const_in, 16)
                pe.wait_ge(par_in, 16)
                parted(k - 1)
                turn_next = []

                def rotated():
                    if turn_next:
                        kind, at = turn_next.pop(0)
                        Job(kind, at).wait_emptied(pe)
                        job = Job("rot", kind, at)
                        job.wait_empty(pe)
                        pe.matmul(job.bank[:, 0:SEQ], C("rotate"), rope_in[:, ROPED.index((kind, at)), :],
                                  start=True, stop=True).then_inc(job.full, 1)

                for n, (kind, at) in enumerate(MIX_TILES):
                    split_feature(Job(kind, at), U_A + n)
                    if n % 3 == 2 or n == len(MIX_TILES) - 1:
                        used.append(w_used[(AT_A + n // 3) % SLOTS])
                    rotated()
                    if (kind, at) in ROPED:
                        turn_next.append((kind, at))
                pe.wait_ge(l_ready, Split(U_B + N_B - 1).count)
                ws = [H_ring[:, 0:N_B * UNIT], ring_r[:, AT_B % SLOTS, :]]
                for i in range(NT):
                    job = Job("tok", i)
                    job.wait_empty(pe)
                    for kk in range(KD):
                        products(job.bank[:, 0:280], [h[:, i, kk, :] for h in (hH, hL)],
                                 [w[:, kk * 280:(kk + 1) * 280] for w in ws],
                                 kk == 0, kk == KD - 1, job.full if kk == KD - 1 else None)
                used.extend([h_room] * N_B + [w_used[AT_B % SLOTS]])
                for c in range(2):
                    for g in range(2):
                        Job("kc" if c == 0 else "vc", g).wait_emptied(pe)
                    jobs = [Job("hid", c, m) for m in range(2)]
                    for jj in range(16):
                        if jj % 8 == 0:
                            w = chunk(AT_D + 2 * c + jj // 8)
                        for m, job in enumerate(jobs):
                            if jj == 0:
                                job.wait_empty(pe)
                            at = jj % 8 * 256 + m * P
                            mm(job.bank[:, 0:2 * NCMP], w[:, at:at + P],
                               flat[:, c, jj, :, :].rearrange("p g n -> p (g n)"),
                               jj == 0, jj == 15, job.full if jj == 15 else None)
                        if jj % 8 == 7:
                            used.append(w_used[(AT_D + 2 * c + jj // 8) % SLOTS])
                job = Job("cmp_kv")
                job.wait_empty(pe)
                for m in range(2):
                    Job("hid", 0, m).wait_emptied(pe)
                for g in range(2):
                    for m in range(2):
                        mm(job.bank[g * HD:(g + 1) * HD, 0:NCMP], A("w2k")[:, m * HD:(m + 1) * HD],
                           hk[:, m, g * NCMP:(g + 1) * NCMP], m == 0, m == 1)
                for m in range(2):
                    Job("hid", 1, m).wait_emptied(pe)
                for g in range(2):
                    for m in range(2):
                        mm(job.bank[:, (g + 1) * HD:(g + 2) * HD], hv[:, m, g].rearrange("p j n -> p (j n)"),
                           A("w2v")[:, m * HD:(m + 1) * HD], m == 0, m == 1, job.full if g and m else None)
                job.wait_emptied(pe)
                for g in range(2):
                    job = Job("cmp_S", g)
                    job.wait_empty(pe)
                    rows = slice(g * HD, (g + 1) * HD)
                    for i in range(NT):
                        for a in range(4):
                            at = (i * 4 + a) * NCMP
                            mm(job.bank[:, at:at + NCMP], rope_in[rows, a, i * P:(i + 1) * P], kcT[rows, :],
                               True, True, job.full if i and a == 3 else None)

                def compressed_turned():
                    pe.wait_ge(cmp_p, lay[0] + 1)
                    job = Job("cmp_PT")
                    job.wait_empty(pe)
                    for g in range(2):
                        for i in range(NT):
                            turn(job.bank[:, g * SEQ + i * P:g * SEQ + (i + 1) * P],
                                 Pc[:, i, 4 * g:4 * g + 4, :].rearrange("p h n -> p (h n)"),
                                 job.full if g and i else None)

                def gates(s):
                    for n in gates_at(s):
                        m, b = divmod(n, 3)
                        split_feature(Job("gate", m, b), U_GATE + n)
                        if b == 2:
                            used.append(w_used[(AT_GATE + m) % SLOTS])
                    if s == 1:
                        compressed_turned()

                def q_of(s, b):
                    kind, a, g = MIX_UNITS[s]
                    return qmT[:, a, :] if kind == "mem" else rope_out[g * HD:(g + 1) * HD, a, :]

                def k_of(s, b):
                    kind, a, g = MIX_UNITS[s]
                    return mkT[:, a, :] if kind == "mem" else rope_out[g * HD:(g + 1) * HD, 4 + b, :]

                def v_of(s, b):
                    kind, a, g = MIX_UNITS[s]
                    if kind == "mem":
                        return [mv[:, n, a * P:(a + 1) * P] for n in range(NT)]
                    at = b * P + g * HD
                    return [vtok[:, n, at:at + HD] for n in range(NT)]

                pe.wait_ge(rope_ready, (lay[0] + 1) * len(ROPED))
                all_emptied(pe, [(n, i) for n in ("tok", "mv") for i in range(NT)]
                            + [(n, h) for n in ("qm", "mk") for h in range(4)])
                attention("mix", MIX_UNITS, q_of, k_of, v_of, gates)
                for m in range(KD):
                    for b in range(3):
                        job = Job("branch", m, b)
                        job.wait_empty(pe)
                        if m == 0:
                            pe.wait_ge(yL_ready, len(Y_GROUPS) * lay[0] + (1 if b == 0 else len(Y_GROUPS)))
                        n = 3 * m + b
                        unit = Split(U_BRANCH + n // 2)
                        pe.wait_ge(l_ready, unit.count)
                        for kk in range(4):
                            at = n % 2 * 512 + kk * P
                            products(job.bank[:, 0:SEQ], [w[:, at:at + P] for w in (unit.high, unit.low)],
                                     [y[:, 4 * b + kk, :] for y in (yH, yL)],
                                     kk == 0, kk == 3, job.full if kk == 3 else None)
                        if n % 2:
                            used.append(h_room)
                        if n % 6 == 5:
                            used.append(w_used[(AT_BRANCH + n // 6) % SLOTS])
                project("mixed", AT_OUT, KD, mergedT, lambda kk: pe.wait_ge(merged, KD * lay[0] + kk + 1))

            def project(name, at, k, lhs, before):
                jobs = [Job(name, j) for j in range(4)]
                for i in range(NT):
                    for kk in range(k):
                        if kk % 3 == 0:
                            w = chunk(at + kk // 3)
                        if i == 0:
                            before(kk)
                        for half in range(2):
                            job = jobs[2 * i + half]
                            if kk == 0:
                                job.wait_empty(pe)
                            c = kk % 3 * D + half * 512
                            mm(job.bank, lhs[:, kk, i * P:(i + 1) * P], w[:, c:c + 512],
                               kk == 0, kk == k - 1, job.full if kk == k - 1 else None)
                        if i and (kk % 3 == 2 or kk == k - 1):
                            used.append(w_used[(at + kk // 3) % SLOTS])

            def token_blocks(name, blocks, at):
                for c in range(blocks):
                    jobs = [Job(name, c, i) for i in range(NT)]
                    for kk in range(KD):
                        n = c * KD + kk
                        if n % 2 == 0:
                            unit = Split(3 * at + n // 2)
                            pe.wait_ge(l_ready, unit.count)
                        for i, job in enumerate(jobs):
                            if kk == 0:
                                job.wait_empty(pe)
                            products(job.bank, [h[:, i, kk, :] for h in (hH, hL)],
                                     [w[:, n % 2 * 512:(n % 2 + 1) * 512] for w in (unit.high, unit.low)],
                                     kk == 0, kk == KD - 1, job.full if kk == KD - 1 else None)
                        if n % 2:
                            used.append(h_room)
                        if n % 6 == 5:
                            used.append(w_used[(at + n // 6) % SLOTS])

            def heads_turned(tag, n_jobs, tiles):
                for n in range(n_jobs):
                    qk, f = divmod(2 * n, tiles)
                    job = Job("qkT", tag, n)
                    job.wait_empty(pe)
                    base = 4 if tag == "moba" else 0
                    pe.wait_ge(qk_ready, base + 2 * qk + 2)
                    for t in range(2):
                        for i in range(NT):
                            turn(job.bank[:, t * SEQ + i * P:t * SEQ + (i + 1) * P],
                                 QK[:, qk, i, (f + t) * P:(f + t + 1) * P], job.full if t and i else None)
                all_emptied(pe, [("qkT", tag, n) for n in range(n_jobs)])

            pe.wait_ge(ident_in, 16)
            norm("mem", 0)

            def body():
                used[:] = [w_used[LAST_SLOT], h_room]
                ffn(0, 1 + 3 * lay[0])
                mixer(2 + 3 * lay[0])
                ffn(1, 3 + 3 * lay[0])
                assert used == [w_used[LAST_SLOT], h_room] and used[1] is h_room

            layers(pe, body)

            norm("even", 7)
            normed("even")
            parted(6)
            for n in range(20):
                split_feature(Job("xbc", n) if n < 16 else Job("eg", n - 16), U_EA + n)
                if n % 3 == 2 or n == 19:
                    used.append(w_used[(AT_EA + n // 3) % SLOTS])
            pe.wait_ge(conv_act, 16)
            for n in range(4):
                i, half = n // 2, n % 2
                job = Job("xs", n)
                job.wait_empty(pe)
                for kk in range(4):
                    turn(job.bank[:, kk * P:(kk + 1) * P], xbcT[:, 4 * half + kk, i * P:(i + 1) * P],
                         job.full if kk == 3 else None)
            token_blocks("eb", 11, AT_EB)
            unit = Split(U_EB + N_EB - 1)
            pe.wait_ge(l_ready, unit.count)
            for i in range(NT):
                job = Job("dt", i)
                job.wait_empty(pe)
                for kk in range(KD):
                    products(job.bank[:, 0:SSD_H], [h[:, i, kk, :] for h in (hH, hL)],
                             [w[:, kk * SSD_H:(kk + 1) * SSD_H] for w in (unit.high, unit.low)],
                             kk == 0, kk == KD - 1, job.full if kk == KD - 1 else None)
            used.append(h_room)
            used.append(w_used[(AT_EO - 1) % SLOTS])
            heads_turned("dil", 12, 12)
            for g in range(4):
                job = Job("cb", g)
                job.wait_empty(pe)
                b_, c_ = xbcT[:, 8 + g, :], xbcT[:, 12 + g, :]
                mm(job.bank[:, 0:SEQ], b_[:, 0:P], c_, True, True)
                mm(job.bank[:, SEQ:3 * P], b_[:, P:SEQ], c_[:, P:SEQ], True, True, job.full)
            pe.wait_ge(a_ready, 1)
            job = Job("acs")
            job.wait_empty(pe)
            a = dts[:, 7, :].rearrange("p (i h) -> p i h", i=NT)
            mm(job.bank[:, 0:SSD_H], C("upto"), a[:, 0, :], True, True)
            mm(job.bank[:, SSD_H:2 * SSD_H], C("ones"), a[:, 0, :], True, False)
            mm(job.bank[:, SSD_H:2 * SSD_H], C("upto"), a[:, 1, :], False, True, job.full)
            job.wait_emptied(pe)
            acs = dts[:, 2, :].rearrange("p (i h) -> p i h", i=NT)
            job = Job("acsT")
            job.wait_empty(pe)
            for i in range(NT):
                turn(job.bank[0:SSD_H, i * P:(i + 1) * P], acs[:, i, :], job.full if i else None)
            job.wait_emptied(pe)
            pe.wait_ge(xdt_ready, 1)
            outs = [Job("scan", j) for j in range(4)]
            for n in range(9):
                if n < 8:
                    job = Job("decay", n)
                    job.wait_empty(pe)
                    for hh in range(2):
                        h = 2 * n + hh
                        mm(job.bank[:, hh * SEQ:(hh + 1) * SEQ], ident[0:SSD_H, h:h + 1].broadcast_to([SSD_H, P]),
                           acsT[0:SSD_H, :], True, True, job.full if hh else None)
                if n >= 1:
                    pe.wait_ge(decay_done, n)
                    for hh in range(2):
                        h = 2 * (n - 1) + hh
                        e, cols = ebuf[:, (n - 1) % 2, hh, :], slice(h % 8 * HD, (h % 8 + 1) * HD)
                        j0, j1 = outs[h // 8], outs[2 + h // 8]
                        if h % 8 == 0:
                            j0.wait_empty(pe)
                            j1.wait_empty(pe)
                        last = h % 8 == 7
                        mm(j0.bank[:, cols], e[:, 0:P], xs[:, 0, h * HD:(h + 1) * HD], True, True,
                           j0.full if last else None)
                        mm(j1.bank[:, cols], e[:, P:2 * P], xs[:, 0, h * HD:(h + 1) * HD], True, False)
                        mm(j1.bank[:, cols], e[:, 2 * P:3 * P], xs[:, 1, h * HD:(h + 1) * HD], False, True,
                           j1.full if last else None)

            def head_rows(tile, half):
                return qkT[half * HD:(half + 1) * HD, tile, :]

            attention("dil", EVEN_UNITS,
                      lambda s, b: head_rows(4 * b + s // 2, s % 2),
                      lambda s, b: head_rows(12 + 4 * b + s // 2, s % 2),
                      lambda s, b: [V[:, n, (8 * b + s) * HD:(8 * b + s + 1) * HD] for n in range(NT)])
            pe.wait_ge(y_ready, 1)
            for n in range(4):
                i, half = n // 2, n % 2
                job = Job("yT", n)
                job.wait_empty(pe)
                for kk in range(4):
                    f = 4 * half + kk
                    turn(job.bank[:, kk * P:(kk + 1) * P], ysb[:, i, f * P:(f + 1) * P],
                         job.full if kk == 3 else None)
            all_emptied(pe, [("yT", n) for n in range(4)] + [("PV", "dil", s) for s in range(8)])
            project("even_out", AT_EO, 12, mixedT, lambda kk: None)

            norm("odd", 8)
            normed("odd")
            parted(7)
            token_blocks("ob", 6, AT_OB)
            for n in range(8):
                split_feature(Job("og", n), U_OA + n)
                if n % 3 == 2 or n == 7:
                    used.append(w_used[(AT_OA + n // 3) % SLOTS])
            heads_turned("moba", 8, 8)
            attention("moba", ODD_UNITS,
                      lambda s, b: head_rows(s // 2, s % 2),
                      lambda s, b: head_rows(8 + s // 2, s % 2),
                      lambda s, b: [V[:, n, s * HD:(s + 1) * HD] for n in range(NT)])
            all_emptied(pe, [("PV", "moba", s) for s in range(MOBA_H)])
            project("odd_out", AT_OO, 8, mixedT, lambda kk: None)

        @block.scalar
        def _(act_):
            lay[0] = 0
            own = Own(act_, sem("act_own"), ACT_OWN)

            def table(func):
                own(act_.activation(small[:, 15:16], eps4, func))

            def norm(k, source=x, after=None, tiles=range(NT)):
                for i in tiles:
                    if after is not None:
                        for half in range(2):
                            Job(after, 2 * i + half).wait_emptied(act_)
                    elif source is x:
                        act_.wait_ge(x_ready, NT * (k - 1) + i + 1)
                    own(act_.activation(junk, source[:, i, :], ACT.Square, accum_out=ss[:, i:i + 1]))
                    own.settle()
                    act_.activation(std[:, i:i + 1], ss[:, i:i + 1], ACT.Sqrt, bias=eps, scale=1.0 / D)\
                        .then_inc(std_ready, 1)

            def post(name, weight, tiles=range(NT)):
                for i in tiles:
                    for half in range(2):
                        Job(name, 2 * i + half).wait_full(act_)
                    y = psum[:, 4 + 2 * i:6 + 2 * i, :].rearrange("p b n -> p (b n)")
                    own(act_.activation(junk, y, ACT.Square, accum_out=pss[:, i:i + 1]))
                    own.settle()
                    act_.activation(pstd[:, i:i + 1], pss[:, i:i + 1], ACT.Sqrt, bias=eps if weight == 1.0 else eps4,
                                    scale=1.0 / (D * weight**2))\
                        .then_inc(post_std, 1)

            def split(first, lo, hi):
                for u in range(first + lo, first + hi):
                    high_part(act_, u)

            def norm_parts(name):
                for i in range(NT):
                    for half in range(2):
                        Job("norm", name, i, half).wait_emptied(act_)
                        act_.activation(hH[:, i, 4 * half:4 * half + 4, :],
                                        h_whole[:, i, 4 * half:4 * half + 4, :], ACT.Copy).then_inc(nH_ready, 1)

            def ffn(f, k):
                norm_parts(("ffn", f))
                first = U_FFN2 if f else U_FFN1
                split(first, AHEAD, HIGHS)
                table(ACT.Silu)

                def silu(t, it=0):
                    job = Job("ff", f, t, plus=2 * it)
                    job.wait_full(act_)
                    act_.activation(sil[:, t % 2, :], job.bank[:, 0:SEQ], ACT.Silu).then_inc(sil_ready, 1)

                def body(it):
                    for c in range(SLOTS):
                        silu(c, it)
                        for n in range(3):
                            high_part(act_, first + HIGHS + 3 * c + n, it)

                repeat(act_, (FT - 2) // SLOTS, body)
                silu(FT - 2)
                silu(FT - 1)
                table(ACT.Sqrt)
                if f == 1:
                    split(3 * LAYER_CHUNKS, 0, AHEAD)
                post(("ffn_out", f), 0.5)
                if f == 1:
                    norm(k + 1)

            def copy(job, dst, src, func=ACT.Copy, **kw):
                job.wait_full(act_)
                act_.activation(dst, src, func, **kw).then_inc(job.free, 1)

            def attention(tag, units, extra=None):
                base = unit_base(tag)

                def exps(s):
                    kind = units[s][0]
                    act_.wait_ge(mx_ready, base + s + 1)
                    scale = SCALE_MEM if kind == "mem" else SCALE
                    todo = probs_of(kind, s)
                    for n, ((a, b), c) in enumerate(todo):
                        p = scores_of(kind, s)[:, a:b]
                        ins = act_.activation(p, p, ACT.Exp, bias=nmx[:, s % 2, c:c + 1],
                                              scale=scale, accum_out=sm[:, s % 2, c:c + 1])
                        if n == len(todo) - 1:
                            ins.then_inc(exp_done, 1)

                def evacuate(s, branches):
                    kind = units[s][0]
                    for b in branches:
                        job = Job("PT", tag, s, b)
                        if b == 0 and s >= 2:
                            Job("PV", tag, s - 2).wait_full(act_)
                        n = 512 if kind == "mem" else 384
                        copy(job, PTs[:, s % 2, b * 384:b * 384 + n], job.bank[:, 0:n])

                for s in range(len(units) + LAG[tag]):
                    turned = s - LAG[tag]
                    n = BRANCHES[units[turned][0]] if turned >= 0 else 0
                    if n == 3:
                        evacuate(turned, range(0, 2))
                    if s < len(units):
                        exps(s)
                    if extra is not None:
                        extra(s)
                    evacuate(turned, range(2 if n == 3 else 0, n))

            def mixer(k):
                def memory_keys(h):
                    job = Job("mk", h)
                    copy(job, mkT[:, h, :], job.bank[:, 0:SEQ])

                memory_keys(0)
                norm(k, tiles=[0])
                memory_keys(1)
                norm(k, tiles=[1])
                memory_keys(2)
                norm_parts("mix")
                for u in AB_UNITS[:HIGHS]:
                    high_part(act_, u)
                act_.wait_ge(trig_in, 1)
                own(act_.activation(sinT, sin_angle, ACT.Sin))
                act_.activation(cosT, cos_angle, ACT.Sin).then_inc(trig_done, 1)
                memory_keys(3)
                for i in range(NT):
                    job = Job("mv", i)
                    copy(job, mv[:, i, :], job.bank)
                for n, (kind, at) in enumerate(MIX_TILES):
                    if 1 <= n < len(AB_UNITS) - HIGHS + 1:
                        high_part(act_, AB_UNITS[n + HIGHS - 1])
                    job = Job(kind, at)
                    if kind == "u":
                        copy(job, usb[:, at % 2, :], job.bank[:, 0:SEQ])
                    elif (kind, at) in ROPED:
                        copy(job, rope_in[:, ROPED.index((kind, at)), :], job.bank[:, 0:SEQ])
                    elif kind == "qm":
                        copy(job, qmT[:, at, :], job.bank[:, 0:SEQ])
                for i in range(NT):
                    job = Job("tok", i)
                    job.wait_full(act_)
                    own(act_.activation(vtok[:, i, :], job.bank[:, 0:2 * P], ACT.Copy))
                    copy(job, gate[:, i, :], job.bank[:, 2 * P:2 * P + 24], ACT.Sigmoid)
                for m in range(2):
                    job = Job("hid", 0, m)
                    copy(job, hk[:, m, :], job.bank[:, 0:2 * NCMP], ACT.Gelu_apprx_tanh, bias=A("b1k")[:, m:m + 1])
                for u in GATE_UNITS[:3]:
                    high_part(act_, u)
                for m in range(2):
                    job = Job("hid", 1, m)
                    job.wait_full(act_)
                    for g in range(2):
                        ins = act_.activation(hv[:, m, g, :, 0:NCMP],
                                              bc(job.bank[:, g * NCMP:(g + 1) * NCMP], 1, 4),
                                              ACT.Gelu_apprx_tanh, bias=A("b1v")[:, m:m + 1])
                        if g == 1:
                            ins.then_inc(job.free, 1)
                job = Job("cmp_kv")
                job.wait_full(act_)
                own(act_.activation(kcT, job.bank[:, 0:NCMP], ACT.Copy))
                copy(job, vc, job.bank[:, HD:3 * HD].rearrange("p (g d) -> p g d", g=2))
                act_.wait_ge(cmp_sub, lay[0] + 1)
                act_.activation(cs, cs, ACT.Exp, scale=SCALE).then_inc(cmp_exp, 1)

                def gates(s):
                    for n in gates_at(s):
                        if n + 3 < N_GATE:
                            high_part(act_, GATE_UNITS[n + 3])
                        job = Job("gate", *divmod(n, 3))
                        copy(job, sg[:, n, :], job.bank[:, 0:SEQ], ACT.Sigmoid)
                    if s == 1:
                        job = Job("cmp_PT")
                        copy(job, PcT, job.bank.rearrange("p (g t) -> p g t", g=2))

                    if s in Y_STEPS:
                        branch_high(Y_STEPS.index(s))
                    if s >= len(MIX_UNITS):
                        high_part(act_, BRANCH_UNITS[s - len(MIX_UNITS)])

                def branch_high(g):
                    a, b = Y_GROUPS[g]
                    if g == 0:
                        Job("PV", "mix", 3).wait_full(act_)
                        Job("bg", 3).wait_emptied(act_)
                    elif g == 1:
                        all_emptied(act_, [("PV", "mix", u) for u in range(4)])
                    else:
                        all_emptied(act_, [("PV", "mix", 4 + 2 * (g - 2) + u) for u in range(2)])
                    act_.activation(yH[:, a:b, :], y_whole[:, a:b, :], ACT.Copy).then_inc(yH_ready, 1)

                attention("mix", MIX_UNITS, gates)
                for n in range(2):
                    branch_high(4 + n)
                    high_part(act_, BRANCH_UNITS[2 + n])
                table(ACT.Sqrt)
                for u in BRANCH_UNITS[PLACES:]:
                    high_part(act_, u)
                act_.wait_ge(merged, KD * lay[0] + KD)
                split(U_FFN2, 0, AHEAD)
                for i in range(NT):
                    post("mixed", 1.0, [i])
                    norm(k + 1, tiles=[i])

            act_.wait_ge(x_ready, 2)
            table(ACT.Sqrt)
            act_.wait_ge(mem_here, 16)
            norm(0, xs)
            act_.activation(small[:, 14:15], eps, ACT.Copy).then_inc(h_room, HIGHS - 1)
            act_.wait_ge(xs_ready, NT)
            act_.wait_ge(x_here, 16)
            norm(1)
            split(U_FFN1, 0, AHEAD)

            def body():
                ffn(0, 1 + 3 * lay[0])
                mixer(2 + 3 * lay[0])
                ffn(1, 3 + 3 * lay[0])

            layers(act_, body, own)

            act_.wait_ge(par2_in, 16)
            norm_parts("even")
            split(U_EA, AHEAD, HIGHS)
            act_.wait_ge(conv_done, 1)

            def convolved(t):
                act_.wait_ge(conv_done, t + 2)
                act_.activation(xbcT[:, t, :], cv[:, t % 2, :], ACT.Silu, bias=A2("cb")[:, t:t + 1])\
                    .then_inc(conv_act, 1)

            for t in range(16):
                if 1 <= t < N_EA - HIGHS + 1:
                    high_part(act_, U_EA + t + HIGHS - 1)
                job = Job("xbc", t)
                copy(job, xp[:, t % 2, 3:3 + SEQ], job.bank[:, 0:SEQ])
                if t >= 1:
                    convolved(t - 1)
            convolved(15)
            for t in range(4):
                job = Job("eg", t)
                copy(job, egT[:, t, :], job.bank[:, 0:SEQ], ACT.Silu)
            split(U_EB, 0, 3)
            for n in range(4):
                i, half = n // 2, n % 2
                job = Job("xs", n)
                copy(job, xtok[:, i, half * 512:(half + 1) * 512], job.bank)

            def qk_roots(n, heads):
                act_.wait_ge(qk_var, n)
                v = stat[:, 1, 0:4 * heads]
                act_.activation(stat[:, 2, 0:4 * heads], v, ACT.Sqrt).then_inc(qk_std, 1)

            for c in range(11):
                split(U_EB, 4 * c + 3 if c == 0 else 4 * c + 4, min(4 * c + 8, N_EB))
                for i in range(NT):
                    job = Job("eb", c, i)
                    if c < 6:
                        copy(job, QK[:, c // 3, i, c % 3 * 512:(c % 3 + 1) * 512], job.bank)
                    elif c < 9:
                        copy(job, V[:, i, (c - 6) * 512:(c - 5) * 512], job.bank)
                    else:
                        copy(job, Z[:, i, (c - 9) * 512:(c - 8) * 512], job.bank, ACT.Silu)
                if c == 8:
                    qk_roots(1, DIL_H)
            dt3 = dts[:, :, :].rearrange("p k (i h) -> p k i h", i=NT)
            for i in range(NT):
                job = Job("dt", i)
                copy(job, dt3[:, 0, i, :], job.bank[:, 0:SSD_H])
            own(act_.activation(neg_a, A2("alog"), ACT.Exp))
            act_.wait_ge(dt_abs, 1)
            act_.activation(dts[:, 2, :], dts[:, 2, :], ACT.Exp, scale=-1.0).then_inc(dt_exp, 1)
            for n in range(12):
                job = Job("qkT", "dil", n)
                copy(job, qkT[:, 2 * n:2 * n + 2, :], job.bank.rearrange("p (t s) -> p t s", t=2))
            job = Job("acs")
            copy(job, dts[:, 2, :], job.bank[:, 0:2 * SSD_H])
            job = Job("acsT")
            copy(job, acsT[0:SSD_H, :], job.bank[0:SSD_H, 0:SEQ])
            for n in range(8):
                act_.wait_ge(decay_in, n + 1)
                e = ebuf[:, n % 2]
                act_.activation(e, e, ACT.Exp).then_inc(decay_exp, 1)

            def y_root(s):
                if s == 8:
                    act_.wait_ge(y_sq, 1)
                    act_.activation(stat[:, 1, 0:8], stat[:, 0, 0:8], ACT.Sqrt, bias=eps, scale=1.0 / 256)\
                        .then_inc(y_std, 1)

            attention("dil", EVEN_UNITS, y_root)
            table(ACT.Sqrt)

            norm(8, after="even_out", tiles=[0])
            split(U_OB, 0, AHEAD)
            norm(8, after="even_out", tiles=[1])
            norm_parts("odd")
            for c in range(6):
                split(U_OB, AHEAD if c == 0 else 4 * c + 4, min(4 * c + 8, N_OB + 4))
                for i in range(NT):
                    job = Job("ob", c, i)
                    dst = QK[:, c // 2, i] if c < 4 else V[:, i, :]
                    copy(job, dst[:, c % 2 * 512:(c % 2 + 1) * 512], job.bank)
            qk_roots(2, MOBA_H)
            for t in range(8):
                if t + 4 < N_OA:
                    high_part(act_, U_OA + t + 4)
                job = Job("og", t)
                copy(job, ogT[:, t, :], job.bank[:, 0:SEQ], ACT.Silu)
            for n in range(8):
                job = Job("qkT", "moba", n)
                copy(job, qkT[:, 2 * n:2 * n + 2, :], job.bank.rearrange("p (t s) -> p t s", t=2))
            attention("moba", ODD_UNITS)

        @block.vector
        def _(dve):
            lay[0] = 0
            own = Own(dve, sem("dve_own"), DVE_OWN)

            def scaled(i, k, source=x):
                dve.wait_ge(std_ready, NT * k + i + 1)
                own(dve.reciprocal(rstd[:, i:i + 1], std[:, i:i + 1]))
                own.settle()
                dve.tensor_scalar(xs[:, i, :], source[:, i, :], rstd[:, i:i + 1], None, ALU.mult)\
                    .then_inc(xs_ready, 1)

            def norm(name, k, gain, dst=None, scale_last=False):
                def turned(i, half):
                    job = Job("norm", name, i, half)
                    job.wait_full(dve)
                    if dst is None:
                        to = h_whole[:, i, 4 * half:4 * half + 4, :]
                    else:
                        to = dst[:, 4 * half:4 * half + 4, i * P:(i + 1) * P]
                    tiles = job.bank.rearrange("p (k t) -> p k t", k=4)
                    if gain is None:
                        ins = dve.tensor_copy(to, tiles)
                    else:
                        ins = dve.tensor_tensor(to, tiles, bc(gain[:, 4 * half:4 * half + 4], 2, P), ALU.mult)
                    ins.then_inc(job.free, 1)

                def low(i, half):
                    if dst is not None:
                        return
                    dve.wait_ge(nH_ready, 4 * (k - 1) + 2 * i + half + 1)
                    ks = slice(4 * half, 4 * half + 4)
                    dve.tensor_tensor(hL[:, i, ks, :], h_whole[:, i, ks, :], hH[:, i, ks, :].bitcast(F32),
                                      ALU.subtract).then_inc(nL_ready, 1)

                turned(0, 0)
                turned(0, 1)
                if scale_last:
                    scaled(1, k)
                low(0, 0)
                turned(1, 0)
                low(0, 1)
                turned(1, 1)
                low(1, 0)
                low(1, 1)

            def split(first, lo, hi):
                for u in range(first + lo, first + hi):
                    low_part(dve, u)

            def post(name, p, slot, loads, tiles=range(NT)):
                dve.wait_ge(gp_full[slot], 16 * loads)
                for i in tiles:
                    dve.wait_ge(post_std, NT * p + i + 1)
                    own(dve.reciprocal(prstd[:, i:i + 1], pstd[:, i:i + 1]))
                    own.settle()
                    jobs = [Job(name, 2 * i + half) for half in range(2)]
                    for half, job in enumerate(jobs):
                        cols = slice(half * 512, (half + 1) * 512)
                        dve.scalar_tensor_tensor(xs[:, i, cols], job.bank, prstd[:, i:i + 1], gpost[:, slot, cols],
                                                 ALU.mult, ALU.mult).then_inc(job.free, 1)
                    for job in jobs:
                        job.wait_emptied(dve)
                    dve.tensor_tensor(x[:, i, :], x[:, i, :], xs[:, i, :], ALU.add).then_inc(x_ready, 1)

            def ffn(f, k, gain):
                norm(("ffn", f), k, gain, scale_last=f == 1)
                first = U_FFN2 if f else U_FFN1
                split(first, AHEAD, HIGHS)
                if f == 0:
                    dve.tensor_tensor(hmT, memT, bc(A("gmem"), 2, SEQ), ALU.mult).then_inc(hm_ready, 1)

                def gated(t, it=0):
                    job = Job("ff", f, t, plus=2 * it)
                    before = lay[0] * (2 * FT) + it * SLOTS + (f * FT + t)
                    dve.wait_ge(sil_ready, before + 1)
                    g = gT[:, t % 2, :]
                    dve.tensor_tensor(g, sil[:, t % 2, :], job.bank[:, SEQ:2 * SEQ], ALU.mult).then_inc(g_steps, 1)
                    dve.wait_ge(g_steps, 2 * before + 1)
                    dve.tensor_copy(gH[:, t % 2, :], g).then_inc(g_steps, 1)
                    dve.wait_ge(g_steps, 2 * before + 2)
                    dve.tensor_tensor(gL[:, t % 2, :], g, gH[:, t % 2, :].bitcast(F32), ALU.subtract)\
                        .then_inc(job.free, 1)

                def body(it):
                    for c in range(SLOTS):
                        gated(c, it)
                        for n in range(3):
                            low_part(dve, first + HIGHS + 3 * c + n, it)

                repeat(dve, (FT - 2) // SLOTS, body)
                gated(FT - 2)
                gated(FT - 1)
                if f == 1:
                    split(3 * LAYER_CHUNKS, 0, AHEAD)

            def attention(tag, units, evacuate, extra=None):
                base = unit_base(tag)

                def front(s):
                    kind = units[s][0]
                    S_, m = scores_of(kind, s), mx3[:, s % 2, :]
                    n = SCORE_BUFFERS
                    if s >= n:
                        Job("PT", tag, s - n, BRANCHES[units[s - n][0]] - 1).wait_full(dve)
                    for b in range(BRANCHES[kind]):
                        job = Job("S", tag, s, b)
                        job.wait_full(dve)
                        if kind == "mem":
                            own(dve.tensor_reduce(m[:, 0:2], job.bank.rearrange("p (i n) -> p i n", i=NT), AX.X, ALU.max))
                            dve.tensor_copy(S_[:, 0:512], job.bank).then_inc(job.free, 1)
                            continue
                        own(dve.memset(small[:, 64 + 2 * s + b % 2:65 + 2 * s + b % 2], 0.0))
                        mask = C(f"dil{b}") if kind == "dil" else C("causal")
                        if kind == "dil":
                            to, at = [(b * P, P), (384 + b * SEQ, SEQ)], (b, 3 + b)
                        else:
                            to, at = [(b * 384, P), (b * 384 + P, SEQ)], (2 * b, 2 * b + 1)
                        for i, ((o, n), c) in enumerate(zip(to, at)):
                            src = i * P
                            ins = dve.tensor_tensor_reduce(S_[:, o:o + n], job.bank[:, src:src + n], mask[:, src:src + n],
                                                           1.0, NEG, ALU.add, ALU.max, m[:, c:c + 1])
                            if i:
                                ins.then_inc(job.free, 1)
                            else:
                                own(ins)
                    job.wait_emptied(dve)
                    if kind == "dil":
                        own(dve.tensor_reduce(m[:, 0:2], m[:, 0:6].rearrange("p (i b) -> p i b", i=NT), AX.X, ALU.max))
                        own.settle()
                    n = len(probs_of(kind, s))
                    dve.tensor_scalar(nmx[:, s % 2, 0:n], m[:, 0:n], -(SCALE_MEM if kind == "mem" else SCALE), None,
                                      ALU.mult).then_inc(mx_ready, 1)

                def back(s):
                    kind, a, g = units[s]
                    dve.wait_ge(exp_done, base + s + 1)
                    todo = probs_of(kind, s)
                    r = rs[:, s % 2, 0:len(todo)]
                    own(dve.reciprocal(r, sm[:, s % 2, 0:len(todo)]))
                    own.settle()
                    if kind == "nsa":
                        h = 4 * g + a
                        w = gate[:, :, 3 * h + 1:3 * h + 3].rearrange("p i b -> p b i")
                        own(dve.tensor_tensor(r.rearrange("p (b i) -> p b i", b=2), r.rearrange("p (b i) -> p b i", b=2),
                                              w, ALU.mult))
                        own.settle()
                    for n, ((u, v), c) in enumerate(todo):
                        p = scores_of(kind, s)[:, u:v]
                        ins = dve.tensor_scalar(p, p, r[:, c:c + 1], None, ALU.mult)
                        if n == len(todo) - 1:
                            ins.then_inc(p_ready, 1)

                def collect(s):
                    job = Job("PV", tag, s)
                    job.wait_full(dve)
                    evacuate(units[s], job, out_half(units[s]))

                behind = LAG[tag] + 2
                for s in range(len(units) + behind):
                    if s < len(units):
                        front(s)
                    if 1 <= s <= len(units):
                        back(s - 1)
                    if extra is not None:
                        extra(s)
                    if s >= behind:
                        collect(s - behind)

            def mixer(k, p):
                for i in range(NT):
                    scaled(i, k)
                norm("mix", k, A("gm"))
                dve.wait_ge(const_in, 16)
                dve.wait_ge(trig_done, lay[0] + 1)
                for u in AB_UNITS[:HIGHS]:
                    low_part(dve, u)
                own(dve.memset(cu[:, :, 0:2], 0.0))
                pending = []

                def rotated():
                    if not pending:
                        return
                    kind, at = pending.pop(0)
                    r = ROPED.index((kind, at))
                    job = Job("rot", kind, at)
                    Job(kind, at).wait_emptied(dve)
                    own(dve.tensor_tensor(rt[:, r % 2, 0, :], rope_in[:, r, :], cosT, ALU.mult))
                    job.wait_full(dve)
                    dve.tensor_tensor(rt[:, r % 2, 1, :], job.bank[:, 0:SEQ], sinT, ALU.mult).then_inc(job.free, 1)
                    own.settle()
                    job.wait_emptied(dve)
                    dve.tensor_tensor(rope_out[:, r, :], rt[:, r % 2, 0, :], rt[:, r % 2, 1, :], ALU.add)\
                        .then_inc(rope_ready, 1)

                for n, (kind, at) in enumerate(MIX_TILES):
                    if 1 <= n < len(AB_UNITS) - HIGHS + 1:
                        low_part(dve, AB_UNITS[n + HIGHS - 1])
                    job = Job(kind, at)
                    if kind == "cg":
                        c_, v_ = cu[:, at % 2, :], cacc[:, at % 2, :]
                        w = A("convw")[:, 3 * at:3 * at + 3]
                        Job("u", at).wait_emptied(dve)
                        job.wait_full(dve)
                        dve.tensor_tensor(c_[:, 2:2 + SEQ], job.bank[:, 0:SEQ], usb[:, at % 2, :], ALU.mult)\
                            .then_inc(job.free, 1)
                        job.wait_emptied(dve)
                        own(dve.tensor_scalar(v_, c_[:, 0:SEQ], w[:, 0:1], None, ALU.mult))
                        for t in (1, 2):
                            own.settle()
                            own(dve.scalar_tensor_tensor(v_, c_[:, t:t + SEQ], w[:, t:t + 1], v_, ALU.mult, ALU.add))
                    elif kind == "bg":
                        job.wait_full(dve)
                        own.settle()
                        dve.tensor_tensor(yconvT[:, at, :], job.bank[:, 0:SEQ], cacc[:, at % 2, :], ALU.mult)\
                            .then_inc(job.free, 1)
                    elif kind in ("kc", "vc"):
                        c = 0 if kind == "kc" else 1
                        pos = A("posk" if c == 0 else "posv")
                        job.wait_full(dve)
                        for odd in range(2):
                            rows = slice(odd * HD, (odd + 1) * HD)
                            tokens = job.bank[rows, 0:SEQ].rearrange("p (n j two) -> p two j n", j=8, two=2)[:, odd]
                            for jh in range(2):
                                ins = dve.tensor_tensor(flat[rows, c, 8 * jh:8 * jh + 8, at, :],
                                                        tokens[:, :, jh:jh + NCMP],
                                                        bc(pos[rows, 8 * jh:8 * jh + 8], 2, NCMP), ALU.add)
                                if odd and jh:
                                    ins.then_inc(job.free, 1)
                    rotated()
                    if (kind, at) in ROPED:
                        pending.append((kind, at))
                add = C("cmp_add").rearrange("p (i n) -> p i n", i=NT)
                one = C("cmp_one").rearrange("p (i n) -> p i n", i=NT)
                for g in range(2):
                    job = Job("cmp_S", g)
                    job.wait_full(dve)
                    s4 = job.bank[:, 0:NT * 4 * NCMP].rearrange("p (i h n) -> p i h n", i=NT, h=4)
                    for i in range(NT):
                        ins = dve.tensor_tensor(cs[:, i, 4 * g:4 * g + 4], s4[:, i], bc(add[:, i], 1, 4), ALU.add)
                        if i:
                            ins.then_inc(job.free, 1)
                    job.wait_emptied(dve)
                flat_cs = cs.rearrange("p i h n -> p (i h) n")
                own(dve.tensor_reduce(cstat[:, 0, :], flat_cs, AX.X, ALU.max))
                own.settle()
                dve.tensor_tensor(flat_cs, flat_cs, bc(cstat[:, 0, :], 2, NCMP), ALU.subtract).then_inc(cmp_sub, 1)
                dve.wait_ge(cmp_exp, lay[0] + 1)
                for i in range(NT):
                    own(dve.tensor_tensor(cs[:, i], cs[:, i], bc(one[:, i], 1, NHEAD), ALU.mult))
                own.settle()
                own(dve.tensor_reduce(cstat[:, 1, :], flat_cs, AX.X, ALU.add))
                own.settle()
                own(dve.tensor_scalar(cstat[:, 1, :], cstat[:, 1, :], 1e-30, None, ALU.max))
                own.settle()
                own(dve.reciprocal(cstat[:, 2, :], cstat[:, 1, :]))
                own.settle()
                g0 = gate.rearrange("p i (h b) -> p i h b", b=3)[:, :, :, 0]
                c3 = cstat[:, 3, :].rearrange("p (i h) -> p i h", i=NT)
                own(dve.tensor_tensor(c3, cstat[:, 2, :].rearrange("p (i h) -> p i h", i=NT), g0, ALU.mult))
                own.settle()
                for i in range(NT):
                    ins = dve.tensor_tensor(Pc[:, i, :, 0:NCMP], cs[:, i], bc(c3[:, i], 2, NCMP), ALU.mult)
                    if i:
                        ins.then_inc(cmp_p, 1)
                    else:
                        own(ins)

                def evacuate(unit, job, rows):
                    kind, a, g = unit
                    y = ymemT if kind == "mem" else ynsaT
                    dve.tensor_copy(y[rows, a, :], job.bank[rows, 0:SEQ]).then_inc(job.free, 1)

                def branch_low(g):
                    a, b = Y_GROUPS[g]
                    dve.wait_ge(yH_ready, len(Y_GROUPS) * lay[0] + g + 1)
                    dve.tensor_tensor(yL[:, a:b, :], y_whole[:, a:b, :], yH[:, a:b, :].bitcast(F32), ALU.subtract)\
                        .then_inc(yL_ready, 1)

                def lows(s):
                    if s - 1 in Y_STEPS:
                        branch_low(Y_STEPS.index(s - 1))

                attention("mix", MIX_UNITS, evacuate, lows)
                for g in (4, 5):
                    branch_low(g)
                for m in range(KD):
                    for b in range(3):
                        job = Job("branch", m, b)
                        job.wait_full(dve)
                        Job("gate", m, b).wait_emptied(dve)
                        dst = mergedT[:, m, :] if b == 0 else mt[:, b - 1, :]
                        dve.tensor_tensor(dst, job.bank[:, 0:SEQ], sg[:, 3 * m + b, :], ALU.mult).then_inc(job.free, 1)
                        job.wait_emptied(dve)
                        if b:
                            ins = dve.tensor_tensor(mergedT[:, m, :], mergedT[:, m, :], mt[:, b - 1, :], ALU.add)
                            if b == 2:
                                ins.then_inc(merged, 1)
                            else:
                                own(ins)
                                own.settle()
                split(U_FFN2, 0, AHEAD)
                for i in range(NT):
                    post("mixed", p, 1, lay[0] + 1, [i])
                    if i == 0:
                        scaled(0, k + 1)

            dve.memset(eps, EPS).then_inc(x_ready, 1)
            for b in range(8):
                dve.memset(small[:, 56 + b:57 + b], 0.0).then_inc(free[b], 1)
            dve.memset(eps4, 4 * EPS).then_inc(x_ready, 1)
            for i in range(NT):
                scaled(i, 0, xs)
            norm("mem", 0, None, memT)
            dve.wait_ge(x_here, 16)
            for i in range(NT):
                scaled(i, 1)
            split(U_FFN1, 0, AHEAD)
            dve.wait_ge(par_in, 16)
            n_par = par_at["w2v"][1]

            def body():
                own.settle()
                own(dve.tensor_copy(pl[:, :], pars[:, bass.ds(lay[0] * n_par, n_par)]))
                own.settle()
                ffn(0, 1 + 3 * lay[0], A("g1"))
                post(("ffn_out", 0), 3 * lay[0], 0, 2 * lay[0] + 1)
                mixer(2 + 3 * lay[0], 3 * lay[0] + 1)
                ffn(1, 3 + 3 * lay[0], A("g2"))
                post(("ffn_out", 1), 3 * lay[0] + 2, 0, 2 * lay[0] + 2)
                for i in range(NT):
                    scaled(i, 4 + 3 * lay[0])

            layers(dve, body, own)

            dve.wait_ge(par2_in, 16)
            norm("even", 7, A2("ge"))
            dve.memset(xp[:, :, 0:3], 0.0).then_inc(conv_done, 1)
            for t in range(16):
                w = A2("cw")[:, 4 * t:4 * t + 4]
                c_, v_ = xp[:, t % 2, :], cv[:, t % 2, :]
                Job("xbc", t).wait_emptied(dve)
                if t >= 2:
                    dve.wait_ge(conv_act, t - 1)
                own(dve.tensor_scalar(v_, c_[:, 0:SEQ], w[:, 0:1], None, ALU.mult))
                for j in (1, 2, 3):
                    own.settle()
                    ins = dve.scalar_tensor_tensor(v_, c_[:, j:j + SEQ], w[:, j:j + 1], v_, ALU.mult, ALU.add)
                    if j == 3:
                        ins.then_inc(conv_done, 1)
                    else:
                        own(ins)

            def heads_normed(n, heads, copied, gains, pieces):
                width = heads * HD
                view = [[QK[:, qk, i, 0:width].rearrange("p (h d) -> p h d", h=heads) for i in range(NT)]
                        for qk in range(2)]
                sq = Sflat[:, 0:width]
                sums = stat[:, 0, 0:4 * heads]
                for qk in range(2):
                    for i in range(NT):
                        copied(qk, i)
                        own.settle()
                        own(dve.tensor_tensor(sq, QK[:, qk, i, 0:width], QK[:, qk, i, 0:width], ALU.mult))
                        own.settle()
                        at = (2 * qk + i) * heads
                        own(dve.tensor_reduce(sums[:, at:at + heads], sq.rearrange("p (h d) -> p h d", h=heads),
                                              AX.X, ALU.add))
                own.settle()
                v, root, r = (stat[:, j, 0:4 * heads] for j in (1, 2, 3))
                dve.tensor_scalar(v, sums, 1.0 / HD, EPS, ALU.mult, ALU.add).then_inc(qk_var, 1)
                dve.wait_ge(qk_std, n)
                own(dve.reciprocal(r, root))
                own.settle()
                own(dve.tensor_tensor(sums, r, r, ALU.mult))
                own.settle()
                own(dve.tensor_tensor(sums, sums, v, ALU.mult))
                own.settle()
                own(dve.tensor_scalar(sums, sums, -0.5, 1.5, ALU.mult, ALU.add))
                own.settle()
                own(dve.tensor_tensor(r, r, sums, ALU.mult))
                own.settle()
                cos2 = C("cos2").rearrange("p (i d) -> p i d", i=NT)
                sin2 = C("sin2").rearrange("p (i d) -> p i d", i=NT)
                t_ = Sflat[:, 0:4 * heads * ROT].rearrange("p (k h d) -> p k h d", k=4, h=heads)
                for qk in range(2):
                    for i in range(NT):
                        w = view[qk][i]
                        at = (2 * qk + i) * heads
                        own(dve.tensor_tensor(w, w, bc(r[:, at:at + heads], 2, HD), ALU.mult))
                        own.settle()
                        own(dve.tensor_tensor(w, w, bc(gains[qk], 1, heads), ALU.mult))
                        own.settle()
                        a, b = w[:, :, 0:ROT], w[:, :, ROT:2 * ROT]
                        c, s = bc(cos2[:, i], 1, heads), bc(sin2[:, i], 1, heads)
                        for j, (u, z) in enumerate(((a, c), (b, s), (b, c), (a, s))):
                            own(dve.tensor_tensor(t_[:, j], u, z, ALU.mult))
                        own.settle()
                        own(dve.tensor_tensor(a, t_[:, 0], t_[:, 1], ALU.subtract))
                        dve.tensor_tensor(b, t_[:, 2], t_[:, 3], ALU.add).then_inc(qk_ready, 1)
                        dve.wait_ge(qk_ready, 4 * (n - 1) + 2 * qk + i + 1)

            def even_copied(qk, i):
                for c in range(3):
                    Job("eb", 3 * qk + c, i).wait_emptied(dve)

            heads_normed(1, DIL_H, even_copied, (A2("qn_dil"), A2("kn_dil")), 3)
            dt3 = dts[:, :, :].rearrange("p k (i h) -> p k i h", i=NT)
            for i in range(NT):
                Job("dt", i).wait_emptied(dve)
            own(dve.tensor_tensor(dt3[:, 0], dt3[:, 0], bc(A2("dtb"), 1, NT), ALU.add))
            own.settle()
            own(dve.tensor_scalar(dts[:, 1, :], dts[:, 0, :], 0.0, None, ALU.max))
            own(dve.tensor_scalar(dts[:, 3, :], dts[:, 0, :], -1.0, None, ALU.mult))
            own.settle()
            dve.tensor_tensor(dts[:, 2, :], dts[:, 0, :], dts[:, 3, :], ALU.max).then_inc(dt_abs, 1)
            dve.wait_ge(dt_exp, 1)
            own(dve.tensor_scalar(dts[:, 3, :], dts[:, 2, :], 2.0, None, ALU.add))
            own.settle()
            own(dve.reciprocal(dts[:, 4, :], dts[:, 3, :]))
            own.settle()
            own(dve.tensor_tensor(dts[:, 3, :], dts[:, 2, :], dts[:, 4, :], ALU.mult))
            own.settle()
            own(dve.tensor_tensor(dts[:, 4, :], dts[:, 3, :], dts[:, 3, :], ALU.mult))
            own.settle()
            own(dve.tensor_scalar(dts[:, 5, :], dts[:, 4, :], 1.0 / 17, None, ALU.mult))
            for odd in (15, 13, 11, 9, 7, 5, 3):
                own.settle()
                own(dve.scalar_tensor_tensor(dts[:, 5, :], dts[:, 5, :], 1.0 / odd, dts[:, 4, :], ALU.add, ALU.mult))
            own.settle()
            own(dve.scalar_tensor_tensor(dts[:, 5, :], dts[:, 5, :], 1.0, dts[:, 3, :], ALU.add, ALU.mult))
            own.settle()
            own(dve.scalar_tensor_tensor(dts[:, 6, :], dts[:, 5, :], 2.0, dts[:, 1, :], ALU.mult, ALU.add))
            own(dve.tensor_scalar(neg_a, neg_a, -1.0, None, ALU.mult))
            own.settle()
            dve.tensor_tensor(dt3[:, 7], dt3[:, 6], bc(neg_a, 1, NT), ALU.mult).then_inc(a_ready, 1)
            all_emptied(dve, [("xs", n) for n in range(4)])
            for i in range(NT):
                ins = dve.tensor_tensor(xs[:, i, :].rearrange("p (h d) -> p h d", h=SSD_H),
                                        xtok[:, i, :].rearrange("p (h d) -> p h d", h=SSD_H),
                                        bc(dt3[:, 6, i], 2, HD), ALU.mult)
                if i:
                    ins.then_inc(xdt_ready, 1)
            for g in range(4):
                job = Job("cb", g)
                job.wait_full(dve)
                dve.tensor_tensor(cbm[:, g, :], job.bank[:, 0:384], C("reach"), ALU.mult).then_inc(job.free, 1)
            Job("acs").wait_emptied(dve)
            acs = dts[:, 2, :]
            for n in range(9):
                if n >= 1:
                    dve.wait_ge(decay_exp, n)
                    e = ebuf[:, (n - 1) % 2]
                    dve.tensor_tensor(e, e, bc(cbm[:, (n - 1) // 2, :], 1, 2), ALU.mult).then_inc(decay_done, 1)
                if n < 8:
                    job = Job("decay", n)
                    job.wait_full(dve)
                    for hh in range(2):
                        h = 2 * n + hh
                        for i in range(NT):
                            e = ebuf[:, n % 2, hh, 0:SEQ] if i == 0 else ebuf[:, n % 2, hh, SEQ:384]
                            ins = dve.tensor_scalar(e, job.bank[:, hh * SEQ + i * P:(hh + 1) * SEQ],
                                                    acs[:, i * SSD_H + h:i * SSD_H + h + 1], 0.0,
                                                    ALU.subtract, ALU.min)
                            if hh and i:
                                ins.then_inc(job.free, 1)
                            else:
                                own(ins)
                    job.wait_emptied(dve)
                    dve.memset(small[:, 52:53], 0.0).then_inc(decay_in, 1)

            def even_out(unit, job, rows):
                _, h, _ = unit
                dve.tensor_tensor(mixedT[rows, 8 + h // 2, :], job.bank[rows, 0:SEQ], egT[rows, h // 2, :],
                                  ALU.mult).then_inc(job.free, 1)

            for i in range(NT):
                own(dve.tensor_tensor(yt[:, i, :].rearrange("p (h d) -> p h d", h=SSD_H),
                                      xtok[:, i, :].rearrange("p (h d) -> p h d", h=SSD_H),
                                      bc(A2("dskip"), 2, HD), ALU.mult))
            own.settle()
            for i in range(NT):
                for half in range(2):
                    job = Job("scan", 2 * i + half)
                    cols = slice(half * 512, (half + 1) * 512)
                    job.wait_full(dve)
                    dve.tensor_tensor(ysb[:, i, cols], job.bank, yt[:, i, cols], ALU.add).then_inc(job.free, 1)
                    job.wait_emptied(dve)
            y8 = ysb.rearrange("p i (g d) -> p (i g) d", g=4)

            def y_steps(s):
                if s in (1, 2):
                    own(dve.tensor_tensor(ysb[:, s - 1], ysb[:, s - 1], Z[:, s - 1, :], ALU.mult))
                elif s in (3, 4):
                    own.settle()
                    own(dve.tensor_tensor(yt[:, s - 3], ysb[:, s - 3], ysb[:, s - 3], ALU.mult))
                elif s == 5:
                    own.settle()
                    dve.tensor_reduce(stat[:, 0, 0:8], yt.rearrange("p i (g d) -> p (i g) d", g=4), AX.X, ALU.add)\
                        .then_inc(y_sq, 1)
                elif s == 9:
                    dve.wait_ge(y_std, 1)
                    own(dve.reciprocal(stat[:, 2, 0:8], stat[:, 1, 0:8]))
                elif s == 10:
                    own.settle()
                    dve.tensor_tensor(y8, y8, bc(stat[:, 2, 0:8], 2, 256), ALU.mult).then_inc(y_ready, 1)

            attention("dil", EVEN_UNITS, even_out, y_steps)
            for n in range(4):
                i, half = n // 2, n % 2
                job = Job("yT", n)
                job.wait_full(dve)
                dve.tensor_tensor(mixedT[:, 4 * half:4 * half + 4, i * P:(i + 1) * P],
                                  job.bank.rearrange("p (k t) -> p k t", k=4),
                                  bc(A2("gssd")[:, 4 * half:4 * half + 4], 2, P), ALU.mult).then_inc(job.free, 1)

            def residual(name, banks=range(4)):
                for j in banks:
                    job = Job(name, j)
                    job.wait_full(dve)
                    to = x[:, j // 2, j % 2 * 512:(j % 2 + 1) * 512]
                    dve.tensor_tensor(to, to, job.bank, ALU.add).then_inc(job.free, 1)

            residual("even_out", [0, 1])
            for j in (0, 1):
                Job("even_out", j).wait_emptied(dve)
            scaled(0, 8)
            residual("even_out", [2, 3])

            for j in (2, 3):
                Job("even_out", j).wait_emptied(dve)
            norm("odd", 8, A2("go"), scale_last=True)

            def odd_copied(qk, i):
                for c in range(2):
                    Job("ob", 2 * qk + c, i).wait_emptied(dve)

            heads_normed(2, MOBA_H, odd_copied, (A2("qn_moba"), A2("kn_moba")), 2)

            def odd_out(unit, job, rows):
                _, h, _ = unit
                dve.tensor_tensor(mixedT[rows, h // 2, :], job.bank[rows, 0:SEQ], ogT[rows, h // 2, :],
                                  ALU.mult).then_inc(job.free, 1)

            attention("moba", ODD_UNITS, odd_out)
            residual("odd_out")


def constants():
    token = np.arange(SEQ)
    t, s = token[:, None], token[None, :]

    def blocks(ok):
        return np.concatenate([ok[:P, :P], ok[P:, :]], 1)

    def added(ok):
        return np.where(blocks(ok), 0.0, NEG)

    causal = s <= t
    c = {
        "ident": np.eye(P), "causal": added(causal), "dil0": added(causal & (t - s <= 128)),
        "dil1": added(causal & ((t - s) % 4 == 0)), "dil2": added(causal & ((t - s) % 16 == 0)),
    }
    reach = causal.T.astype(float)
    c["reach"] = np.concatenate([reach[:P, :], reach[P:, P:]], 1)
    ends = np.arange(NCMP) * 16 + 31
    seen = (ends[None, None, :] <= token.reshape(NT, P, 1)).transpose(1, 0, 2).reshape(P, -1)
    c["cmp_add"], c["cmp_one"] = np.where(seen, 0.0, NEG), seen
    c["upto"], c["ones"] = reach[:P, :P], np.ones((P, P))
    rotate = np.zeros((P, P))
    inv = np.zeros((P, 1))
    freq = THETA ** (-np.arange(ROT) * 2.0 / (2 * ROT))
    for base in (0, HD):
        for d in range(ROT):
            rotate[base + d + ROT, base + d] = -1.0
            rotate[base + d, base + d + ROT] = 1.0
            inv[base + d] = inv[base + d + ROT] = freq[d]
    c["rotate"], c["inv"] = rotate, inv
    angle = (token[:, None].astype(np.float32) * freq.astype(np.float32)).astype(np.float64)
    for name, f in (("cos2", np.cos), ("sin2", np.sin)):
        c[name] = f(angle).reshape(NT, P, ROT).transpose(1, 0, 2).reshape(P, -1)
    assert all(c[k].shape == (P, CONST[k]) for k in CONST)
    return np.concatenate([c[k] for k in CONST], 1).astype(np.float32)


def by_partition(v):
    return v.reshape(-1, P).T


def mtile(w, a, n=P):
    k = w.shape[0] // P
    return w[:, a:a + n].reshape(k, P, n).transpose(1, 0, 2).reshape(P, k * n)


def packed(rows):
    out = np.zeros((len(rows), P, CHUNK), np.float32)
    for c, pieces in enumerate(rows):
        at = 0
        for piece in pieces:
            out[c, :, at:at + piece.shape[1]] = piece
            at += piece.shape[1]
    return out


def groups(pieces, n):
    return [pieces[i:i + n] for i in range(0, len(pieces), n)]


def layer_chunks(v, l):
    def ffn(w_in, w_out):
        a, b = ([mtile(w_in, z + t * P) for t in range(FT)] for z in (0, FF))
        o = [w_out[t * P:(t + 1) * P] for t in range(FT)]
        tiles = [a[0], b[0], a[1], b[1], o[0]]
        for t in range(2, FT):
            tiles += [a[t], b[t], o[t - 1]]
        return groups(tiles + [o[-1]], 3)

    w = v["w_mix_in"][l]
    q0, kv0 = 3 * CONV, 3 * CONV + 512
    g0 = kv0 + 768
    qm0, mg0 = g0 + 24, g0 + 24 + 512

    def pick(columns):
        return mtile(w[:, columns], 0)

    def head_pair(a):
        return pick(np.r_[q0 + a * HD:q0 + (a + 1) * HD, q0 + (4 + a) * HD:q0 + (5 + a) * HD])

    def twice(c, g):
        at = kv0 + c * P + g * HD
        return pick(np.r_[at:at + HD, at:at + HD])

    tiles = [mtile(w, o * CONV + f * P) for f in range(CF) for o in (0, 2, 1)]
    tiles += [head_pair(a) for a in range(4)] + [mtile(w, kv0 + 2 * P), mtile(w, kv0 + 4 * P)]
    tiles += [twice(c, g) for c in range(2) for g in range(2)] + [mtile(w, qm0 + h * P) for h in range(4)]
    m = v["w_mem_kv"][l]
    mk = [mtile(m, h * P) for h in range(4)]
    mv = mtile(m, 512, 512)
    rows = [mk[:3], [mk[3], mv[:, :2048]], [mv[:, 2048:]]]
    rows += groups(tiles, 3)
    columns_b = np.r_[kv0 + 3 * P:kv0 + 4 * P, kv0 + 5 * P:kv0 + 6 * P, g0:g0 + 24]
    rows += [[mtile(w[:, columns_b], 0, 280)]]
    for name in ("cmp_k_w1", "cmp_v_w1"):
        t = mtile(v[name][l], 0, 256)
        rows += [[t[:, :2048]], [t[:, 2048:]]]
    rows += [[mtile(w, mg0 + b * D + t * P) for b in range(3)] for t in range(KD)]
    nsa = v["w_branch_nsa"][l].reshape(2, 4, HD, D).transpose(1, 0, 2, 3).reshape(512, D)
    branch = (v["w_branch_conv"][l], nsa, v["w_branch_mem"][l])
    rows += [[mtile(w_, t * P) for t in pair for w_ in branch] for pair in groups(list(range(KD)), 2)]
    rows += groups([v["w_mix_out"][l][k * P:(k + 1) * P] for k in range(KD)], 3)
    rows = ffn(v["ffn1_w_in"][l], v["ffn1_w_out"][l]) + rows + ffn(v["ffn2_w_in"][l], v["ffn2_w_out"][l])
    assert len(rows) == LAYER_CHUNKS
    return packed(rows)


def tail_chunks(v):
    w, o = v["even_w_in_2"][0], v["odd_w_in_2"][0]
    xbc0, dt0, q0 = D, 3 * D, 3 * D + SSD_H
    k0, v0, g0 = q0 + 1536, q0 + 3072, q0 + 4608
    rows = groups([mtile(w, xbc0 + t * P) for t in range(16)] + [mtile(w, g0 + t * P) for t in range(4)], 3)

    def blocks(w_, starts):
        return [w_[k * P:(k + 1) * P, a:a + 512] for a in starts for k in range(KD)]

    starts = [b + c * 512 for b in (q0, k0, v0) for c in range(3)] + [0, 512]
    last = groups(blocks(w, starts), 6)
    last[-1] = last[-1] + [mtile(w, dt0, SSD_H)]
    rows += last
    rows += groups([v["even_w_out_2"][0][k * P:(k + 1) * P] for k in range(12)], 3)
    rows += groups(blocks(o, [c * 512 for c in range(6)]), 6)
    rows += groups([mtile(o, 3 * D + t * P) for t in range(8)], 3)
    rows += groups([v["odd_w_out_2"][0][k * P:(k + 1) * P] for k in range(8)], 3)
    assert len(rows) == CHUNKS - DEPTH * LAYER_CHUNKS
    return packed(rows)


def layer_parameters(v, l):
    def positions(p):
        return p.reshape(16, 2, HD).transpose(1, 2, 0).reshape(P, 16)

    p = {
        "g1": by_partition(v["ffn1_norm_pre"][l]), "gm": by_partition(v["mix_norm_pre"][l]),
        "g2": by_partition(v["ffn2_norm_pre"][l]), "gmem": by_partition(v["mem_norm"][l]),
        "convw": v["conv_w"][l].reshape(3, CF, P).transpose(2, 1, 0).reshape(P, -1),
        "posk": positions(v["cmp_pos_k"][l]), "posv": positions(v["cmp_pos_v"][l]),
        "b1k": by_partition(v["cmp_k_b1"][l]), "b1v": by_partition(v["cmp_v_b1"][l]),
        "w2k": mtile(v["cmp_k_w2"][l], 0, HD), "w2v": mtile(v["cmp_v_w2"][l], 0, HD),
    }
    assert all(p[k].shape == (P, PARAM[k]) for k in PARAM)
    return np.concatenate([p[k] for k in PARAM], 1)


def tail_parameters(v):
    def everywhere(a):
        return np.broadcast_to(a, (P, a.size))

    p = {
        "ge": by_partition(v["even_norm_w_2"][0]), "go": by_partition(v["odd_norm_w_2"][0]),
        "gssd": by_partition(v["even_ssd_norm_w_2"][0]),
        "cw": v["even_conv_w_2"][0].reshape(16, P, 4).transpose(1, 0, 2).reshape(P, 64),
        "cb": by_partition(v["even_conv_b_2"][0]),
        "dtb": everywhere(v["even_dt_bias_2"][0]), "alog": everywhere(v["even_a_log_2"][0]),
        "dskip": everywhere(v["even_d_skip_2"][0]), "qn_dil": everywhere(v["even_q_norm_2"][0]),
        "kn_dil": everywhere(v["even_k_norm_2"][0]), "qn_moba": everywhere(v["odd_q_norm_2"][0]),
        "kn_moba": everywhere(v["odd_k_norm_2"][0]),
    }
    assert all(p[k].shape == (P, PARAM2[k]) for k in PARAM2)
    return np.concatenate([p[k] for k in PARAM2], 1)


def kernel(**inputs):
    import concourse.bacc as bacc
    from concourse.bass_utils import run_bass_kernel_spmd

    v = {k: np.asarray(a) for k, a in inputs.items()}

    def tiles(a):
        return np.ascontiguousarray(a[0].reshape(NT, P, D).transpose(1, 0, 2))

    arrays = {
        "weights": np.concatenate([layer_chunks(v, l) for l in range(DEPTH)] + [tail_chunks(v)]),
        "par": np.concatenate([layer_parameters(v, l) for l in range(DEPTH)], 1),
        "par2": tail_parameters(v),
        "const": constants(),
        "posts": np.stack([v[n][l] for l in range(DEPTH) for n in ("ffn1_norm_post", "mix_norm_post", "ffn2_norm_post")]),
        "x": tiles(v["x"]), "mem": tiles(v["mem"]), "positions": v["positions"],
    }
    arrays = {k: np.ascontiguousarray(a) for k, a in arrays.items()}
    nc = bacc.Bacc("TRN2", target_bir_lowering=False, num_devices=1)
    ins = {
        k: nc.dram_tensor(f"in_{k}", a.shape, mybir.dt.from_np(a.dtype), kind="ExternalInput").ap()
        for k, a in arrays.items()
    }
    out = nc.dram_tensor("out", (P, NT, D), F32, kind="ExternalOutput").ap()
    build(nc, ins["weights"], ins["par"], ins["par2"], ins["const"], ins["posts"], ins["x"], ins["mem"],
          ins["positions"], out)
    r = run_bass_kernel_spmd(nc, [{f"in_{k}": a for k, a in arrays.items()}], core_ids=[0])
    got = np.asarray(r.results[0]["out"])
    return np.ascontiguousarray(got.transpose(1, 0, 2).reshape(1, SEQ, D))
```
